# Optimizing a Trainium2 kernel written in Bass

```python
import math
import jax
import jax.numpy as jnp
from jax import lax
import numpy as np
import jax, jax.numpy as jnp

D_MODEL = 1024
BATCH = 1
SEQ = 256
DEPTH = 1

GRID_W = 64
CTX_LEN = 256

M_HEADS = 8
M_QK_DIM = 64
M_V_DIM = 128
M_QK = M_HEADS * M_QK_DIM
M_V = M_HEADS * M_V_DIM
M_CHUNK = 64

H_HEADS = 8
H_K_DIM = 128
H_V_DIM = 128
H_K = H_HEADS * H_K_DIM
H_V = H_HEADS * H_V_DIM
H_CHUNK = 16

FFN_HIDDEN = 2816
N_MOD = 9
EPS = 1e-6

PROJ_SIZES = (M_QK, M_QK, M_V, M_V, 2 * M_HEADS, 2 * M_HEADS,
              H_K, 2 * H_K, H_V, H_V, D_MODEL, D_MODEL)


def _rms(x, g):
    xf = x.astype(jnp.float32)
    y = xf * lax.rsqrt(jnp.mean(xf * xf, axis=-1, keepdims=True) + EPS)
    return y.astype(x.dtype) * g

def _head_rms(y, g, heads):
    B, T, W = y.shape
    return _rms(y.reshape(B, T, heads, W // heads), g.reshape(heads, W // heads)).reshape(B, T, W)

def _modulate(xn, shift, scale):
    return xn * (1.0 + scale) + shift

def _swiglu(xm, w_in, w_out):
    a, u = jnp.split(xm @ w_in, 2, axis=-1)
    return (jax.nn.silu(a) * u) @ w_out

def _split_proj(p):
    idx = np.cumsum(PROJ_SIZES)[:-1].tolist()
    return jnp.split(p, idx, axis=-1)

def _to_chunks(a, L):
    B, H, T = a.shape[:3]
    rest = a.shape[3:]
    return jnp.moveaxis(a.reshape(B, H, T // L, L, *rest), 2, 0)

def _from_chunks(a):
    NC, B, H, L = a.shape[:4]
    rest = a.shape[4:]
    return jnp.moveaxis(a, 0, 2).reshape(B, H, NC * L, *rest)

def _to_col_major(a):
    B, T, C = a.shape
    rows = T // GRID_W
    return a.reshape(B, rows, GRID_W, C).transpose(0, 2, 1, 3).reshape(B, T, C)

def _to_row_major(a):
    B, T, C = a.shape
    rows = T // GRID_W
    return a.reshape(B, GRID_W, rows, C).transpose(0, 2, 1, 3).reshape(B, T, C)

def _mlstm_scan(q, k, v, ig, fg, state):
    L = M_CHUNK
    mask = jnp.tril(jnp.ones((L, L), dtype=bool))
    scale = M_QK_DIM ** -0.5
    f32 = jnp.float32
    xs = (_to_chunks(q.astype(f32) * scale, L), _to_chunks(k.astype(f32), L),
          _to_chunks(v.astype(f32), L), _to_chunks(ig.astype(f32), L),
          _to_chunks(jax.nn.log_sigmoid(fg.astype(f32)), L))

    def body(carry, inp):
        C, n, m = carry
        qc, kc, vc, ic, lf = inp
        b = jnp.cumsum(lf, axis=-1)
        dlog = jnp.where(mask, b[..., :, None] - b[..., None, :] + ic[..., None, :], -jnp.inf)
        inter_log = b + m[..., None]
        m_t = jnp.maximum(inter_log, jnp.max(dlog, axis=-1))
        s = jnp.einsum('bhtd,bhsd->bhts', qc, kc) * jnp.exp(dlog - m_t[..., None])
        w_inter = jnp.exp(inter_log - m_t)
        num = w_inter[..., None] * jnp.einsum('bhtd,bhdv->bhtv', qc, C) + jnp.einsum('bhts,bhsv->bhtv', s, vc)
        den = w_inter * jnp.einsum('bhtd,bhd->bht', qc, n) + jnp.sum(s, axis=-1)
        h = num / jnp.maximum(jnp.abs(den), jnp.exp(-m_t))[..., None]
        b_last = b[..., -1]
        w_log = b_last[..., None] - b + ic
        m_new = jnp.maximum(b_last + m, jnp.max(w_log, axis=-1))
        decay = jnp.exp(b_last + m - m_new)
        w = jnp.exp(w_log - m_new[..., None])
        C_new = decay[..., None, None] * C + jnp.einsum('bhs,bhsd,bhsv->bhdv', w, kc, vc)
        n_new = decay[..., None] * n + jnp.einsum('bhs,bhsd->bhd', w, kc)
        return (C_new, n_new, m_new), h

    state, h = lax.scan(body, state, xs)
    return _from_chunks(h), state

def _hgrn_scan(q, k, v, logf, S):
    L = H_CHUNK
    mask = jnp.tril(jnp.ones((L, L), dtype=bool))[:, :, None]
    f32 = jnp.float32
    xs = tuple(_to_chunks(a.astype(f32), L) for a in (q, k, v, logf))

    def body(S, inp):
        qc, kc, vc, lf = inp
        b = jnp.cumsum(lf, axis=2)
        diff = b[:, :, :, None, :] - b[:, :, None, :, :]
        decay = jnp.exp(jnp.where(mask, diff, -jnp.inf))
        attn = jnp.einsum('bhtd,bhtsd,bhsd->bhts', qc, decay, kc)
        o = jnp.einsum('bhtd,bhdv->bhtv', qc * jnp.exp(b), S) + jnp.einsum('bhts,bhsv->bhtv', attn, vc)
        b_last = b[:, :, -1]
        S_new = jnp.exp(b_last)[..., None] * S + jnp.einsum(
            'bhsd,bhsv->bhdv', kc * jnp.exp(b_last[:, :, None, :] - b), vc)
        return S_new, o

    S, o = lax.scan(body, S, xs)
    return _from_chunks(o), S

def _flip_t(args):
    return tuple(jnp.flip(a, axis=2) for a in args)

def _bidir_scan(scan_fn, ctx_fwd, ctx_bwd, lat_fwd, lat_bwd, init):
    hcf, s_f = scan_fn(*ctx_fwd, init)
    hlf, _ = scan_fn(*lat_fwd, s_f)
    hcb, s_b = scan_fn(*_flip_t(ctx_bwd), init)
    hlb, _ = scan_fn(*_flip_t(lat_bwd), s_b)
    return hcf + jnp.flip(hcb, axis=2), hlf + jnp.flip(hlb, axis=2)

def _mlstm_branch(seg_c, seg_l, gain, dtype):
    f32 = jnp.float32

    def prep(seg):
        q, k, v, o, ig, fg = seg
        B, T, _ = q.shape
        hd = lambda a: a.reshape(B, T, M_HEADS, -1).transpose(0, 2, 1, 3)
        ig = ig.astype(f32).transpose(0, 2, 1)
        fg = fg.astype(f32).transpose(0, 2, 1)
        qh, kh, vh = hd(q), hd(k), hd(v)
        fwd = (qh, kh, vh, ig[:, :M_HEADS], fg[:, :M_HEADS])
        bwd = (qh, kh, vh, ig[:, M_HEADS:], fg[:, M_HEADS:])
        return fwd, bwd, o

    cf, cb, oc = prep(seg_c)
    lf, lb, ol = prep(seg_l)
    B = oc.shape[0]
    init = (jnp.zeros((B, M_HEADS, M_QK_DIM, M_V_DIM), f32),
            jnp.zeros((B, M_HEADS, M_QK_DIM), f32),
            jnp.zeros((B, M_HEADS), f32))
    hc, hl = _bidir_scan(_mlstm_scan, cf, cb, lf, lb, init)

    def out(h, o):
        B_, H, T, dv = h.shape
        h = h.transpose(0, 2, 1, 3).reshape(B_, T, H * dv)
        return (_head_rms(h, gain, M_HEADS) * jax.nn.sigmoid(o.astype(f32))).astype(dtype)

    return out(hc, oc), out(hl, ol)

def _hgrn_gates(f_pre, lb):
    fp = f_pre.astype(jnp.float32)
    logf = jnp.log(lb + (1.0 - lb) * jax.nn.sigmoid(fp))
    k = (1.0 - lb) * jax.nn.sigmoid(-fp)
    return logf, k

def _hgrn_branch(seg_c, seg_l, lb, gain, dtype):
    f32 = jnp.float32

    def prep(seg):
        q, f, i, g = seg
        B, T, _ = q.shape
        hd = lambda a: a.astype(f32).reshape(B, T, H_HEADS, -1).transpose(0, 2, 1, 3)
        qh = hd(jax.nn.silu(q.astype(f32)))
        vh = hd(i)
        lf_f, k_f = _hgrn_gates(f[..., :H_K], lb[0])
        lf_b, k_b = _hgrn_gates(f[..., H_K:], lb[1])
        return (qh, hd(k_f), vh, hd(lf_f)), (qh, hd(k_b), vh, hd(lf_b)), g

    cf, cb, gc = prep(seg_c)
    lf, lbw, gl = prep(tuple(_to_col_major(a) for a in seg_l))
    B = gc.shape[0]
    init = jnp.zeros((B, H_HEADS, H_K_DIM, H_V_DIM), f32)
    hc, hl = _bidir_scan(_hgrn_scan, cf, cb, lf, lbw, init)

    def out(h, g):
        B_, H, T, dv = h.shape
        h = h.transpose(0, 2, 1, 3).reshape(B_, T, H * dv)
        return (_head_rms(h, gain, H_HEADS) * jax.nn.silu(g.astype(f32))).astype(dtype)

    return out(hc, gc), _to_row_major(out(hl, gl))

def _token_mix(xc, xl, w_in, b_in, m_gain, lb, h_gain, proj_m, proj_h, w_out, need_ctx):
    seg_c = _split_proj(xc @ w_in + b_in)
    seg_l = _split_proj(xl @ w_in + b_in)
    hm_c, hm_l = _mlstm_branch(seg_c[0:6], seg_l[0:6], m_gain, xl.dtype)
    hh_c, hh_l = _hgrn_branch(seg_c[6:10], seg_l[6:10], lb, h_gain, xl.dtype)

    def merge(hm, hh, gm, gh):
        return (jax.nn.sigmoid(gm) * (hm @ proj_m) + jax.nn.sigmoid(gh) * (hh @ proj_h)) @ w_out

    y_l = merge(hm_l, hh_l, seg_l[10], seg_l[11])
    y_c = merge(hm_c, hh_c, seg_c[10], seg_c[11]) if need_ctx else None
    return y_c, y_l

def first_inputs(seed: int = 0) -> dict:
    key = jax.random.key(seed)
    ks = jax.random.split(key, 24)
    D, F = D_MODEL, FFN_HIDDEN
    P = int(sum(PROJ_SIZES))
    nrm = lambda k, shape, s: jax.random.normal(k, shape, jnp.float32) * s
    gains = lambda k, shape: 1.0 + nrm(k, shape, 0.05)
    f_start = int(sum(PROJ_SIZES[:5]))
    f_bias = jnp.tile(jnp.linspace(3.0, 6.0, M_HEADS), 2)
    b_off = jnp.zeros((P,), jnp.float32).at[f_start:f_start + 2 * M_HEADS].set(f_bias)
    return {
        "x": nrm(ks[0], (BATCH, SEQ, D), 1.0),
        "c": nrm(ks[1], (BATCH, D), 1.0),
        "ctx": nrm(ks[2], (BATCH, CTX_LEN, D), 1.0),
        "c_ctx": nrm(ks[3], (D,), 1.0),
        "ada_w": nrm(ks[4], (DEPTH, D, N_MOD * D), D ** -0.5),
        "ada_b": nrm(ks[5], (DEPTH, N_MOD * D), 0.02),
        "ffn1_norm": gains(ks[6], (DEPTH, D)),
        "ffn1_w_in": nrm(ks[7], (DEPTH, D, 2 * F), D ** -0.5),
        "ffn1_w_out": nrm(ks[8], (DEPTH, F, D), F ** -0.5),
        "mix_norm": gains(ks[9], (DEPTH, D)),
        "mix_w_in": nrm(ks[10], (DEPTH, D, P), D ** -0.5),
        "mix_b_in": b_off[None, :] + nrm(ks[11], (DEPTH, P), 0.02),
        "mlstm_norm": gains(ks[12], (DEPTH, M_V)),
        "hgrn_lb_logits": nrm(ks[13], (2, DEPTH + 1, H_K), 0.5),
        "hgrn_norm": gains(ks[14], (DEPTH, H_V)),
        "proj_m": nrm(ks[15], (DEPTH, M_V, D), M_V ** -0.5),
        "proj_h": nrm(ks[16], (DEPTH, H_V, D), H_V ** -0.5),
        "mix_w_out": nrm(ks[17], (DEPTH, D, D), D ** -0.5),
        "ffn2_norm": gains(ks[18], (DEPTH, D)),
        "ffn2_w_in": nrm(ks[19], (DEPTH, D, 2 * F), D ** -0.5),
        "ffn2_w_out": nrm(ks[20], (DEPTH, F, D), F ** -0.5),
        "final_norm": gains(ks[21], (D,)),
    }

def first_block(x, c, ctx, c_ctx, ada_w, ada_b, ffn1_norm, ffn1_w_in, ffn1_w_out, mix_norm,
              mix_w_in, mix_b_in, mlstm_norm, hgrn_lb_logits, hgrn_norm, proj_m, proj_h,
              mix_w_out, ffn2_norm, ffn2_w_in, ffn2_w_out, final_norm):
    B = x.shape[0]
    D = x.shape[-1]
    lb_all = jnp.cumsum(jax.nn.softmax(hgrn_lb_logits.astype(jnp.float32), axis=1), axis=1)
    h = ctx
    for l in range(DEPTH):
        last = l == DEPTH - 1
        ml = (jax.nn.silu(c) @ ada_w[l] + ada_b[l]).reshape(B, N_MOD, 1, D)
        mc = (jax.nn.silu(c_ctx) @ ada_w[l] + ada_b[l]).reshape(N_MOD, 1, 1, D)
        x = x + 0.5 * ml[:, 2] * _swiglu(_modulate(_rms(x, ffn1_norm[l]), ml[:, 0], ml[:, 1]), ffn1_w_in[l], ffn1_w_out[l])
        h = h + 0.5 * mc[2] * _swiglu(_modulate(_rms(h, ffn1_norm[l]), mc[0], mc[1]), ffn1_w_in[l], ffn1_w_out[l])
        y_c, y_l = _token_mix(_modulate(_rms(h, mix_norm[l]), mc[3], mc[4]),
                              _modulate(_rms(x, mix_norm[l]), ml[:, 3], ml[:, 4]),
                              mix_w_in[l], mix_b_in[l], mlstm_norm[l], lb_all[:, l], hgrn_norm[l],
                              proj_m[l], proj_h[l], mix_w_out[l], not last)
        x = x + ml[:, 5] * y_l
        if not last:
            h = h + mc[5] * y_c
            h = h + 0.5 * mc[8] * _swiglu(_modulate(_rms(h, ffn2_norm[l]), mc[6], mc[7]), ffn2_w_in[l], ffn2_w_out[l])
        x = x + 0.5 * ml[:, 8] * _swiglu(_modulate(_rms(x, ffn2_norm[l]), ml[:, 6], ml[:, 7]), ffn2_w_in[l], ffn2_w_out[l])
    return _rms(x, final_norm)


DEPTH_2 = 2

D_FF = 2816
NSA_HEADS = 8
NSA_GROUPS = 2
NSA_HPG = NSA_HEADS // NSA_GROUPS
NSA_DH = 64
CMP_BLOCK = 32
CMP_STRIDE = 16
CMP_HIDDEN = 256
SEL_BLOCK = 64
SEL_TOPN = 16
WINDOW = 512
Q_BLOCK = 64
GLA_HEADS = 4
GLA_DK = 128
GLA_DV = 256
GLA_RANK = 16
GLA_TAU = 16.0
GLA_CHUNK = 64
REL_BUCKETS = 32
REL_MAX_DIST = 1024
NEG = -1e30

W_IN_SPLITS = (
    NSA_HEADS * NSA_DH,
    6 * NSA_GROUPS * NSA_DH,
    3 * NSA_HEADS,
    GLA_HEADS * GLA_DK,
    GLA_HEADS * GLA_DK,
    GLA_HEADS * GLA_DV,
    GLA_RANK,
    GLA_HEADS * GLA_DV,
    2 * D_MODEL,
)
D_IN = sum(W_IN_SPLITS)


def rmsnorm(x, g):
    xf = x.astype(jnp.float32)
    y = xf * lax.rsqrt(jnp.mean(xf * xf, axis=-1, keepdims=True) + EPS)
    return (y * g.astype(jnp.float32)).astype(x.dtype)

def swiglu(x, w_gate, w_up, w_down):
    return (jax.nn.silu(x @ w_gate) * (x @ w_up)) @ w_down

def rel_bucket(dist):
    n = jnp.maximum(dist, 0)
    exact = REL_BUCKETS // 2
    nf = jnp.maximum(n, 1).astype(jnp.float32)
    log_b = exact + (jnp.log(nf / exact) / math.log(REL_MAX_DIST / exact)
                     * (REL_BUCKETS - exact)).astype(jnp.int32)
    return jnp.where(n < exact, n, jnp.minimum(log_b, REL_BUCKETS - 1))

def masked_softmax(logits, mask):
    p = jax.nn.softmax(jnp.where(mask, logits, NEG), axis=-1)
    return jnp.where(mask, p, 0.0)

def nsa_compress(k, pos, w1, w2):
    B, S, G, dh = k.shape
    nc = (S - CMP_BLOCK) // CMP_STRIDE + 1
    idx = jnp.arange(nc)[:, None] * CMP_STRIDE + jnp.arange(CMP_BLOCK)[None, :]
    blocks = k[:, idx] + pos[None, None, :, None, :]
    blocks = blocks.transpose(0, 1, 3, 2, 4).reshape(B, nc, G, CMP_BLOCK * dh)
    return jax.nn.silu(blocks @ w1) @ w2

def nsa_attention(q, k_cmp, v_cmp, k_slc, v_slc, k_win, v_win, gates, rel_table):
    B, S, H, dh = q.shape
    G, HPG = NSA_GROUPS, NSA_HPG
    nqb = S // Q_BLOCK
    ns = S // SEL_BLOCK
    nc = k_cmp.shape[1]
    n_sel = min(SEL_TOPN, ns)
    kw_len = WINDOW + Q_BLOCK

    c_start = jnp.arange(nc) * CMP_STRIDE
    cmp_end = c_start + CMP_BLOCK - 1
    sb_start = jnp.arange(ns) * SEL_BLOCK
    overlap = ((c_start[:, None] < sb_start[None, :] + SEL_BLOCK)
               & (c_start[:, None] + CMP_BLOCK > sb_start[None, :])).astype(jnp.float32)
    js = jnp.arange(ns)
    table_g = rel_table.reshape(REL_BUCKETS, G, HPG).transpose(1, 0, 2)

    kb = k_slc.reshape(B, ns, SEL_BLOCK, G, dh).transpose(0, 3, 1, 2, 4)
    vb = v_slc.reshape(B, ns, SEL_BLOCK, G, dh).transpose(0, 3, 1, 2, 4)
    pad = ((0, 0), (WINDOW, 0), (0, 0), (0, 0))
    kw = jnp.pad(k_win, pad)
    vw = jnp.pad(v_win, pad)

    def to_blocks(a):
        return a.reshape(B, nqb, Q_BLOCK, *a.shape[2:]).swapaxes(0, 1)

    qs = to_blocks(q * (dh ** -0.5))
    gs = to_blocks(gates)
    bi = jnp.arange(B)[:, None, None, None]
    gi = jnp.arange(G)[None, :, None, None]

    def block_fn(args):
        c, qc, gc = args
        t = c * Q_BLOCK + jnp.arange(Q_BLOCK)
        qg = qc.reshape(B, Q_BLOCK, G, HPG, dh)

        lc = jnp.einsum('bqghd,bcgd->bghqc', qg, k_cmp).astype(jnp.float32)
        bias_c = rel_table[rel_bucket(t[:, None] - cmp_end[None, :])]
        lc = lc + bias_c.reshape(Q_BLOCK, nc, G, HPG).transpose(2, 3, 0, 1)
        p_cmp = masked_softmax(lc, cmp_end[None, :] <= t[:, None])
        o_cmp = jnp.einsum('bghqc,bcgd->bqghd', p_cmp.astype(v_cmp.dtype), v_cmp)

        imp = jnp.einsum('bghqc,cs->bgqs', p_cmp, overlap)
        jcur = t // SEL_BLOCK
        forced = (js[None, :] == 0) | (js[None, :] == jcur[:, None]) | (js[None, :] == jcur[:, None] - 1)
        valid = js[None, :] <= jcur[:, None]
        score = jnp.where(forced, 1e6, jnp.where(valid, imp, -1e6))
        _, sel = lax.top_k(score, n_sel)
        ks = kb[bi, gi, sel]
        vs = vb[bi, gi, sel]
        s_pos = sel[..., None] * SEL_BLOCK + jnp.arange(SEL_BLOCK)
        ls = jnp.einsum('bqghd,bgqnrd->bghqnr', qg, ks).astype(jnp.float32)
        bias_s = table_g[gi[..., None], rel_bucket(t[:, None, None] - s_pos)]
        ls = ls + bias_s.transpose(0, 1, 5, 2, 3, 4)
        ksel = n_sel * SEL_BLOCK
        ls = ls.reshape(B, G, HPG, Q_BLOCK, ksel)
        ms = (s_pos <= t[:, None, None]).reshape(B, G, Q_BLOCK, ksel)[:, :, None]
        p_s = masked_softmax(ls, ms)
        o_slc = jnp.einsum('bghqk,bgqkd->bqghd', p_s.astype(vs.dtype),
                           vs.reshape(B, G, Q_BLOCK, ksel, dh))

        kwc = lax.dynamic_slice_in_dim(kw, c * Q_BLOCK, kw_len, axis=1)
        vwc = lax.dynamic_slice_in_dim(vw, c * Q_BLOCK, kw_len, axis=1)
        s_w = c * Q_BLOCK - WINDOW + jnp.arange(kw_len)
        dist = t[:, None] - s_w[None, :]
        mw = (s_w[None, :] >= 0) & (dist >= 0) & (dist < WINDOW)
        lw = jnp.einsum('bqghd,bkgd->bghqk', qg, kwc).astype(jnp.float32)
        lw = lw + rel_table[rel_bucket(dist)].reshape(Q_BLOCK, kw_len, G, HPG).transpose(2, 3, 0, 1)
        p_w = masked_softmax(lw, mw)
        o_win = jnp.einsum('bghqk,bkgd->bqghd', p_w.astype(vwc.dtype), vwc)

        o = jnp.stack([o_cmp, o_slc, o_win], axis=-1)
        g = gc.reshape(B, Q_BLOCK, G, HPG, 3)[..., None, :]
        return jnp.sum(o * g, axis=-1).reshape(B, Q_BLOCK, H * dh).astype(q.dtype)

    out = lax.map(block_fn, (jnp.arange(nqb), qs, gs))
    return out.swapaxes(0, 1).reshape(B, S, H * dh)

def gla_attention(q, k, v, log_a):
    B, S, Hb, dk = q.shape
    dv = v.shape[-1]
    C = GLA_CHUNK
    n = S // C

    def chunks(a):
        return a.reshape(B, n, C, *a.shape[2:])

    qc, kc, vc, la = chunks(q * (dk ** -0.5)), chunks(k), chunks(v), chunks(log_a)
    b = jnp.cumsum(la.astype(jnp.float32), axis=2)
    b_last = b[:, :, -1:]
    q_dec = qc * jnp.exp(b)
    k_intra = kc * jnp.exp(-b)
    k_state = kc * jnp.exp(b_last - b)
    causal = jnp.tril(jnp.ones((C, C), dtype=bool))
    A = jnp.where(causal, jnp.einsum('bnihd,bnjhd->bnhij', q_dec, k_intra), 0.0)
    o_intra = jnp.einsum('bnhij,bnjhv->bnihv', A, vc.astype(jnp.float32))
    decay_chunk = jnp.exp(b_last[:, :, 0])

    def step(state, inp):
        qd, ksd, vcc, dch = inp
        o = jnp.einsum('bihd,bhdv->bihv', qd, state)
        state = dch[..., None] * state + jnp.einsum('bjhd,bjhv->bhdv', ksd, vcc.astype(jnp.float32))
        return state, o

    s0 = jnp.zeros((B, Hb, dk, dv), jnp.float32)
    _, o_inter = lax.scan(step, s0, (q_dec.swapaxes(0, 1), k_state.swapaxes(0, 1),
                                     vc.swapaxes(0, 1), decay_chunk.swapaxes(0, 1)))
    o = o_intra + o_inter.swapaxes(0, 1)
    return o.reshape(B, S, Hb, dv).astype(v.dtype)

def second_inputs(seed: int = 0) -> dict:
    key = jax.random.key(seed)
    ks = jax.random.split(key, 32)
    f32 = jnp.float32
    L, D = DEPTH_2, D_MODEL

    def w(k, shape, fan_in):
        return jax.random.normal(k, shape, f32) * fan_in ** -0.5

    def gain(k, shape):
        return 1.0 + 0.05 * jax.random.normal(k, shape, f32)

    return {
        "x": jax.random.normal(ks[0], (BATCH, SEQ, D), f32),
        "rel_table": 0.2 * jax.random.normal(ks[1], (REL_BUCKETS, NSA_HEADS), f32),
        "ffn1_norm": gain(ks[2], (L, D)),
        "ffn1_w_gate": w(ks[3], (L, D, D_FF), D),
        "ffn1_w_up": w(ks[4], (L, D, D_FF), D),
        "ffn1_w_down": w(ks[5], (L, D_FF, D), D_FF),
        "mix_norm": gain(ks[6], (L, D)),
        "w_in": w(ks[7], (L, D, D_IN), D),
        "cmp_pos_k": 0.5 * jax.random.normal(ks[8], (L, CMP_BLOCK, NSA_DH), f32),
        "cmp_pos_v": 0.5 * jax.random.normal(ks[9], (L, CMP_BLOCK, NSA_DH), f32),
        "cmp_k_w1": w(ks[10], (L, CMP_BLOCK * NSA_DH, CMP_HIDDEN), CMP_BLOCK * NSA_DH),
        "cmp_k_w2": w(ks[11], (L, CMP_HIDDEN, NSA_DH), CMP_HIDDEN),
        "cmp_v_w1": w(ks[12], (L, CMP_BLOCK * NSA_DH, CMP_HIDDEN), CMP_BLOCK * NSA_DH),
        "cmp_v_w2": w(ks[13], (L, CMP_HIDDEN, NSA_DH), CMP_HIDDEN),
        "gla_a_w2": w(ks[14], (L, GLA_RANK, GLA_HEADS * GLA_DK), GLA_RANK),
        "gla_a_b": 0.1 * jax.random.normal(ks[15], (L, GLA_HEADS * GLA_DK), f32),
        "gla_out_norm": gain(ks[16], (L, GLA_HEADS * GLA_DV)),
        "w_branch_nsa": w(ks[17], (L, NSA_HEADS * NSA_DH, D), NSA_HEADS * NSA_DH),
        "w_branch_gla": w(ks[18], (L, GLA_HEADS * GLA_DV, D), GLA_HEADS * GLA_DV),
        "w_out": w(ks[19], (L, D, D), D),
        "ffn2_norm": gain(ks[20], (L, D)),
        "ffn2_w_gate": w(ks[21], (L, D, D_FF), D),
        "ffn2_w_up": w(ks[22], (L, D, D_FF), D),
        "ffn2_w_down": w(ks[23], (L, D_FF, D), D_FF),
        "final_norm": gain(ks[24], (D,)),
    }

def second_block(x, rel_table, ffn1_norm, ffn1_w_gate, ffn1_w_up, ffn1_w_down, mix_norm, w_in,
              cmp_pos_k, cmp_pos_v, cmp_k_w1, cmp_k_w2, cmp_v_w1, cmp_v_w2, gla_a_w2, gla_a_b,
              gla_out_norm, w_branch_nsa, w_branch_gla, w_out, ffn2_norm, ffn2_w_gate, ffn2_w_up,
              ffn2_w_down, final_norm):
    B, S, D = x.shape
    offsets = np.cumsum(W_IN_SPLITS)[:-1].tolist()
    for l in range(DEPTH_2):
        x = x + 0.5 * swiglu(rmsnorm(x, ffn1_norm[l]), ffn1_w_gate[l], ffn1_w_up[l], ffn1_w_down[l])

        h = rmsnorm(x, mix_norm[l])
        proj = h @ w_in[l]
        q_a, kv_a, g_a, q_b, k_b, v_b, a_lr, r_b, g_merge = jnp.split(proj, offsets, axis=-1)

        q_a = q_a.reshape(B, S, NSA_HEADS, NSA_DH)
        kv_a = kv_a.reshape(B, S, 6, NSA_GROUPS, NSA_DH)
        k_cmp = nsa_compress(kv_a[:, :, 0], cmp_pos_k[l], cmp_k_w1[l], cmp_k_w2[l])
        v_cmp = nsa_compress(kv_a[:, :, 1], cmp_pos_v[l], cmp_v_w1[l], cmp_v_w2[l])
        gates_a = jax.nn.sigmoid(g_a).reshape(B, S, NSA_HEADS, 3)
        o_a = nsa_attention(q_a, k_cmp, v_cmp, kv_a[:, :, 2], kv_a[:, :, 3],
                            kv_a[:, :, 4], kv_a[:, :, 5], gates_a, rel_table)

        log_a = jax.nn.log_sigmoid((a_lr @ gla_a_w2[l] + gla_a_b[l]).astype(jnp.float32)) / GLA_TAU
        o_b = gla_attention(q_b.reshape(B, S, GLA_HEADS, GLA_DK),
                            k_b.reshape(B, S, GLA_HEADS, GLA_DK),
                            v_b.reshape(B, S, GLA_HEADS, GLA_DV),
                            log_a.reshape(B, S, GLA_HEADS, GLA_DK))
        o_b = rmsnorm(o_b, gla_out_norm[l].reshape(GLA_HEADS, GLA_DV))
        o_b = o_b.reshape(B, S, GLA_HEADS * GLA_DV) * jax.nn.silu(r_b)

        gm = jax.nn.sigmoid(g_merge).reshape(B, S, 2, D)
        y = gm[:, :, 0] * (o_a @ w_branch_nsa[l]) + gm[:, :, 1] * (o_b @ w_branch_gla[l])
        x = x + y @ w_out[l]

        x = x + 0.5 * swiglu(rmsnorm(x, ffn2_norm[l]), ffn2_w_gate[l], ffn2_w_up[l], ffn2_w_down[l])
    return rmsnorm(x, final_norm)


def setup_inputs(seed=0):
    out = dict(first_inputs(seed))
    for name, value in second_inputs(seed + 1).items():
        if name != "x":
            out[name + "_2"] = value
    return out


def reference(
    x, c, ctx, c_ctx, ada_w, ada_b, ffn1_norm, ffn1_w_in, ffn1_w_out, mix_norm, mix_w_in,
    mix_b_in, mlstm_norm, hgrn_lb_logits, hgrn_norm, proj_m, proj_h, mix_w_out, ffn2_norm,
    ffn2_w_in, ffn2_w_out, final_norm, rel_table_2, ffn1_norm_2, ffn1_w_gate_2, ffn1_w_up_2,
    ffn1_w_down_2, mix_norm_2, w_in_2, cmp_pos_k_2, cmp_pos_v_2, cmp_k_w1_2, cmp_k_w2_2,
    cmp_v_w1_2, cmp_v_w2_2, gla_a_w2_2, gla_a_b_2, gla_out_norm_2, w_branch_nsa_2,
    w_branch_gla_2, w_out_2, ffn2_norm_2, ffn2_w_gate_2, ffn2_w_up_2, ffn2_w_down_2,
    final_norm_2,
):
    x = first_block(
        x, c, ctx, c_ctx, ada_w, ada_b, ffn1_norm, ffn1_w_in, ffn1_w_out, mix_norm, mix_w_in,
        mix_b_in, mlstm_norm, hgrn_lb_logits, hgrn_norm, proj_m, proj_h, mix_w_out, ffn2_norm,
        ffn2_w_in, ffn2_w_out, final_norm,
    )
    return second_block(
        x, rel_table_2, ffn1_norm_2, ffn1_w_gate_2, ffn1_w_up_2, ffn1_w_down_2, mix_norm_2,
        w_in_2, cmp_pos_k_2, cmp_pos_v_2, cmp_k_w1_2, cmp_k_w2_2, cmp_v_w1_2, cmp_v_w2_2,
        gla_a_w2_2, gla_a_b_2, gla_out_norm_2, w_branch_nsa_2, w_branch_gla_2, w_out_2,
        ffn2_norm_2, ffn2_w_gate_2, ffn2_w_up_2, ffn2_w_down_2, final_norm_2,
    )


_drawn_inputs = setup_inputs


def setup_inputs(seed=0):
    import zlib

    import numpy as np

    out = dict(_drawn_inputs(seed))
    spreads = {}
    factors = {'mlstm_norm': 4.247,
     'hgrn_lb_logits': 5.844,
     'hgrn_norm': 2.743,
     'cmp_pos_k_2': 4.309,
     'gla_a_b_2': 2.905,
     'ffn2_norm': 3.015}
    for name, (base, spread) in spreads.items():
        noise = np.random.default_rng([zlib.crc32(name.encode()), seed]).standard_normal(out[name].shape)
        drawn = base * np.exp(spread * noise) if base else spread * noise
        out[name] = jnp.asarray(drawn.astype(out[name].dtype))
    for name, factor in factors.items():
        out[name] = (out[name] * factor).astype(out[name].dtype)
    return out
```

```python
import math
import numpy as np
import concourse.bass as bass
from concourse import mybir
from contextlib import ExitStack

F32 = mybir.dt.float32
I32 = mybir.dt.int32
ALU = mybir.AluOpType
ACT = mybir.ActivationFunctionType
AX = mybir.AxisListType

P = 128
D = 1024
KD = D // P
S = 256
ST = S // P
F = 2816
FT = F // P
UG = F // 256
N = 512
CW = 4
SLOTS = 4
EPS = 1e-6
MODS = (0, 1, 3, 4, 6, 7, 2, 5, 8)


def build(nc, t, out):
    ctx = ExitStack()
    with ctx:
        def sb(name, shape, dt=F32):
            return ctx.enter_context(nc.sbuf_tensor(name, shape, dt))

        def sem(name):
            return ctx.enter_context(nc.semaphore(name))

        ring = sb("ring", [P, SLOTS, CW, N])
        X = sb("X", [P, 2 * ST, D])
        xT = sb("xT", [P, KD, 2 * S])
        xn = sb("xn", [P, 2, D])
        ident = sb("ident", [P, P])
        cT = sb("cT", [P, KD, 2])
        scT = sb("scT", [P, KD, 2])
        gains = sb("gains", [P, 3, KD])
        pick = sb("pick", [2, 2, P])
        modT = sb("modT", [P, 48, 2])
        normA = sb("normA", [P, 5, KD])
        gateB = sb("gateB", [P, 4, D])
        ss = sb("ss", [P, 4])
        var = sb("var", [P, 4])
        sd = sb("sd", [P, 4])
        rstd = sb("rstd", [P, 4])
        tmp = sb("tmp", [P, 2, N])
        modrow = sb("modrow", [2, 2, N])

        ARENA = 26 * 1024
        arena = sb("arena", [P, ARENA])

        def room(at, *shape, parts=P):
            size = int(np.prod(shape))
            assert at + size <= ARENA
            v = arena[0:parts, at:at + size]
            if len(shape) == 2:
                return v.rearrange("p (a b) -> p a b", b=shape[1])
            if len(shape) == 3:
                return v.rearrange("p (a b c) -> p a b c", b=shape[1], c=shape[2])
            return v

        gT = room(0, FT, 2 * S)
        adab = room(0, 18 * N, parts=2)
        junk = room(FT * 2 * S, D)
        sil = room(FT * 2 * S + D, 2, 256)
        gtok = room(FT * 2 * S + D + 512, 2, 256)

        H = 8
        wg = room(ARENA - KD * P, KD, P)
        biasB = room(0, 3 * D)
        gainB = room(3072, D)
        qm = room(4096, 4, S)
        km = room(5120, 4, 2 * S)
        va = room(7168, 4, H, P + 1)
        om = room(11296, ST, D)
        gmx = room(13344, ST, D)
        Hm = room(15392, ST, D)
        Pm = room(17440, 4, 4, S)
        hT = room(21536, KD, S)
        vi = room(4096, 4, D)
        ghx = room(8192, ST, D)
        qh = room(10240, 4, S)
        kh = room(11264, 4, 2 * S)
        gx = room(11264, ST, D)
        cum = room(13312, 4, 2, S + 1)
        lf = room(15376, 4, 2 * S)
        E = room(15376, 2, 4, S)
        G = room(17424, 2, 4, S)
        Pl = room(19472, 4, 2, S)
        Pc = room(21520, 4, 2, S)
        kd = room(23568, 4, S)
        Hx = xn[:, :, :]
        y = X[:, 2:4, :]
        rows = xn[:, :, :].rearrange("p a b -> p (a b)")
        igr, lfr, br, gr = (rows[0:40, n * N:(n + 1) * N] for n in range(4))
        zr = gateB[0:40, 3, 0:N]
        gcol = sb("gcol", [P, 4, 40])
        emc = sb("emc", [P, ST, 40])
        bF = sb("bF", [P, 33])
        den = sb("den", [P, 2, ST])
        rden = sb("rden", [P, 2, ST])
        ones = sb("ones", [P, S])
        ssq = sb("ssq", [P, 16])
        lbl = sb("lbl", [P, 2, 2, H])
        lb = sb("lb", [P, 2, H])
        omlb = sb("omlb", [P, 2, H])
        nbF = sb("nbF", [P, 33])
        maskf = gateB[:, 3, 0:7 * P].rearrange("p (a b) -> p a b", b=P).bitcast(I32)
        maskb = tmp[:, :, :].rearrange("p a b -> p (a b)")[:, 0:7 * P].rearrange("p (a b) -> p a b", b=P).bitcast(I32)
        gains2 = sb("gains2", [P, 6, KD])
        TB = X[:, 2:4, :].rearrange("p a b -> p (a b)").rearrange("p (a b) -> p a b", b=S)
        RW = 384
        rep_rows = room(14336, H, RW)
        onehot = room(17408, RW, parts=33)
        table = room(17792, H, parts=33)
        qa = room(0, 4, S)
        kk = room(1024, 2, S)
        KK = room(1536, 2, 2, 240)
        pos = room(2496, 2, 16)
        w2c = room(2528, 2, 2, 64)
        hid = room(2784, 2, 2, 32)
        kcT = room(2912, 16)
        vcmp = room(2928, 2, 64, parts=15)
        vsw = room(3056, 2, S)
        ga = room(3568, 2, 24)
        alr = room(3616, S, parts=16)
        wa2 = room(3872, N, parts=16)
        ab = room(4384, 4)
        gm2 = room(4400, ST, 2 * D)
        oaT = room(8496, 4, S)
        Lb = room(10240, 2, 800)
        PT = room(11840, 2, 1024)
        mx = room(13888, 2, 6)
        sm = room(13900, 2, 6)
        wt = room(13912, 2, 6)
        vb = room(21520, ST, D)
        rx = gateB[:, 0:2, :]
        gainC = gateB[:, 2, :]
        y2 = gm2[:, :, 0:D]
        LEVELS = (128, 64, 32, 16, 8, 4, 2, 1)

        bank = [ctx.enter_context(nc.psum_tensor(f"bank{i}", [P, N], F32)) for i in range(8)]
        acc, trb, misc = bank[0:4], bank[4:6], bank[6:8]

        loaded = [sem(f"chunk_loaded{i}") for i in range(SLOTS)]
        read = [sem(f"chunk_read{i}") for i in range(SLOTS)]
        consts = sem("consts_loaded")
        acc_full = sem("acc_full")
        evac = [sem(f"evacuated{i}") for i in range(4)]
        sil_done = sem("sil_done")
        tr_full = sem("transposed")
        tr_out = sem("transposed_out")
        sc_done = sem("sc_done")
        bc_full = sem("gate_rows_broadcast")
        bc_out = sem("gate_rows_out")
        mod_done = sem("mod_done")
        resid = sem("residual_updated")
        squares = sem("squares_summed")
        var_done = sem("var_done")
        sd_done = sem("sd_done")
        xn_done = sem("xn_done")
        stored = sem("stored")
        bias_in = sem("mix_biases_loaded")
        rows_a = sem("gate_rows_ready")
        rows_b = sem("gate_rows_log")
        rows_c = sem("gate_rows_scanned")
        cols_full = sem("gate_columns")
        cols_out = sem("gate_columns_out")
        em_done = sem("exp_minus_m")
        s_full = sem("mlstm_scores")
        d_done = sem("mlstm_decays")
        p_done = sem("mlstm_weights")
        pm_done = sem("mlstm_weights_masked")
        pv_full = sem("mlstm_values")
        h_done = sem("mlstm_head_done")
        hn_sq = sem("head_norm_squares")
        hn_var = sem("head_norm_var")
        hn_sd = sem("head_norm_sd")
        hn_gate = sem("head_norm_gate")
        hn_out = sem("head_norm_done")
        lb_step = sem("lower_bound")
        bias_rows = sem("bias_rows")
        bias_out = sem("bias_rows_out")
        bias_dma = sem("bias_dma")
        bias_done = sem("bias_toeplitz")
        layer_in = sem("layer_constants_loaded")
        final_in = sem("final_gain_loaded")
        ga_done = sem("branch_gates")
        ns_s = sem("nsa_scores")
        ns_m = sem("nsa_maxima")
        ns_e = sem("nsa_exponentials")
        ns_w = sem("nsa_probabilities")
        ns_t = sem("nsa_transposed")
        ns_pa = sem("nsa_transposed_out_a")
        ns_pb = sem("nsa_transposed_out_b")
        ns_o = sem("nsa_outputs")
        ns_h = sem("nsa_head_done")
        gl_a = sem("gla_abs")
        gl_l = sem("gla_log")
        pad_set = sem("pad_set")
        out_done = sem("out_done")
        masks_in = sem("level_masks_loaded")
        permuted = sem("column_major_input")
        lf_done = sem("log_decays")
        lv_d = sem("level_differences")
        lv_e = sem("level_decays")
        lv_g = sem("level_operands")
        lv_a = sem("level_products")
        lv_p = sem("level_collected")
        attn_done = sem("attention_whole")
        merge_gate = sem("merge_gate")
        y_done = sem("merged")
        ones_set = sem("ones_set")
        dve_seq = sem("vector_step")
        act_seq = sem("scalar_step")

        NCH = t["stream"].shape[0]
        block = ctx.enter_context(nc.Block())

        class Count:
            def __init__(self):
                self.chunk = self.acc = self.tr = self.bc = self.sil = self.resid = self.norm = self.xn = self.seq = 0
                self.hn = self.y = self.d = self.e = self.g = self.a = self.lf = self.p = self.ns = self.layer = self.gl = self.at = 0

        def up(v, i, per):
            return v if i is None else v + i * per

        @block.sync
        def _(sp):
            for j in range(SLOTS):
                sp.dma_start(ring[:, j], t["stream"][j]).then_inc(loaded[j], 16)
            turns = NCH // SLOTS
            with sp.Fori(1, turns) as i:
                for j in range(SLOTS):
                    sp.wait_ge(read[j], i)
                    sp.dma_start(ring[:, j], t["stream"][i * SLOTS + j]).then_inc(loaded[j], 16)
            for n in range(turns * SLOTS, NCH):
                sp.wait_ge(read[n % SLOTS], n // SLOTS)
                sp.dma_start(ring[:, n % SLOTS], t["stream"][n]).then_inc(loaded[n % SLOTS], 16)

        @block.tensor
        def _(pe):
            c = Count()
            owed = []

            def mm(o, l, r, start, stop, inc=None):
                m = pe.matmul(o, l, r, start=start, stop=stop)
                if inc is not None:
                    m.then_inc(inc, 1)
                elif owed:
                    m.then_inc(owed.pop(), 1)

            def chunk_wait(n, i=None, per=0):
                pe.wait_ge(loaded[n % SLOTS], up(16 * (n // SLOTS + 1), i, 16 * per))

            def bank_wait(n, i=None, per=0):
                if n >= 4:
                    pe.wait_ge(evac[n % 4], up(n // 4, i, per))

            def group_tile(n, ch, first, last, lhs, width, rows=P, i=None, cper=0, nper=0):
                bank_wait(n, i, nper)
                for k in range(KD):
                    if first and k % CW == 0:
                        chunk_wait(ch + k // CW, i, cper)
                    inc = None
                    if k == KD - 1:
                        inc = acc_full
                    elif last and k == CW - 1:
                        inc = read[ch % SLOTS]
                    mm(acc[n % 4][0:rows, 0:width], lhs(k), ring[:, (ch + k // CW) % SLOTS, k % CW, 0:width],
                       k == 0, k == KD - 1, inc)
                if last:
                    owed.append(read[(ch + 1) % SLOTS])

            def modulation():
                pe.wait_ge(consts, CONSTS)
                pe.wait_ge(sc_done, 1)

                def rows_of(g, i=None):
                    n, ch = c.acc + g, c.chunk + 2 * g
                    group_tile(n, ch, True, True, lambda k: scT[:, k, :], N, 2, i, 2, 1)
                    pe.wait_ge(evac[n % 4], up(n // 4 + 1, i, 1))

                with pe.Fori(0, 3) as i:
                    for g in range(4):
                        rows_of(g, i)
                        tr = c.tr + g
                        if g >= 2:
                            pe.wait_ge(tr_out, up(tr - 1, i, 4))
                        for j in range(4):
                            m = pe.matmul(trb[g % 2][:, 2 * j:2 * j + 2], modrow[:, g % 2, j * P:(j + 1) * P],
                                          ident[0:2, 0:2], start=True, stop=True)
                            if j == 0:
                                m.then_inc(owed.pop(), 1)
                        m.then_inc(tr_full, 1)
                    pe.wait_ge(tr_out, up(c.tr + 4, i, 4))
                c.acc += 12
                c.chunk += 24
                c.tr += 12
                for g in range(6):
                    rows_of(g)
                    for r in range(2 if g < 2 else 1):
                        if c.bc >= 2:
                            pe.wait_ge(bc_out, c.bc - 1)
                        mm(misc[c.bc % 2][:, :], pick[:, r, :], modrow[:, g % 2, :], True, True, bc_full)
                        c.bc += 1
                c.acc += 6
                c.chunk += 12

            def norm(tiles):
                for t_ in tiles:
                    pe.wait_ge(xn_done, c.xn + 1)
                    for h in range(2):
                        pe.wait_ge(tr_out, c.tr - 1) if c.tr >= 2 else None
                        for j in range(4):
                            m = pe.transpose(trb[c.tr % 2][:, j * P:(j + 1) * P],
                                             xn[:, c.xn % 2, (4 * h + j) * P:(4 * h + j + 1) * P], ident[:, :])
                        m.then_inc(tr_full, 1)
                        c.tr += 1
                    c.xn += 1
                pe.wait_ge(tr_out, c.tr)

            def ffn(nt):
                def flip(n, tr, i=None, nper=0, tper=0):
                    pe.wait_ge(evac[n % 4], up(n // 4 + 1, i, nper))
                    pe.wait_ge(tr_out, up(tr - 1, i, tper))
                    for j in range(2):
                        m = pe.transpose(trb[tr % 2][:, j * P:(j + 1) * P], gtok[:, tr % 2, j * P:(j + 1) * P],
                                         ident[:, :])
                        if j == 0 and owed:
                            m.then_inc(owed.pop(), 1)
                    m.then_inc(tr_full, 1)

                def group(g, i=None):
                    for t_ in range(nt):
                        q = g * nt + t_
                        group_tile(c.acc + q, c.chunk + 2 * g, t_ == 0, t_ == nt - 1,
                                   lambda k: xT[:, k, t_ * P:(t_ + 1) * P], N, P, i, 1, nt // 2)
                        if q:
                            flip(c.acc + q - 1, c.tr + q - 1, i, nt // 2, 2 * nt)

                group(0)
                with pe.Fori(0, (UG - 1) // 2) as i:
                    group(1, i)
                    group(2, i)
                c.acc += UG * nt
                c.chunk += 2 * UG
                c.tr += UG * nt
                flip(c.acc - 1, c.tr - 1)
                pe.wait_ge(tr_out, c.tr)
                down(nt, FT, gT)

            def down(nt, kt, src, w=0):
                for n in range(2):
                    for k in range(kt):
                        q = n * kt + k
                        ch = c.chunk + q // CW
                        if q % CW == 0:
                            chunk_wait(ch)
                        for t_ in range(nt):
                            if k == 0:
                                bank_wait(c.acc + t_)
                            inc = None
                            if k == kt - 1:
                                inc = acc_full
                            elif q % CW == CW - 1 and t_ == nt - 1:
                                inc = read[ch % SLOTS]
                            mm(acc[(c.acc + t_) % 4][:, :], src[:, k, t_ * P:(t_ + 1) * P],
                               ring[:, ch % SLOTS, q % CW, :], k == 0, k == kt - 1, inc)
                            if k == kt - 1 and q % CW == CW - 1 and t_ == nt - 1:
                                owed.append(read[ch % SLOTS])
                    c.acc += nt
                c.chunk += 2 * kt // CW

            def settled():
                for n in range(c.acc - 4, c.acc):
                    pe.wait_ge(evac[n % 4], n // 4 + 1)

            def dense_tokens(groups, tiles, src, width=N):
                for g in range(groups):
                    for n, t_ in enumerate(tiles):
                        group_tile(c.acc, c.chunk, n == 0, n == len(tiles) - 1,
                                   lambda k: src[:, k, t_ * P:(t_ + 1) * P], width)
                        c.acc += 1
                    c.chunk += 2

            def dense_features(lo, hi, jobs=(0, 1, 2, 3), rows=P):
                for m, j in enumerate(jobs):
                    bank_wait(c.acc)
                    last = m == len(jobs) - 1
                    for k in range(KD):
                        if m == 0 and k % CW == 0:
                            chunk_wait(c.chunk + k // CW)
                        inc = acc_full if k == KD - 1 else read[c.chunk % SLOTS] if last and k == CW - 1 else None
                        mm(acc[c.acc % 4][0:rows, 0:hi - lo],
                           ring[:, (c.chunk + k // CW) % SLOTS, k % CW, j * P:j * P + rows], xT[:, k, lo:hi],
                           k == 0, k == KD - 1, inc)
                    c.acc += 1
                owed.append(read[(c.chunk + 1) % SLOTS])
                c.chunk += 2

            def flips(src, tiles, kt):
                for t_ in tiles:
                    for u in range(kt // 4):
                        pe.wait_ge(tr_out, c.tr - 1)
                        for j in range(4):
                            m = pe.transpose(trb[c.tr % 2][:, j * P:(j + 1) * P],
                                             src[:, t_, (4 * u + j) * P:(4 * u + j + 1) * P], ident[:, :])
                        m.then_inc(tr_full, 1)
                        c.tr += 1
                pe.wait_ge(tr_out, c.tr)

            def mlstm():
                dense_features(0, S)
                dense_features(0, 2 * S)
                dense_tokens(2, range(4), xT)
                bank_wait(c.acc)
                for k in range(KD):
                    mm(acc[c.acc % 4][:, :], wg[:, k, :], xT[:, k, :], k == 0, k == KD - 1,
                       acc_full if k == KD - 1 else None)
                c.acc += 1
                dense_tokens(2, range(2), xT)
                dense_tokens(2, range(2), xT)
                settled()
                pe.wait_ge(rows_c, 2)
                for n in range(4):
                    pe.matmul(misc[0][:, n * 40:(n + 1) * 40], gr[:, n * P:(n + 1) * P], ident[0:40, 0:40],
                              start=True, stop=True)
                pe.wait_ge(em_done, 1)
                for n in range(2):
                    m = pe.matmul(misc[0][:, (4 + n) * 40:(5 + n) * 40], lfr[:, n * P:(n + 1) * P],
                                  ident[0:40, 0:40], start=True, stop=True)
                m.then_inc(cols_full, 1)
                pe.wait_ge(cols_out, 1)

                def scores(h):
                    a, lo = 2 * (h % 2), 64 * (h % 2)
                    if h >= 2:
                        pe.wait_ge(p_done, 2 * (h - 1))
                    for n in range(4):
                        pe.matmul(acc[a + n // 2][:, (n % 2) * S:(n % 2 + 1) * S],
                                  km[lo:lo + 64, h // 2, n * P:(n + 1) * P], qm[lo:lo + 64, h // 2, :],
                                  start=True, stop=True)
                    for d in range(2):
                        m = pe.matmul(trb[h % 2][:, d * S:(d + 1) * S],
                                      ident[0:40, 32 * d + h:32 * d + h + 1].to_broadcast([40, P]), zr[:, 0:S],
                                      start=True, stop=True)
                    m.then_inc(s_full, 1)

                def values(h):
                    if h >= 1:
                        pe.wait_ge(h_done, h)
                    for d in range(2):
                        pe.wait_ge(pm_done, 2 * h + d + 1)
                        for tt in range(2):
                            keys = [n for n in range(4) if n >= 2 or (n <= tt if d == 0 else n >= tt)]
                            for n in keys:
                                m = pe.matmul(misc[d][:, tt * 129:(tt + 1) * 129],
                                              Pm[:, 2 * (h % 2) + d, n, tt * P:(tt + 1) * P], va[:, n, h, :],
                                              start=n == keys[0], stop=n == keys[-1])
                    m.then_inc(pv_full, 1)

                for h in range(H + 1):
                    if h < H:
                        scores(h)
                    if h >= 1:
                        values(h - 1)

            def branch_out(src):
                c.hn += 1
                pe.wait_ge(hn_out, c.hn)
                flips(src, range(2), KD)
                dense_tokens(2, range(2), hT)

            def mix_out():
                c.y += 4
                pe.wait_ge(y_done, c.y)
                flips(y, range(2), KD)
                dense_tokens(2, range(2), hT)

            def pairs(l):
                return (trb, misc)[l % 2]

            def levels(d):
                for l, B in enumerate(LEVELS):
                    c.g += 1
                    pe.wait_ge(lv_g, c.g)
                    for hh in range(4):
                        if B == P:
                            k_, q_ = (0, 1) if d == 0 else (1, 0)
                            m = pe.matmul(pairs(l)[0][:, hh * P:(hh + 1) * P], G[:, l % 2, hh, k_ * P:(k_ + 1) * P],
                                          G[:, l % 2, hh, q_ * P:(q_ + 1) * P], start=True, stop=True)
                        else:
                            for st in range(2):
                                v = G[:, l % 2, hh, st * P:(st + 1) * P]
                                m = pe.matmul(pairs(l)[st][:, hh * P:(hh + 1) * P], v, v, start=True, stop=True)
                    m.then_inc(lv_a, 1)
                c.p += 8

            def context_products():
                c.g += 1
                pe.wait_ge(lv_g, c.g)
                for hh in range(4):
                    bank_wait(c.acc)
                    for st in range(2):
                        m = pe.matmul(acc[c.acc % 4][:, st * S:(st + 1) * S], G[:, 0, hh, st * P:(st + 1) * P],
                                      G[:, 1, hh, :], start=True, stop=True)
                    m.then_inc(acc_full, 1)
                    c.acc += 1

            def diagonal():
                pe.wait_ge(lv_p, c.p - 1)
                for hh in range(4):
                    for st in range(2):
                        m = pe.matmul(trb[st][:, hh * P:(hh + 1) * P], kd[:, hh, st * P:(st + 1) * P],
                                      qh[:, hh, st * P:(st + 1) * P], start=True, stop=True)
                m.then_inc(lv_a, 1)

            def hgrn():
                dense_tokens(2, range(2), xT)
                pe.wait_ge(permuted, 1)
                dense_tokens(2, range(4), xT)
                for hg in range(2):
                    dense_features(0, S)
                    for d in range(2):
                        dense_features(0, 2 * S)
                        levels(d)
                        context_products()
                    diagonal()
                    c.at += 1
                    pe.wait_ge(attn_done, c.at)
                    for tt in range(2):
                        bank_wait(c.acc)
                        for hh in range(4):
                            for n in range(4):
                                src = (Pl if n < 2 else Pc)[:, hh, n % 2, tt * P:(tt + 1) * P]
                                h = 4 * hg + hh
                                mm(acc[c.acc % 4][:, hh * P:(hh + 1) * P], src, vi[:, n, h * P:(h + 1) * P],
                                   n == 0, n == 3, acc_full if n == 3 and hh == 3 else None)
                        c.acc += 1
                dense_tokens(2, range(2), xT)

            def bias_toeplitz():
                pe.wait_ge(bias_dma, 32)
                for h in range(H):
                    if h >= 2:
                        pe.wait_ge(bias_out, h - 1)
                    pe.matmul(misc[h % 2][:, 0:RW], table[:, h:h + 1].to_broadcast([33, P]), onehot,
                              start=True, stop=True).then_inc(bias_rows, 1)

            def compress():
                for x in range(2):
                    bank_wait(c.acc)
                    for ht in range(2):
                        for l in range(16):
                            ch = c.chunk + l // 8
                            if ht == 0 and l % 8 == 0:
                                chunk_wait(ch)
                            inc = None
                            if ht == 1 and l == 15:
                                inc = acc_full
                            elif ht == 1 and l == 7:
                                inc = read[ch % SLOTS]
                            mm(acc[c.acc % 4][:, ht * 32:ht * 32 + 30],
                               ring[:, ch % SLOTS, l // 2 % CW, (l % 2) * S + ht * P:(l % 2) * S + (ht + 1) * P],
                               KK[:, x, :, l * 15:(l + 1) * 15], l == 0, l == 15, inc)
                    owed.append(read[(c.chunk + 1) % SLOTS])
                    c.acc += 1
                    c.chunk += 2
                settled()
                bank_wait(c.acc)
                b = acc[c.acc % 4]
                for g in range(2):
                    for ht in range(2):
                        mm(b[64 * g:64 * g + 64, 0:15], w2c[:, 0, ht, :], hid[:, 0, ht, 15 * g:15 * g + 15],
                           ht == 0, ht == 1)
                for g in range(2):
                    for ht in range(2):
                        mm(b[0:15, 64 + 64 * g:128 + 64 * g], hid[:, 1, ht, 15 * g:15 * g + 15], w2c[:, 1, ht, :],
                           ht == 0, ht == 1, acc_full if g and ht else None)
                c.acc += 1

            def attention():
                def scores(h):
                    g, j = divmod(h, 4)
                    a, f = 2 * (h % 2), slice(64 * g, 64 * g + 64)
                    if h >= 2:
                        pe.wait_ge(ns_m, c.ns + h - 1)
                    for kind in range(2):
                        b = acc[a + kind]
                        pe.matmul(b[:, 0:P], qa[f, j, 0:P], kk[f, kind, 0:P], start=True, stop=True)
                        pe.matmul(b[:, P:P + S], qa[f, j, P:S], kk[f, kind, :], start=True, stop=True)
                    pe.matmul(acc[a][:, 384:391], qa[f, j, 0:P], kcT[f, 0:7], start=True, stop=True)
                    pe.matmul(acc[a][:, 400:415], qa[f, j, P:S], kcT[f, 0:15], start=True,
                              stop=True).then_inc(ns_s, 1)

                def turn(h):
                    pe.wait_ge(ns_w, c.ns + h + 1)
                    if c.ns + h:
                        pe.wait_ge(ns_pa, c.ns + h)
                        pe.wait_ge(ns_pb, c.ns + h)
                    L = Lb[:, h % 2, :]
                    for kind in range(2):
                        for u in range(3):
                            o = kind * 384 + u * P
                            pe.transpose(trb[kind][:, u * P:(u + 1) * P], L[:, o:o + P], ident[:, :])
                    for tt in range(2):
                        m = pe.transpose(trb[tt][0:15, 384:N], L[:, 768 + 16 * tt:783 + 16 * tt], ident[:, :])
                    m.then_inc(ns_t, 1)

                def values(h):
                    g = h // 4
                    if h >= 2:
                        pe.wait_ge(ns_h, c.ns + h - 1)
                    pe.wait_ge(ns_pa, c.ns + h + 1)
                    pe.wait_ge(ns_pb, c.ns + h + 1)
                    f = slice(64 * g, 64 * g + 64)
                    b, T = misc[h % 2], PT[:, h % 2, :]
                    for kind in range(2):
                        pe.matmul(b[f, 0:S], vsw[:, 0, kind * P + 64 * g:kind * P + 64 * g + 64],
                                  T[:, kind * 384:kind * 384 + S], start=kind == 0, stop=False)
                    pe.matmul(b[f, 0:S], vcmp[:, g, :], T[0:15, 768:1024], start=False, stop=False)
                    for kind in range(2):
                        m = pe.matmul(b[f, P:S], vsw[:, 1, kind * P + 64 * g:kind * P + 64 * g + 64],
                                      T[:, kind * 384 + S:kind * 384 + 384], start=False, stop=kind == 1)
                    m.then_inc(ns_o, 1)

                for h in range(H + 2):
                    if h < H:
                        scores(h)
                    if h >= 2:
                        values(h - 2)
                    if 1 <= h <= H:
                        turn(h - 1)
                c.ns += H
                pe.wait_ge(ns_h, c.ns)

            def layer():
                norm(range(2))
                ffn(2)
                norm(range(2))
                dense_features(0, S)
                dense_features(0, S)
                bank_wait(c.acc)
                for k in range(KD):
                    if k % CW == 0:
                        chunk_wait(c.chunk + k // CW)
                    mm(acc[c.acc % 4][0:16, 0:S], ring[:, (c.chunk + k // CW) % SLOTS, k % CW, 280:296],
                       xT[:, k, 0:S], k == 0, k == KD - 1, acc_full if k == KD - 1 else None)
                c.acc += 1
                dense_tokens(1, range(2), xT, 280)
                settled()
                c.layer += 1
                pe.wait_ge(layer_in, LAYER * c.layer)
                compress()
                dense_tokens(2, range(2), xT)
                settled()
                attention()
                down(2, 4, oaT)
                dense_features(0, S)
                dense_features(0, S)
                for j in range(4):
                    bank_wait(c.acc)
                    mm(acc[c.acc % 4][:, 0:S], wa2[:, j * P:(j + 1) * P], alr, True, True, acc_full)
                    c.acc += 1
                dense_tokens(2, range(2), xT)
                levels(0)
                diagonal()
                c.at += 1
                pe.wait_ge(attn_done, c.at)
                settled()
                for tt in range(2):
                    for pair in range(2):
                        bank_wait(c.acc)
                        for hh in range(2):
                            for n in range(tt + 1):
                                h = 2 * pair + hh
                                mm(acc[c.acc % 4][:, hh * S:(hh + 1) * S], Pl[:, h, n, tt * P:(tt + 1) * P],
                                   vb[:, n, h * S:(h + 1) * S], n == 0, n == tt,
                                   acc_full if n == tt and hh == 1 else None)
                        c.acc += 1
                dense_tokens(2, range(2), xT)
                dense_tokens(2, range(2), xT)
                branch_out(Hx)
                mix_out2()
                norm(range(2))
                ffn(2)

            def mix_out2():
                c.y += 4
                pe.wait_ge(y_done, c.y)
                flips(y2, range(2), KD)
                dense_tokens(2, range(2), hT)

            modulation()
            norm(range(4))
            ffn(4)
            norm(range(4))
            mlstm()
            branch_out(Hm)
            hgrn()
            branch_out(Hx)
            mix_out()
            norm(range(2))
            ffn(2)
            bias_toeplitz()
            layer()
            layer()

        @block.scalar
        def _(act):
            c = Count()

            def step(ins):
                c.seq += 1
                ins.then_inc(act_seq, 1)
                act.wait_ge(act_seq, c.seq)

            act.dma_start(cT[:, :, :], t["cT"]).then_inc(consts, 16)
            act.dma_start(ident[:, :], t["ident"]).then_inc(consts, 16)
            act.dma_start(pick[:, :, :], t["pick"]).then_inc(consts, 16)
            act.dma_start(adab, t["adab"]).then_inc(consts, 16)
            act.dma_start(gains[:, :, :], t["gains"]).then_inc(consts, 16)
            act.dma_start(bF[:, :], t["bF"]).then_inc(consts, 16)
            act.dma_start(wg, t["wg"]).then_inc(consts, 16)
            act.dma_start(lbl[:, :, :, :], t["lbl"]).then_inc(consts, 16)
            act.dma_start(gains2[:, :, :], t["gains2"]).then_inc(consts, 16)
            act.dma_start(X[:, 0:2, :], t["x"]).then_inc(consts, 16)
            act.dma_start(X[:, 2:4, :], t["ctx"]).then_inc(consts, 16)

            def modulation():
                act.wait_ge(consts, CONSTS)
                act.activation(scT[:, :, :], cT[:, :, :], ACT.Silu).then_inc(sc_done, 1)
                c.acc += 12
                for g in range(6):
                    for r in range(2 if g < 2 else 1):
                        act.wait_ge(bc_full, c.bc + 1)
                        slot = 3 if r else g // 2
                        act.activation(gateB[:, slot, (g % 2) * N:(g % 2 + 1) * N], misc[c.bc % 2][:, :], ACT.Copy,
                                       scale=1.0 if slot == 1 else 0.5).then_inc(bc_out, 1)
                        c.bc += 1
                c.acc += 6

            def norm(tiles, last=False):
                if c.resid:
                    act.wait_ge(resid, c.resid)
                if c.layer:
                    settled()
                for n, t_ in enumerate(tiles):
                    step(act.activation(junk, X[:, t_, :], ACT.Square, accum_out=ss[:, n:n + 1]))
                act.activation(ss[:, 0:len(tiles)], ss[:, 0:len(tiles)], ACT.Copy, scale=1.0 / D).then_inc(squares, 1)
                c.norm += 1
                act.wait_ge(var_done, c.norm)
                act.activation(sd[:, 0:len(tiles)], var[:, 0:len(tiles)], ACT.Sqrt).then_inc(sd_done, 1)

            def ffn(nt):
                def gate(q, i=None):
                    n = c.acc + q
                    act.wait_ge(acc_full, up(n + 1, i, 2 * nt))
                    if q >= 2:
                        act.wait_ge(evac[(n - 2) % 4], up((n - 2) // 4 + 1, i, nt // 2))
                    act.activation(sil[:, n % 2, :], acc[n % 4][:, 0:256], ACT.Silu).then_inc(sil_done, 1)

                for q in range(nt):
                    gate(q)
                with act.Fori(0, (UG - 1) // 2) as i:
                    for q in range(nt, 3 * nt):
                        gate(q, i)
                c.acc += UG * nt + 2 * nt

            def mlstm():
                act.wait_ge(tr_out, c.tr_at_mix)
                act.dma_start(biasB, t["bT"][0:1, 0:3 * D].to_broadcast([P, 3 * D])).then_inc(bias_in, 16)
                act.dma_start(gainB, t["mgain"].to_broadcast([P, D])).then_inc(bias_in, 16)
                c.acc += 4
                for j in range(4):
                    act.wait_ge(acc_full, c.acc + 1)
                    act.activation(km[:, j, :], acc[c.acc % 4][:, :], ACT.Identity,
                                   bias=bF[:, 4 + j:5 + j]).then_inc(evac[c.acc % 4], 1)
                    c.acc += 1
                c.acc += 8 + 1 + 4 + 4
                act.wait_ge(rows_a, 1)
                step(act.activation(br, br, ACT.Exp, scale=-1.0))
                act.activation(br, br, ACT.Ln, bias=1.0).then_inc(rows_b, 1)
                act.wait_ge(rows_c, 2)
                act.activation(lfr[:, 0:S], lfr[:, 0:S], ACT.Exp, scale=-1.0).then_inc(em_done, 1)
                act.wait_ge(cols_out, 1)
                for h in range(H):
                    act.wait_ge(s_full, h + 1)
                    if h >= 2:
                        act.wait_ge(pv_full, h - 1)
                    for d in range(2):
                        for n in range(4):
                            lo = P if (n == 1 and d == 0) else 0
                            hi = P if (n == 0 and d == 1) else S
                            ins = act.activation(Pm[:, 2 * (h % 2) + d, n, lo:hi],
                                                 trb[h % 2][:, d * S + lo:d * S + hi], ACT.Exp,
                                                 bias=gcol[:, n, 32 * d + h:32 * d + h + 1])
                        ins.then_inc(d_done, 1)
                act.wait_ge(h_done, H)
                head_norm(ACT.Sigmoid, Hm, om)
                act.activation(gmx, gmx, ACT.Sigmoid).then_inc(merge_gate, 1)
                c.acc += 4
                c.tr += 4
                settled()

            def lower_bounds():
                act.wait_ge(lb_step, 1)
                act.activation(lbl[:, :, :, :], lbl[:, :, :, :], ACT.Exp).then_inc(lb_step, 1)

            def levels(d):
                for l, B in enumerate(LEVELS):
                    c.d += 1
                    act.wait_ge(lv_d, c.d)
                    v = E[:, l % 2, :, :].rearrange("p h (n a b) -> p (h n) a b", a=2, b=B)
                    act.activation(v[:, :, 1, :], v[:, :, 1, :], ACT.Exp)
                    act.activation(v[:, :, 0, :], v[:, :, 0, :], ACT.Exp, scale=-1.0).then_inc(lv_e, 1)

            def hgrn():
                act.dma_start(biasB, t["bT"][0:1, 3 * D:6 * D].to_broadcast([P, 3 * D])).then_inc(bias_in, 16)
                act.dma_start(gainB, t["hgain"].to_broadcast([P, D])).then_inc(bias_in, 16)
                act.dma_start(gateB[:, 3, 0:7 * P], t["masks"][0]).then_inc(masks_in, 16)
                act.dma_start(tmp[:, :, :].rearrange("p a b -> p (a b)")[:, 0:7 * P],
                              t["masks"][1]).then_inc(masks_in, 16)
                c.acc += 4 + 8
                for hg in range(2):
                    if hg:
                        act.wait_ge(attn_done, hg)
                    for j in range(4):
                        act.wait_ge(acc_full, c.acc + 1)
                        act.activation(qh[:, j, :], acc[c.acc % 4][:, 0:S], ACT.Silu,
                                       bias=bF[:, 8 + 4 * hg + j:9 + 4 * hg + j]).then_inc(evac[c.acc % 4], 1)
                        c.acc += 1
                    for d in range(2):
                        if d:
                            settled()
                        for j in range(4):
                            act.wait_ge(acc_full, c.acc + 1)
                            col = 16 + 8 * d + 4 * hg + j
                            act.activation(kh[:, j, :], acc[c.acc % 4][:, :], ACT.Sigmoid, scale=-1.0,
                                           bias=nbF[:, col:col + 1])
                            act.activation(lf[:, j, :], acc[c.acc % 4][:, :], ACT.Sigmoid,
                                           bias=bF[:, col:col + 1]).then_inc(evac[c.acc % 4], 1)
                            c.acc += 1
                        settled()
                        for j in range(4):
                            h = 4 * hg + j
                            ins = act.activation(lf[:, j, :], lf[:, j, :], ACT.Ln, scale=omlb[:, d, h:h + 1],
                                                 bias=lb[:, d, h:h + 1])
                        ins.then_inc(lf_done, 1)
                        levels(d)
                        c.g += 8
                        act.wait_ge(lv_g, c.g)
                        for j in range(4):
                            if d == 0:
                                act.activation(E[:, 0, j, :], cum[:, j, 1, 1:], ACT.Exp, scale=-1.0,
                                               bias=cum[:, j, 1, S:S + 1])
                            else:
                                act.activation(E[:, 1, j, :], cum[:, j, 0, 0:S], ACT.Exp, scale=-1.0,
                                               bias=cum[:, j, 0, S:S + 1])
                        if d == 0:
                            ins = act.activation(E[:, 1, :, :], cum[:, :, 0, 1:], ACT.Exp)
                        else:
                            ins = act.activation(E[:, 0, :, :], cum[:, :, 1, 0:S], ACT.Exp)
                        ins.then_inc(lv_e, 1)
                        c.g += 1
                        c.acc += 4
                    c.acc += 2
                for n in (c.acc - 2, c.acc - 1):
                    act.wait_ge(evac[n % 4], n // 4 + 1)
                c.acc += 4
                head_norm(ACT.Silu, Hx, gx)
                act.activation(ghx, ghx, ACT.Sigmoid).then_inc(merge_gate, 1)
                c.acc += 4 + 4
                c.resid += 4

            def settled():
                for n in range(c.acc - 4, c.acc):
                    act.wait_ge(evac[n % 4], n // 4 + 1)

            def head_norm(func, src, gate, heads=H):
                c.hn += 1
                act.activation(Pm[:, 0:2, :, :].rearrange("p a b c -> p (a b c)"),
                               src.rearrange("p a b -> p (a b)"), ACT.Square).then_inc(hn_sq, 1)
                act.wait_ge(hn_var, c.hn)
                act.activation(ssq[:, 0:2 * heads], ssq[:, 0:2 * heads], ACT.Sqrt).then_inc(hn_sd, 1)
                settled()
                act.activation(gate, gate, func).then_inc(hn_gate, 1)

            def attention():
                def exps(h):
                    act.wait_ge(ns_m, c.ns + h + 1)
                    L = Lb[:, h % 2, :]
                    for i, (lo, hi) in enumerate(SEGMENTS):
                        ins = act.activation(L[:, lo:hi], L[:, lo:hi], ACT.Exp, bias=mx[:, h % 2, i:i + 1],
                                             accum_out=sm[:, h % 2, i:i + 1])
                    ins.then_inc(ns_e, 1)

                def turned(h):
                    act.wait_ge(ns_t, c.ns + h + 1)
                    if h >= 2:
                        act.wait_ge(ns_o, c.ns + h - 1)
                    act.activation(PT[:, h % 2, 0:384], trb[0][:, 0:384], ACT.Copy)
                    act.activation(PT[0:15, h % 2, 768:896], trb[0][0:15, 384:N], ACT.Copy).then_inc(ns_pa, 1)

                def output(h):
                    act.wait_ge(ns_o, c.ns + h + 1)
                    g, j = divmod(h, 4)
                    f = slice(64 * g, 64 * g + 64)
                    act.activation(oaT[f, j, :], misc[h % 2][f, 0:S], ACT.Copy).then_inc(ns_h, 1)

                for h in range(H + 3):
                    if h < H:
                        exps(h)
                    if 2 <= h < H + 2:
                        turned(h - 2)
                    if h >= 3:
                        output(h - 3)
                c.ns += H

            def layer(l):
                norm(range(2))
                c.layer += 1
                ffn(2)
                norm(range(2))
                act.wait_ge(squares, c.norm)
                act.dma_start(pos, t["pos"][l]).then_inc(layer_in, 16)
                act.dma_start(w2c, t["w2c"][l]).then_inc(layer_in, 16)
                act.dma_start(wa2, t["wa2"][l]).then_inc(layer_in, 16)
                act.dma_start(ab, t["ab"][l]).then_inc(layer_in, 16)
                act.dma_start(gainC, t["ggain"][l:l + 1].to_broadcast([P, D])).then_inc(layer_in, 16)
                c.acc += 4 + 4 + 1 + 2
                settled()
                for x in range(2):
                    act.wait_ge(acc_full, c.acc + 1)
                    act.activation(hid[:, x, :, 0:30],
                                   acc[c.acc % 4][:, 0:64].rearrange("p (a b) -> p a b", b=32)[:, :, 0:30],
                                   ACT.Silu).then_inc(evac[c.acc % 4], 1)
                    c.acc += 1
                act.activation(ga, ga, ACT.Sigmoid).then_inc(ga_done, 1)
                c.acc += 1
                for g in range(2):
                    for t_ in range(2):
                        act.wait_ge(acc_full, c.acc + 1)
                        act.activation(gm2[:, t_, g * N:(g + 1) * N], acc[c.acc % 4][:, :],
                                       ACT.Sigmoid).then_inc(evac[c.acc % 4], 1)
                        c.acc += 1
                attention()
                c.acc += 4
                c.acc += 4
                for j in range(4):
                    act.wait_ge(acc_full, c.acc + 1)
                    act.activation(kh[:, j, 0:S], acc[c.acc % 4][:, 0:S], ACT.Copy).then_inc(evac[c.acc % 4], 1)
                    c.acc += 1
                c.acc += 4
                act.wait_ge(gl_a, 2 * l + 1)
                step(act.activation(G[:, 0, :, :], G[:, 0, :, :], ACT.Exp, scale=-1.0))
                act.activation(G[:, 0, :, :], G[:, 0, :, :], ACT.Ln, bias=1.0).then_inc(gl_l, 1)
                for n in range(4):
                    act.wait_ge(acc_full, c.acc + 1)
                    g, t_ = divmod(n, 2)
                    act.activation(vb[:, t_, g * N:(g + 1) * N], acc[c.acc % 4][:, :],
                                   ACT.Copy).then_inc(evac[c.acc % 4], 1)
                    c.acc += 1
                levels(0)
                c.g += 8
                c.acc += 4
                for dst, off, func in ((rx, 0, ACT.Copy), (gm2, D, ACT.Sigmoid)):
                    for n in range(4):
                        act.wait_ge(acc_full, c.acc + 1)
                        g, t_ = divmod(n, 2)
                        act.activation(dst[:, t_, off + g * N:off + (g + 1) * N], acc[c.acc % 4][:, :],
                                       func).then_inc(evac[c.acc % 4], 1)
                        c.acc += 1
                settled()
                head_norm(ACT.Silu, Hx, rx, 4)
                c.acc += 4 + 4
                c.tr += 8
                norm(range(2))
                ffn(2)

            modulation()
            lower_bounds()
            norm(range(4))
            ffn(4)
            c.resid += 8
            norm(range(4))
            c.tr_at_mix = 12 + 8 + 44 + 8
            mlstm()
            hgrn()
            norm(range(2))
            ffn(2)
            c.resid += 4
            norm(range(2))
            c.resid += 2
            layer(0)
            layer(1)
            norm(range(2))

        @block.vector
        def _(dve):
            c = Count()

            def step(ins):
                c.seq += 1
                ins.then_inc(dve_seq, 1)
                dve.wait_ge(dve_seq, c.seq)

            def modulation():
                dve.wait_ge(consts, CONSTS)

                def row(g, i=None):
                    n = c.acc + g
                    dve.wait_ge(acc_full, up(n + 1, i, 4))
                    at = n * N if i is None else (i * 4 + n) * N
                    a = adab[:, n * N:(n + 1) * N] if i is None else adab[:, bass.ds(i * (4 * N) + n * N, N)]
                    dve.tensor_tensor(out=modrow[:, n % 2, :], in0=acc[n % 4][0:2, :], in1=a,
                                      op=ALU.add).then_inc(evac[n % 4], 1)

                with dve.Fori(0, 3) as i:
                    for g in range(4):
                        row(g, i)
                        dve.wait_ge(tr_full, up(c.tr + g + 1, i, 4))
                        dve.tensor_copy(modT[:, bass.ds(i * 16 + 4 * g, 4), :],
                                        trb[g % 2][:, 0:8].rearrange("p (a b) -> p a b", b=2)).then_inc(tr_out, 1)
                c.acc += 12
                c.tr += 12
                for g in range(6):
                    if g >= 2:
                        dve.wait_ge(bc_full, 2 * (g - 1) if g <= 3 else g + 1)
                    row(g)
                c.acc += 6
                dve.wait_ge(tr_out, c.tr)
                for u, (s, r) in enumerate(((0, 0), (0, 1), (1, 0), (1, 1), (2, 0))):
                    dve.scalar_tensor_tensor(out=normA[:, u, :], in0=modT[:, (2 * s + 1) * 8:(2 * s + 2) * 8, r],
                                             scalar=1.0, in1=gains[:, s, :], op0=ALU.add,
                                             op1=ALU.mult).then_inc(mod_done, 1)
                dve.wait_ge(mod_done, 5)

            def norm(tiles, a_of, b_of):
                c.norm += 1
                m = len(tiles)
                dve.wait_ge(squares, c.norm)
                dve.tensor_scalar(var[:, 0:m], ss[:, 0:m], EPS, None, ALU.add).then_inc(var_done, 1)
                dve.wait_ge(sd_done, c.norm)
                step(dve.reciprocal(rstd[:, 0:m], sd[:, 0:m]))

                def scale(n):
                    if n >= 2:
                        dve.wait_ge(tr_full, c.tr + 2 * (n - 1))
                    dve.tensor_scalar(xn[:, (c.xn + n) % 2, :], X[:, tiles[n], :], rstd[:, n:n + 1], None,
                                      ALU.mult).then_inc(xn_done, 1)

                scale(0)
                for n, t_ in enumerate(tiles):
                    if n + 1 < m:
                        scale(n + 1)
                    for h in range(2):
                        tr = c.tr + 2 * n + h
                        dve.wait_ge(tr_full, tr + 1)
                        for j in range(4):
                            k = 4 * h + j
                            a, b = a_of(t_), b_of(t_)
                            ins = dve.tensor_scalar(xT[:, k, t_ * P:(t_ + 1) * P], trb[tr % 2][:, j * P:(j + 1) * P],
                                                    a[:, k:k + 1], None if b is None else b[:, k:k + 1], ALU.mult,
                                                    *([] if b is None else [ALU.add]))
                        ins.then_inc(tr_out, 1)
                c.tr += 2 * m
                c.xn += m

            def ffn(nt, update):
                def product(q, i=None):
                    n = c.acc + q
                    dve.wait_ge(sil_done, up(c.sil + q + 1, i, 2 * nt))
                    if q >= 2:
                        dve.wait_ge(tr_full, up(c.tr + q - 1, i, 2 * nt))
                    dve.tensor_tensor(out=gtok[:, (c.tr + q) % 2, :], in0=sil[:, n % 2, :], in1=acc[n % 4][:, 256:512],
                                      op=ALU.mult).then_inc(evac[n % 4], 1)

                def collect(q, i=None):
                    tr = c.tr + q
                    dve.wait_ge(tr_full, up(tr + 1, i, 2 * nt))
                    g, t_ = divmod(q, nt)
                    dst = gT[:, 2 * g:2 * g + 2, t_ * P:(t_ + 1) * P] if i is None else \
                        gT[:, bass.ds(i * 4 + 2 * g, 2), t_ * P:(t_ + 1) * P]
                    dve.tensor_copy(dst, trb[tr % 2][:, 0:256].rearrange("p (a b) -> p a b", b=P)).then_inc(tr_out, 1)

                for q in range(nt):
                    product(q)
                    if q:
                        collect(q - 1)
                with dve.Fori(0, (UG - 1) // 2) as i:
                    for q in range(nt, 3 * nt):
                        product(q, i)
                        collect(q - 1, i)
                c.acc += UG * nt
                c.sil += UG * nt
                collect(UG * nt - 1)
                c.tr += UG * nt
                for n in range(2):
                    for t_ in range(nt):
                        a = c.acc
                        dve.wait_ge(acc_full, a + 1)
                        update(t_, n, a)
                        c.acc += 1

            def gated(slot_of):
                def update(t_, n, a):
                    cols = slice(n * N, (n + 1) * N)
                    dve.tensor_tensor(out=tmp[:, a % 2, :], in0=acc[a % 4][:, :], in1=gateB[:, slot_of(t_), cols],
                                      op=ALU.mult).then_inc(evac[a % 4], 1)
                    dve.wait_ge(evac[a % 4], a // 4 + 1)
                    dve.tensor_tensor(out=X[:, t_, cols], in0=X[:, t_, cols], in1=tmp[:, a % 2, :],
                                      op=ALU.add).then_inc(resid, 1)
                return update

            def evacuate(dst, fn):
                dve.wait_ge(acc_full, c.acc + 1)
                fn(dst, acc[c.acc % 4]).then_inc(evac[c.acc % 4], 1)
                c.acc += 1

            def mlstm():
                dve.wait_ge(bias_in, 32)
                dve.memset(zr, 0.0)
                dve.memset(va[:, :, :, P:P + 1], 1.0)
                for j in range(4):
                    evacuate(qm[:, j, :], lambda o, b: dve.tensor_scalar(o, b[:, 0:S], bF[:, j:j + 1],
                                                                         64 ** -0.5, ALU.add, ALU.mult))
                c.acc += 4
                for g in range(2):
                    for t_ in range(4):
                        evacuate(va[:, t_, 4 * g:4 * g + 4, 0:P], lambda o, b: dve.tensor_tensor(
                            out=o, in0=b[:, :].rearrange("p (a b) -> p a b", b=P),
                            in1=biasB[:, g * N:(g + 1) * N].rearrange("p (a b) -> p a b", b=P), op=ALU.add))
                dve.wait_ge(acc_full, c.acc + 1)
                b = acc[c.acc % 4]
                dve.tensor_scalar(igr, b[0:40, :], bF[0:40, 32:33], None, ALU.add)
                dve.tensor_scalar(zr, b[64:104, :], bF[64:104, 32:33], None,
                                  ALU.add).then_inc(evac[c.acc % 4], 1)
                dve.wait_ge(evac[c.acc % 4], c.acc // 4 + 1)
                dve.scalar_tensor_tensor(out=br, in0=zr, scalar=-1.0, in1=zr, op0=ALU.mult,
                                         op1=ALU.max).then_inc(rows_a, 1)
                c.acc += 1
                for dst, off in ((om, D), (gmx, 2 * D)):
                    for g in range(2):
                        for t_ in range(2):
                            evacuate(dst[:, t_, g * N:(g + 1) * N], lambda o, b: dve.tensor_tensor(
                                out=o, in0=b[:, :], in1=biasB[:, off + g * N:off + (g + 1) * N], op=ALU.add))
                dve.wait_ge(rows_b, 1)
                step(dve.scalar_tensor_tensor(out=lfr, in0=zr, scalar=0.0, in1=br, op0=ALU.min,
                                              op1=ALU.subtract))
                LAT, CTX = slice(0, S), slice(S, 2 * S)
                BLAT, BCTX = slice(S - 1, None, -1), slice(2 * S - 1, S - 1, -1)

                def scan(dst, src, one, op0, op1, first):
                    for lo, cx, lt, end in ((0, CTX, LAT, 2 * S - 1), (32, BCTX, BLAT, S)):
                        r = slice(lo, lo + 8)
                        a = src if one is None else one
                        x0, x1 = (one[r, 0:S], one[r, 0:S]) if one is not None else (src[r, cx], src[r, lt])
                        step(dve.tensor_tensor_scan(dst[r, cx], x0, src[r, cx], first, op0, op1))
                        step(dve.tensor_tensor_scan(dst[r, lt], x1, src[r, lt], dst[r, end:end + 1], op0, op1))

                step(dve.memset(br, 0.0))
                scan(br, lfr, ones, ALU.mult, ALU.add, 0.0)
                step(dve.tensor_tensor(out=gr, in0=igr, in1=br, op=ALU.subtract))
                dve.memset(zr, 0.0).then_inc(rows_c, 1)
                dve.wait_ge(rows_c, 1)
                scan(zr, gr, None, ALU.max, ALU.max, 0.0)
                dve.tensor_tensor(out=lfr[:, 0:S], in0=br[:, 0:S], in1=zr[:, 0:S], op=ALU.add)
                dve.tensor_scalar(zr[:, 0:S], zr[:, 0:S], -1.0, None, ALU.mult).then_inc(rows_c, 1)
                dve.wait_ge(cols_full, 1)
                dve.tensor_copy(gcol[:, :, :], misc[0][:, 0:160].rearrange("p (a b) -> p a b", b=40))
                dve.tensor_copy(emc[:, :, :],
                                misc[0][:, 160:240].rearrange("p (a b) -> p a b", b=40)).then_inc(cols_out, 1)
                dve.wait_ge(cols_out, 1)

                def weights(h):
                    for d in range(2):
                        dve.wait_ge(d_done, 2 * h + d + 1)
                        a = 2 * (h % 2)
                        Q = Pm[:, a + d, :, :]
                        lat = acc[a][:, :].rearrange("p (a b) -> p a b", b=S)
                        cx = acc[a + 1][:, :].rearrange("p (a b) -> p a b", b=S)
                        lo, hi = (0, S) if d == 0 else (0, P)
                        dve.tensor_tensor(out=Q[:, 0, lo:hi], in0=lat[:, 0, lo:hi], in1=Q[:, 0, lo:hi], op=ALU.mult)
                        lo, hi = (P, S) if d == 0 else (0, S)
                        dve.tensor_tensor(out=Q[:, 1, lo:hi], in0=lat[:, 1, lo:hi], in1=Q[:, 1, lo:hi], op=ALU.mult)
                        dve.tensor_tensor(out=Q[:, 2:4, :], in0=cx, in1=Q[:, 2:4, :], op=ALU.mult).then_inc(p_done, 1)

                def outputs(h):
                    dve.wait_ge(pv_full, h + 1)
                    for d in range(2):
                        o = misc[d][:, 0:258].rearrange("p (a b) -> p a b", b=129)
                        ins = dve.tensor_tensor(out=den[:, d, :], in0=o[:, :, P], in1=emc[:, :, 32 * d + h],
                                                op=ALU.max)
                    step(ins)
                    for d in range(2):
                        o = misc[d][:, 0:258].rearrange("p (a b) -> p a b", b=129)
                        ins = dve.scalar_tensor_tensor(out=den[:, d, :], in0=o[:, :, P], scalar=-1.0,
                                                       in1=den[:, d, :], op0=ALU.mult, op1=ALU.max)
                    step(ins)
                    step(dve.reciprocal(rden[:, :, :], den[:, :, :]))
                    cols = slice(h * P, (h + 1) * P)
                    for tt in range(2):
                        ins = dve.tensor_scalar(Hm[:, tt, cols], misc[0][:, tt * 129:tt * 129 + P],
                                                rden[:, 0, tt:tt + 1], None, ALU.mult)
                    step(ins)
                    for tt in range(2):
                        ins = dve.scalar_tensor_tensor(out=Hm[:, tt, cols], in0=misc[1][:, tt * 129:tt * 129 + P],
                                                       scalar=rden[:, 1, tt:tt + 1], in1=Hm[:, tt, cols],
                                                       op0=ALU.mult, op1=ALU.add)
                    ins.then_inc(h_done, 1)

                for h in range(H + 1):
                    if h < H:
                        weights(h)
                    if h >= 1:
                        outputs(h - 1)
                dve.wait_ge(h_done, H)
                head_norm(H, P, Hm, om)

            def head_norm(heads, w, dst, gate, gain=gainB):
                c.hn += 1
                m = 2 * heads
                v = dst.rearrange("p a (b c) -> p (a b) c", c=w)
                dve.wait_ge(hn_sq, c.hn)
                step(dve.tensor_reduce(ssq[:, 0:m],
                                       Pm[:, 0:2, :, :].rearrange("p a b c -> p (a b c)").rearrange(
                                           "p (a b) -> p a b", b=w), AX.X, ALU.add))
                dve.tensor_scalar(ssq[:, 0:m], ssq[:, 0:m], 1.0 / w, EPS, ALU.mult, ALU.add).then_inc(hn_var, 1)
                dve.wait_ge(hn_sd, c.hn)
                step(dve.reciprocal(ssq[:, 0:m], ssq[:, 0:m]))
                step(dve.tensor_tensor(out=v, in0=v, in1=ssq[:, 0:m].unsqueeze(2).to_broadcast([P, m, w]),
                                       op=ALU.mult))
                step(dve.tensor_tensor(out=dst, in0=dst, in1=gain.unsqueeze(1).to_broadcast([P, 2, D]), op=ALU.mult))
                dve.wait_ge(hn_gate, c.hn)
                dve.tensor_tensor(out=dst, in0=dst, in1=gate, op=ALU.mult).then_inc(hn_out, 1)

            def collect_flips(dst, tiles, kt, grid=False):
                for t_ in tiles:
                    for u in range(kt // 4):
                        dve.wait_ge(tr_full, c.tr + 1)
                        src = trb[c.tr % 2][:, :].rearrange("p (a b) -> p a b", b=P)
                        if grid:
                            o = dst[:, 4 * u:4 * u + 4, :].rearrange("p a (r w) -> p a w r", r=4)
                            o = o[:, :, t_ * 32:(t_ + 1) * 32, :]
                            src = src.rearrange("p a (w r) -> p a w r", r=4)
                            for j in range(4):
                                ins = dve.tensor_copy(o[:, j], src[:, j])
                        else:
                            ins = dve.tensor_copy(dst[:, 4 * u:4 * u + 4, t_ * P:(t_ + 1) * P], src)
                        ins.then_inc(tr_out, 1)
                        c.tr += 1

            def merge_first():
                collect_flips(hT, range(2), KD)
                dve.wait_ge(merge_gate, 1)
                for g in range(2):
                    for t_ in range(2):
                        evacuate(y[:, t_, g * N:(g + 1) * N], lambda o, b: dve.tensor_tensor(
                            out=o, in0=b[:, :], in1=gmx[:, t_, g * N:(g + 1) * N], op=ALU.mult))

            def lower_bounds():
                m = den[:, :, :].rearrange("p a b -> p (a b)")
                dve.tensor_scalar(nbF[:, :], bF[:, :], -1.0, None, ALU.mult)
                step(dve.tensor_tensor(out=lb[:, :, :], in0=lbl[:, :, 0, :], in1=lbl[:, :, 1, :], op=ALU.max))
                dve.tensor_tensor(out=lbl[:, :, :, :].rearrange("p a b c -> p b a c")[:, 0], in0=lbl[:, :, 0, :],
                                  in1=lb[:, :, :], op=ALU.subtract)
                dve.tensor_tensor(out=lbl[:, :, 1, :], in0=lbl[:, :, 1, :], in1=lb[:, :, :],
                                  op=ALU.subtract).then_inc(lb_step, 1)
                dve.wait_ge(lb_step, 2)
                step(dve.tensor_tensor(out=omlb[:, :, :], in0=lbl[:, :, 0, :], in1=lbl[:, :, 1, :], op=ALU.add))
                step(dve.reciprocal(omlb[:, :, :], omlb[:, :, :]))
                step(dve.tensor_tensor(out=lb[:, :, :], in0=lbl[:, :, 0, :], in1=omlb[:, :, :], op=ALU.mult))
                dve.tensor_scalar(omlb[:, :, :], lb[:, :, :], -1.0, 1.0, ALU.mult, ALU.add).then_inc(lb_step, 1)

            def levels(d, mask):
                g0 = c.g

                def difference(l):
                    B = LEVELS[l]
                    if l >= 2:
                        dve.wait_ge(lv_g, g0 + l - 1)
                    nb = S // (2 * B)
                    v = cum[:, :, 0, 1 - d:S + 1 - d].rearrange("p h (n w) -> p h n w", w=2 * B)
                    ref = cum[:, :, 0, B:S:2 * B].unsqueeze(3).to_broadcast([P, 4, nb, 2 * B])
                    o = E[:, l % 2, :, :].rearrange("p h (n w) -> p h n w", w=2 * B)
                    dve.tensor_tensor(out=o, in0=v, in1=ref, op=ALU.subtract).then_inc(lv_d, 1)

                def operands(l):
                    B = LEVELS[l]
                    c.e += 1
                    dve.wait_ge(lv_e, c.e)
                    for half in range(2):
                        src = qh if half != d else kh[:, :, 0:S]
                        e_, g_, s_ = (v.rearrange("p h (n a b) -> p h n a b", a=2, b=B)[:, :, :, half, :]
                                      for v in (E[:, l % 2, :, :], G[:, l % 2, :, :], src))
                        ins = dve.tensor_tensor(out=g_, in0=s_, in1=e_, op=ALU.mult)
                    ins.then_inc(lv_g, 1)
                    c.g += 1

                def collect(l):
                    pair = (trb, misc)[l % 2]
                    c.a += 1
                    dve.wait_ge(lv_a, c.a)
                    if c.p:
                        dve.wait_ge(lv_p, c.p)
                    c.p += 1
                    if LEVELS[l] == P:
                        o = Pl[:, :, 0, P:S] if d == 0 else Pl[:, :, 1, 0:P]
                        dve.tensor_copy(o, pair[0][:, :].rearrange("p (h b) -> p h b", b=P)).then_inc(lv_p, 1)
                    else:
                        for st in range(2):
                            ins = dve.copy_predicated(Pl[:, :, st, st * P:(st + 1) * P],
                                                mask[:, l - 1, :].unsqueeze(1).to_broadcast([P, 4, P]),
                                                pair[st][:, :].rearrange("p (h b) -> p h b", b=P))
                        ins.then_inc(lv_p, 1)

                difference(0)
                for l in range(8):
                    if l < 7:
                        difference(l + 1)
                    operands(l)
                    if l:
                        collect(l - 1)
                collect(7)

            def diagonal():
                c.a += 1
                dve.wait_ge(lv_a, c.a)
                dve.wait_ge(lv_p, c.p)
                for st in range(2):
                    ins = dve.copy_predicated(Pl[:, :, st, st * P:(st + 1) * P],
                                              ident[:, :].bitcast(I32).unsqueeze(1).to_broadcast([P, 4, P]),
                                              trb[st][:, :].rearrange("p (h b) -> p h b", b=P))
                ins.then_inc(attn_done, 1)

            def hgrn():
                dve.wait_ge(bias_in, 64)
                dve.wait_ge(masks_in, 32)
                for g in range(2):
                    for t_ in range(2):
                        evacuate(ghx[:, t_, g * N:(g + 1) * N], lambda o, b: dve.tensor_tensor(
                            out=o, in0=b[:, :], in1=biasB[:, g * N:(g + 1) * N], op=ALU.add))
                step(dve.tensor_copy(xn[:, :, :].rearrange("p a b -> p (a b)").rearrange(
                    "p (a w r) -> p a w r", w=64, r=4), xT[:, :, 0:S].rearrange("p a (r w) -> p a w r", r=4)))
                dve.tensor_copy(xT[:, :, 0:S], xn[:, :, :].rearrange("p a b -> p (a b)").rearrange(
                    "p (a b) -> p a b", b=S)).then_inc(permuted, 1)
                for g in range(2):
                    for t_ in range(4):
                        evacuate(vi[:, t_, g * N:(g + 1) * N], lambda o, b: dve.tensor_tensor(
                            out=o, in0=b[:, :], in1=biasB[:, D + g * N:D + (g + 1) * N], op=ALU.add))
                for hg in range(2):
                    c.acc += 4
                    for d in range(2):
                        dve.memset(cum[:, :, :, 0:1], 0.0)
                        c.acc += 4
                        c.lf += 1
                        dve.wait_ge(lf_done, c.lf)
                        for j in range(4):
                            h = 4 * hg + j
                            dve.tensor_scalar(kh[:, j, :], kh[:, j, :], omlb[:, d, h:h + 1], None, ALU.mult)
                            for sg in range(2):
                                ins = dve.tensor_tensor_scan(cum[:, j, sg, 1:], ones[:, :],
                                                             lf[:, j, sg * S:(sg + 1) * S], 0.0, ALU.mult, ALU.add)
                        step(ins)
                        if d == 0:
                            step(dve.tensor_copy(kd, kh[:, :, 0:S]))
                        else:
                            step(dve.tensor_tensor(out=kd, in0=kd, in1=kh[:, :, 0:S], op=ALU.add))
                        levels(d, (maskf, maskb)[d])
                        c.e += 1
                        dve.wait_ge(lv_e, c.e)
                        dve.tensor_tensor(out=G[:, 0, :, :], in0=kh[:, :, S:2 * S], in1=E[:, 0, :, :], op=ALU.mult)
                        dve.tensor_tensor(out=G[:, 1, :, :], in0=qh, in1=E[:, 1, :, :],
                                          op=ALU.mult).then_inc(lv_g, 1)
                        c.g += 1
                        for j in range(4):
                            o = Pc[:, j, :, :].rearrange("p a b -> p (a b)")
                            evacuate(o, (lambda o, b: dve.tensor_copy(o, b[:, :])) if d == 0 else
                                     (lambda o, b: dve.tensor_tensor(out=o, in0=b[:, :], in1=o, op=ALU.add)))
                    diagonal()
                    for tt in range(2):
                        evacuate(Hx[:, tt, hg * N:(hg + 1) * N], lambda o, b: dve.tensor_copy(o, b[:, :]))
                for g in range(2):
                    for t_ in range(2):
                        evacuate(gx[:, t_, g * N:(g + 1) * N], lambda o, b: dve.tensor_tensor(
                            out=o, in0=b[:, :], in1=biasB[:, 2 * D + g * N:2 * D + (g + 1) * N], op=ALU.add))
                head_norm(H, P, Hx, gx)

            def merge_second():
                collect_flips(hT, range(2), KD, grid=True)
                dve.wait_ge(merge_gate, 2)
                scratch = cum.rearrange("p a b c -> p (a b c)")
                for g in range(2):
                    for t_ in range(2):
                        part = scratch[:, (2 * g + t_) * N:(2 * g + t_ + 1) * N]
                        cols = slice(g * N, (g + 1) * N)
                        evacuate(part, lambda o, b: dve.tensor_tensor(
                            out=o, in0=b[:, :], in1=ghx[:, t_, cols], op=ALU.mult))
                        n = c.acc - 1
                        dve.wait_ge(evac[n % 4], n // 4 + 1)
                        dve.tensor_tensor(out=y[:, t_, cols], in0=y[:, t_, cols], in1=part,
                                          op=ALU.add).then_inc(y_done, 1)
                collect_flips(hT, range(2), KD)

            def residual(update):
                for n in range(2):
                    for t_ in range(2):
                        dve.wait_ge(acc_full, c.acc + 1)
                        update(t_, n, c.acc)
                        c.acc += 1

            def bias_toeplitz():
                for h in range(H):
                    dve.wait_ge(bias_rows, h + 1)
                    dve.tensor_copy(rep_rows[:, h, :], misc[h % 2][:, 0:RW]).then_inc(bias_out, 1)

            def halved(t_, n, a):
                cols = slice(n * N, (n + 1) * N)
                dve.scalar_tensor_tensor(out=X[:, t_, cols], in0=acc[a % 4][:, :], scalar=0.5, in1=X[:, t_, cols],
                                         op0=ALU.mult, op1=ALU.add).then_inc(evac[a % 4], 1)

            def plain(t_, n, a):
                cols = slice(n * N, (n + 1) * N)
                dve.tensor_tensor(out=X[:, t_, cols], in0=acc[a % 4][:, :], in1=X[:, t_, cols],
                                  op=ALU.add).then_inc(evac[a % 4], 1)

            def attention():
                def maxima(h):
                    dve.wait_ge(ns_s, c.ns + h + 1)
                    if h >= 2:
                        dve.wait_ge(ns_t, c.ns + h - 1)
                    a, L = 2 * (h % 2), Lb[:, h % 2, :]
                    for i, (lo, hi) in enumerate(SEGMENTS):
                        tt = i % 2
                        if i < 4:
                            src = acc[a + i // 2][:, (P if tt else 0):(P + S if tt else P)]
                            b = TB[:, h, 0 if tt else P:S]
                        else:
                            src = acc[a][:, 384 + 16 * tt:384 + 16 * tt + hi - lo]
                            b = TB[:, h, (31 if tt else 159):S:16]
                        ins = dve.tensor_tensor_reduce(L[:, lo:hi], src, b, 1.0, MASK_FLOOR, ALU.add, ALU.max,
                                                       mx[:, h % 2, i:i + 1])
                    step(ins)
                    dve.tensor_scalar(mx[:, h % 2, :], mx[:, h % 2, :], -1.0, None, ALU.mult).then_inc(ns_m, 1)

                def scale(h):
                    dve.wait_ge(ns_e, c.ns + h + 1)
                    z, w, L = sm[:, h % 2, :], wt[:, h % 2, :], Lb[:, h % 2, :]
                    step(dve.tensor_scalar(z, z, 1e-30, None, ALU.max))
                    step(dve.reciprocal(z, z))
                    for kind, i in ((1, 0), (2, 2), (0, 4)):
                        ins = dve.tensor_tensor(out=w[:, i:i + 2], in0=z[:, i:i + 2], in1=ga[:, :, 3 * h + kind],
                                                op=ALU.mult)
                    step(ins)
                    for i, (lo, hi) in enumerate(SEGMENTS):
                        ins = dve.tensor_scalar(L[:, lo:hi], L[:, lo:hi], w[:, i:i + 1], None, ALU.mult)
                    ins.then_inc(ns_w, 1)

                def turned(h):
                    dve.wait_ge(ns_t, c.ns + h + 1)
                    if h >= 2:
                        dve.wait_ge(ns_o, c.ns + h - 1)
                    dve.tensor_copy(PT[:, h % 2, 384:768], trb[1][:, 0:384])
                    dve.tensor_copy(PT[0:15, h % 2, 896:1024], trb[1][0:15, 384:N]).then_inc(ns_pb, 1)

                dve.wait_ge(ga_done, c.layer)
                for h in range(H + 2):
                    if h < H:
                        maxima(h)
                    if h >= 2:
                        turned(h - 2)
                    if 1 <= h <= H:
                        scale(h - 1)
                c.ns += H

            def layer(l):
                c.layer += 1
                norm(range(2), lambda t_: gains2[:, 3 * l, :], lambda t_: None)
                ffn(2, halved)
                norm(range(2), lambda t_: gains2[:, 3 * l + 1, :], lambda t_: None)
                dve.wait_ge(layer_in, LAYER * c.layer)
                for j in range(4):
                    evacuate(qa[:, j, :], lambda o, b: dve.tensor_scalar(o, b[:, 0:S], 64 ** -0.5, None, ALU.mult))
                for j in range(2):
                    evacuate(kk[:, j, :], lambda o, b: dve.tensor_copy(o, b[:, 0:S]))
                for x in range(2):
                    dve.wait_ge(acc_full, c.acc + 1)
                    for g in range(2):
                        for half in range(2):
                            f = slice(64 * half, 64 * half + 64)
                            o = KK[f, x, g, :].rearrange("p (l c) -> p l c", c=15)
                            src = acc[c.acc % 4][64 * g:64 * g + 64, 16 * half:16 * half + 240]
                            ins = dve.tensor_tensor(out=o, in0=src.rearrange("p (c l) -> p l c", l=16),
                                                    in1=pos[f, x, :].unsqueeze(2).to_broadcast([64, 16, 15]),
                                                    op=ALU.add)
                    ins.then_inc(evac[c.acc % 4], 1)
                    c.acc += 1
                evacuate(alr, lambda o, b: dve.tensor_copy(o, b[0:16, 0:S]))
                for t_ in range(2):
                    dve.wait_ge(acc_full, c.acc + 1)
                    dve.tensor_copy(ga[:, t_, :], acc[c.acc % 4][:, S:S + 24])
                    dve.tensor_copy(vsw[:, t_, :], acc[c.acc % 4][:, 0:S]).then_inc(evac[c.acc % 4], 1)
                    c.acc += 1
                dve.memset(Lb[:, :, 768:800], 0.0).then_inc(pad_set, 1)
                dve.wait_ge(pad_set, l + 1)
                c.acc += 2
                dve.wait_ge(acc_full, c.acc + 1)
                dve.tensor_copy(kcT[:, 0:15], acc[c.acc % 4][:, 0:15])
                dve.tensor_copy(vcmp.rearrange("p a b -> p (a b)"),
                                acc[c.acc % 4][0:15, 64:192]).then_inc(evac[c.acc % 4], 1)
                c.acc += 1
                c.acc += 4
                attention()
                for n in range(2):
                    for t_ in range(2):
                        cols = slice(n * N, (n + 1) * N)
                        evacuate(y2[:, t_, cols], lambda o, b: dve.tensor_tensor(out=o, in0=b[:, :], in1=o,
                                                                                 op=ALU.mult))
                for j in range(4):
                    evacuate(qh[:, j, :], lambda o, b: dve.tensor_scalar(o, b[:, 0:S], 128 ** -0.5, None, ALU.mult))
                c.acc += 4
                for j in range(4):
                    evacuate(lf[:, j, 0:S], lambda o, b: dve.tensor_scalar(o, b[:, 0:S], ab[:, j:j + 1], None,
                                                                           ALU.add))
                n = c.acc - 1
                dve.wait_ge(evac[n % 4], n // 4 + 1)
                dve.scalar_tensor_tensor(out=G[:, 0, :, :], in0=lf[:, :, 0:S], scalar=-1.0, in1=lf[:, :, 0:S],
                                         op0=ALU.mult, op1=ALU.max).then_inc(gl_a, 1)
                dve.memset(cum[:, :, :, 0:1], 0.0)
                dve.memset(Pl[:, :, :, :], 0.0)
                dve.wait_ge(gl_l, l + 1)
                step(dve.scalar_tensor_tensor(out=lf[:, :, 0:S], in0=lf[:, :, 0:S], scalar=0.0, in1=G[:, 0, :, :],
                                              op0=ALU.min, op1=ALU.subtract))
                step(dve.tensor_scalar(lf[:, :, 0:S], lf[:, :, 0:S], 1.0 / 16, None, ALU.mult))
                for j in range(4):
                    ins = dve.tensor_tensor_scan(cum[:, j, 0, 1:], ones[:, :], lf[:, j, 0:S], 0.0, ALU.mult, ALU.add)
                step(ins)
                n = c.acc - 5
                dve.wait_ge(evac[n % 4], n // 4 + 1)
                dve.tensor_copy(kd, kh[:, :, 0:S]).then_inc(gl_a, 1)
                dve.wait_ge(gl_a, 2 * l + 2)
                c.acc += 4
                levels(0, maskf)
                diagonal()
                for tt in range(2):
                    for pair in range(2):
                        evacuate(Hx[:, tt, pair * N:(pair + 1) * N], lambda o, b: dve.tensor_copy(o, b[:, :]))
                c.acc += 8
                for n in range(c.acc - 4, c.acc):
                    dve.wait_ge(evac[n % 4], n // 4 + 1)
                head_norm(4, S, Hx, rx, gainC)
                collect_flips(hT, range(2), KD)
                scratch = cum.rearrange("p a b c -> p (a b c)")
                for g in range(2):
                    for t_ in range(2):
                        part = scratch[:, (2 * g + t_) * N:(2 * g + t_ + 1) * N]
                        cols = slice(g * N, (g + 1) * N)
                        gate = gm2[:, t_, D + g * N:D + (g + 1) * N]
                        evacuate(part, lambda o, b: dve.tensor_tensor(out=o, in0=b[:, :], in1=gate, op=ALU.mult))
                        n = c.acc - 1
                        dve.wait_ge(evac[n % 4], n // 4 + 1)
                        dve.tensor_tensor(out=y2[:, t_, cols], in0=y2[:, t_, cols], in1=part,
                                          op=ALU.add).then_inc(y_done, 1)
                collect_flips(hT, range(2), KD)
                residual(plain)
                norm(range(2), lambda t_: gains2[:, 3 * l + 2, :], lambda t_: None)
                ffn(2, halved)

            def block_norm(dst, gain, done):
                c.norm += 1
                dve.wait_ge(squares, c.norm)
                dve.tensor_scalar(var[:, 0:2], ss[:, 0:2], EPS, None, ALU.add).then_inc(var_done, 1)
                dve.wait_ge(sd_done, c.norm)
                step(dve.reciprocal(rstd[:, 0:2], sd[:, 0:2]))
                for t_ in range(2):
                    dve.scalar_tensor_tensor(out=dst[:, t_, :], in0=X[:, t_, :], scalar=rstd[:, t_:t_ + 1],
                                             in1=gain, op0=ALU.mult, op1=ALU.mult).then_inc(done, 1)

            modulation()
            dve.wait_ge(bc_out, 8)
            lower_bounds()
            norm(range(4), lambda t_: normA[:, t_ // 2, :], lambda t_: modT[:, 0:8, t_ // 2])
            ffn(4, gated(lambda t_: 0 if t_ < 2 else 3))
            norm(range(4), lambda t_: normA[:, 2 + t_ // 2, :], lambda t_: modT[:, 16:24, t_ // 2])
            dve.memset(ones[:, :], 1.0).then_inc(ones_set, 1)
            dve.wait_ge(ones_set, 1)
            mlstm()
            merge_first()
            hgrn()
            merge_second()
            residual(gated(lambda t_: 1))
            norm(range(2), lambda t_: normA[:, 4, :], lambda t_: modT[:, 32:40, 0])
            ffn(2, gated(lambda t_: 2))
            dve.wait_ge(final_in, 16)
            block_norm(X, gateB[:, 1, :], resid)
            bias_toeplitz()
            dve.wait_ge(bias_done, 32)
            layer(0)
            layer(1)
            dve.wait_ge(final_in, 32)
            block_norm(xn, gainC, out_done)

        @block.gpsimd
        def _(gp):
            c = Count()
            for h in range(H):
                for d in range(2):
                    gp.wait_ge(p_done, 2 * h + d + 1)
                    for n in range(2):
                        v = Pm[:, 2 * (h % 2) + d, n, n * P:(n + 1) * P]
                        sign = 1 if d == 0 else -1
                        ins = gp.affine_select(out=v, in_=v, compare_op=ALU.is_ge, fill=0.0, base=0,
                                               pattern=[[sign, P]], channel_multiplier=-sign)
                    ins.then_inc(pm_done, 1)
            gp.wait_ge(resid, 12)
            gp.dma_start(gateB[:, 1, :], t["fgain"][0:1].to_broadcast([P, D])).then_inc(final_in, 16)
            gp.dma_start(onehot, t["onehot"]).then_inc(bias_dma, 16)
            gp.dma_start(table, t["table"]).then_inc(bias_dma, 16)
            gp.wait_ge(bias_out, H)
            gp.dma_start(t["scratch"], rep_rows).then_inc(bias_done, 16)
            gp.wait_ge(bias_done, 16)
            gp.dma_start(TB, bass.AP(t["scratch"].tensor, P - 1, [[H * RW - 1, P], [RW, H], [1, S]])).then_inc(
                bias_done, 16)
            gp.wait_ge(hn_out, 4)
            gp.dma_start(gainC, t["fgain"][1:2].to_broadcast([P, D])).then_inc(final_in, 16)
            for t_ in range(2):
                gp.wait_ge(out_done, t_ + 1)
                gp.dma_start(out[0, t_ * P:(t_ + 1) * P, :], xn[:, t_, :]).then_inc(stored, 16)
            gp.wait_ge(stored, 32)


CONSTS = 16 * 11
LAYER = 16 * 5
MASK_FLOOR = -1e25
SEGMENTS = ((0, 128), (128, 384), (384, 512), (512, 768), (768, 775), (784, 799))


def level_masks():
    p = np.arange(P)
    out = np.zeros((2, P, 7, P), np.float32)
    for n in range(7):
        B = 64 >> n
        m = (p[:, None] // (2 * B) == p // (2 * B)) & (p[:, None] % (2 * B) < B) & (p % (2 * B) >= B)
        out[0, :, n], out[1, :, n] = m, m.T
    return out.reshape(2, P, 7 * P)


def distance_buckets():
    d = 255 - np.arange(384)
    nf = np.maximum(d, 1).astype(np.float32)
    b = 16 + (np.log(nf / np.float32(16)) / np.float32(math.log(64)) * np.float32(16)).astype(np.int32)
    b = np.where(d < 0, 32, np.where(d < 16, d, np.minimum(b, 31)))
    return (b == np.arange(33)[:, None]).astype(np.float32)


def groups_of(w, col_lists):
    k = w.shape[0] // P
    for cols in col_lists:
        g = np.zeros((P, k, N), np.float32)
        g[:, :, :len(cols)] = w[:, cols].reshape(k, P, len(cols)).transpose(1, 0, 2)
        yield g


def kernel(**inputs):
    import concourse.bacc as bacc
    from concourse.bass_utils import run_bass_kernel_spmd as run

    v = {k: np.asarray(a) for k, a in inputs.items()}
    r = np.arange
    tiles = []

    def add(w, col_lists):
        for g in groups_of(w, col_lists):
            tiles.extend(g[:, k] for k in range(g.shape[1]))

    halves = [r(0, N), r(N, 2 * N)]
    add(v["ada_w"][0], [m * D + h for m in MODS for h in halves])
    up_cols = [np.concatenate([g * 256 + r(256), F + g * 256 + r(256)]) for g in range(UG)]
    add(v["ffn1_w_in"][0], up_cols)
    add(v["ffn1_w_out"][0], halves)
    w, b = v["mix_w_in"][0], v["mix_b_in"][0]
    Q0, K0, V0, O0, I0, F0, HQ0, HF0, HI0, HG0, GM0, GH0 = np.cumsum(
        [0, 512, 512, D, D, 16, 16, D, 2 * D, D, D, D])
    add(w, [Q0 + r(N), K0 + r(N), V0 + r(N), V0 + N + r(N), O0 + r(N), O0 + N + r(N), GM0 + r(N), GM0 + N + r(N)])
    add(v["proj_m"][0], halves)
    add(w, [GH0 + r(N), GH0 + N + r(N), HI0 + r(N), HI0 + N + r(N)])
    for hg in range(2):
        add(w, [HQ0 + hg * N + r(N), HF0 + hg * N + r(N), HF0 + D + hg * N + r(N)])
    add(w, [HG0 + r(N), HG0 + N + r(N)])
    add(v["proj_h"][0], halves)
    add(v["mix_w_out"][0], halves)
    add(v["ffn2_w_in"][0], up_cols)
    add(v["ffn2_w_out"][0], halves)
    WI = np.cumsum([0, 512, 768, 24, 512, 512, D, 16, D, 2 * D])
    QA, KV, GA, QB, KB, VB, AL, RB, GM = WI[:9]
    head_pairs = np.concatenate([np.concatenate([h * 64 + r(64), (h + 4) * 64 + r(64)]) for h in range(4)])
    for l in range(2):
        w2 = v["w_in_2"][l]

        def ffn(a, b, c_):
            add(np.concatenate([v[a][l], v[b][l]], 1), up_cols)
            add(v[c_][l], halves)

        ffn("ffn1_w_gate_2", "ffn1_w_up_2", "ffn1_w_down_2")
        kv = [KV + n * P + r(P) for n in range(6)]
        add(w2, [QA + head_pairs, np.concatenate([kv[2], kv[4], kv[0], kv[1]]),
                 np.concatenate([kv[3], kv[5], GA + r(24), AL + r(16)])])
        for name in ("cmp_k_w1_2", "cmp_v_w1_2"):
            w1 = v[name][l].reshape(2, 16, 64, S).transpose(0, 2, 1, 3).reshape(P, KD, N)
            tiles.extend(w1[:, k] for k in range(KD))
        add(w2, [GM + r(N), GM + N + r(N)])
        add(v["w_branch_nsa_2"][l][head_pairs], halves)
        add(w2, [QB + r(N), KB + r(N), VB + r(N), VB + N + r(N), RB + r(N), RB + N + r(N),
                 GM + D + r(N), GM + D + N + r(N)])
        add(v["w_branch_gla_2"][l], halves)
        add(v["w_out_2"][l], halves)
        ffn("ffn2_w_gate_2", "ffn2_w_up_2", "ffn2_w_down_2")
    wg = np.zeros((D, P), np.float32)
    bg = np.zeros(P, np.float32)
    for n, at in enumerate((I0, I0 + 8, F0, F0 + 8)):
        wg[:, 32 * n:32 * n + 8] = w[:, at:at + 8]
        bg[32 * n:32 * n + 8] = b[at:at + 8]
    bF = np.concatenate([b[Q0:V0], b[HQ0:HI0], bg]).reshape(33, P).T
    bT = np.concatenate([b[V0:I0], b[GM0:GH0], b[GH0:], b[HI0:GM0]])[None]
    stream = np.stack(tiles).reshape(-1, CW, P, N).transpose(0, 2, 1, 3)

    def feat(a):
        return np.moveaxis(a.reshape(*a.shape[:-1], KD, P), -1, 0)

    arrays = {
        "stream": stream,
        "cT": feat(np.stack([v["c"][0], v["c_ctx"]])).transpose(0, 2, 1),
        "ident": np.eye(P, dtype=np.float32),
        "pick": np.repeat(np.eye(2, dtype=np.float32)[:, :, None], P, 2),
        "adab": np.repeat(np.concatenate([v["ada_b"][0][m * D:(m + 1) * D] for m in MODS])[None], 2, 0),
        "gains": feat(np.stack([v["ffn1_norm"][0], v["mix_norm"][0], v["ffn2_norm"][0]])),
        "bF": bF,
        "bT": bT,
        "mgain": v["mlstm_norm"],
        "hgain": v["hgrn_norm"],
        "lbl": v["hgrn_lb_logits"].reshape(2, 2, KD, P).transpose(3, 0, 1, 2),
        "masks": level_masks(),
        "gains2": feat(np.stack([v[n][l] for l in range(2) for n in ("ffn1_norm_2", "mix_norm_2", "ffn2_norm_2")])),
        "onehot": distance_buckets(),
        "table": np.concatenate([v["rel_table_2"], np.full((1, 8), -1e30, np.float32)]),
        "pos": np.stack([v["cmp_pos_k_2"], v["cmp_pos_v_2"]], 1).reshape(2, 2, 2, 16, 64)
                 .transpose(0, 2, 4, 1, 3).reshape(2, P, 2, 16),
        "w2c": np.stack([v["cmp_k_w2_2"], v["cmp_v_w2_2"]], 1).reshape(2, 2, 2, P, 64).transpose(0, 3, 1, 2, 4),
        "wa2": v["gla_a_w2_2"],
        "ab": v["gla_a_b_2"].reshape(2, 4, P).transpose(0, 2, 1),
        "ggain": v["gla_out_norm_2"],
        "fgain": np.stack([v["final_norm"], v["final_norm_2"]]),
        "wg": wg.reshape(KD, P, P).transpose(1, 0, 2),
        "x": v["x"][0].reshape(ST, P, D).transpose(1, 0, 2),
        "ctx": v["ctx"][0].reshape(ST, P, D).transpose(1, 0, 2),
    }
    arrays = {k: np.ascontiguousarray(a) for k, a in arrays.items()}
    nc = bacc.Bacc("TRN2", target_bir_lowering=False, num_devices=1)
    t = {k: nc.dram_tensor("in_" + k, a.shape, F32, kind="ExternalInput").ap() for k, a in arrays.items()}
    t["scratch"] = nc.dram_tensor("bias_scratch", (P, 8, 384), F32).ap()
    out = nc.dram_tensor("out", (1, S, D), F32, kind="ExternalOutput").ap()
    build(nc, t, out)
    res = run(nc, [{"in_" + k: a for k, a in arrays.items()}], core_ids=[0])
    return res.results[0]["out"]
```

```python
import math
import numpy as np
import concourse.bass as bass
from concourse import mybir
from contextlib import ExitStack

F32 = mybir.dt.float32
F32R = mybir.dt.float32r
I32 = mybir.dt.int32
ALU = mybir.AluOpType
ACT = mybir.ActivationFunctionType
AX = mybir.AxisListType

P = 128
D = 1024
KD = D // P
S = 256
ST = S // P
F = 2816
FT = F // P
UG = F // 256
N = 512
CW = 4
FIRST = 16512
SLOTS = 4
EPS = 1e-6
MODS = (0, 1, 3, 4, 6, 7, 2, 5, 8)


def build(nc, t, out):
    ctx = ExitStack()
    with ctx:
        def sb(name, shape, dt=F32):
            return ctx.enter_context(nc.sbuf_tensor(name, shape, dt))

        def sem(name):
            return ctx.enter_context(nc.semaphore(name))

        ring = sb("ring", [P, SLOTS, CW, N])
        xT = sb("xT", [P, KD, 2 * S])
        ARENA = 26 * 1024
        arena = sb("arena", [P, ARENA])
        AT_XT = FIRST + 4 * SLOTS * CW * N
        AT_ARENA = AT_XT + 4 * KD * 2 * S

        def parts(name, at, *shape):
            return nc.alloc_sbuf_tensor_at(name, [P, *shape], F32R, offset=at)

        ring_r = parts("ring_parts", FIRST, SLOTS, CW, N)
        xT_r = parts("xT_parts", AT_XT, KD, 2 * S)
        X = sb("X", [P, 2 * ST, D])
        xn = sb("xn", [P, 2, D])
        ident = sb("ident", [P, P])
        cT = sb("cT", [P, KD, 2])
        scT = sb("scT", [P, KD, 2])
        gains = sb("gains", [P, 3, KD])
        pick = sb("pick", [2, 2, P])
        modT = sb("modT", [P, 48, 2])
        normA = sb("normA", [P, 5, KD])
        gateB = sb("gateB", [P, 4, D])
        ss = sb("ss", [P, 4])
        var = sb("var", [P, 4])
        sd = sb("sd", [P, 4])
        rstd = sb("rstd", [P, 4])
        tmp = sb("tmp", [P, 2, N])
        modrow = sb("modrow", [2, 2, N])

        def room(at, *shape, parts=P):
            size = int(np.prod(shape))
            assert at + size <= ARENA
            v = arena[0:parts, at:at + size]
            if len(shape) == 2:
                return v.rearrange("p (a b) -> p a b", b=shape[1])
            if len(shape) == 3:
                return v.rearrange("p (a b c) -> p a b c", b=shape[1], c=shape[2])
            return v

        gT = room(0, FT, 2 * S)
        adab = room(0, 18 * N, parts=2)
        junk = room(FT * 2 * S, D)
        sil = room(FT * 2 * S + D, 2, 256)
        gtok = room(FT * 2 * S + D + 512, 2, 256)

        xTl = room(13312, KD, 2 * S)
        xTl_r = parts("xT_low_parts", AT_ARENA + 4 * 13312, KD, 2 * S)
        gT_r = parts("gT_parts", AT_ARENA, FT, 2 * S)
        high = parts("ring_high", AT_ARENA + 4 * 17408, SLOTS, CW * N)

        def x_low(nt, k, t_, parts=False):
            if nt == 4:
                return (xTl_r if parts else xTl)[:, k, t_ * P:(t_ + 1) * P]
            return (xT_r if parts else xT)[:, k, S + t_ * P:S + (t_ + 1) * P]

        H = 8
        wg = room(ARENA - KD * P, KD, P)
        biasB = room(0, 3 * D)
        gainB = room(3072, D)
        qm = room(4096, 4, S)
        km = room(5120, 4, 2 * S)
        va = room(7168, 4, H, P + 1)
        om = room(11296, ST, D)
        gmx = room(13344, ST, D)
        Hm = room(15392, ST, D)
        Pm = room(17440, 4, 4, S)
        hT = room(21536, KD, S)
        vi = room(4096, 4, D)
        ghx = room(8192, ST, D)
        qh = room(10240, 4, S)
        kh = room(11264, 4, 2 * S)
        gx = room(11264, ST, D)
        cum = room(13312, 4, 2, S + 1)
        lf = room(15376, 4, 2 * S)
        E = room(15376, 2, 4, S)
        G = room(17424, 2, 4, S)
        Pl = room(19472, 4, 2, S)
        Pc = room(21520, 4, 2, S)
        kd = room(23568, 4, S)
        Hx = xn[:, :, :]
        y = X[:, 2:4, :]
        rows = xn[:, :, :].rearrange("p a b -> p (a b)")
        igr, lfr, br, gr = (rows[0:40, n * N:(n + 1) * N] for n in range(4))
        zr = gateB[0:40, 3, 0:N]
        gcol = sb("gcol", [P, 4, 40])
        emc = sb("emc", [P, ST, 40])
        bF = sb("bF", [P, 33])
        den = sb("den", [P, 2, ST])
        rden = sb("rden", [P, 2, ST])
        ones = sb("ones", [P, S])
        ssq = sb("ssq", [P, 16])
        lbl = sb("lbl", [P, 2, 2, H])
        lb = sb("lb", [P, 2, H])
        omlb = sb("omlb", [P, 2, H])
        nbF = sb("nbF", [P, 33])
        maskf = gateB[:, 3, 0:7 * P].rearrange("p (a b) -> p a b", b=P).bitcast(I32)
        maskb = tmp[:, :, :].rearrange("p a b -> p (a b)")[:, 0:7 * P].rearrange("p (a b) -> p a b", b=P).bitcast(I32)
        gains2 = sb("gains2", [P, 6, KD])
        TB = X[:, 2:4, :].rearrange("p a b -> p (a b)").rearrange("p (a b) -> p a b", b=S)
        RW = 384
        rep_rows = room(14336, H, RW)
        onehot = room(13312, RW, parts=33)
        table = room(13696, H, parts=33)
        qa = room(0, 4, S)
        kk = room(1024, 2, S)
        KK = room(1536, 2, 2, 240)
        pos = room(2496, 2, 16)
        w2c = room(2528, 2, 2, 64)
        hid = room(2784, 2, 2, 32)
        kcT = room(2912, 16)
        vcmp = room(2928, 2, 64, parts=15)
        vsw = room(3056, 2, S)
        ga = room(3568, 2, 24)
        alr = room(3616, S, parts=16)
        wa2 = room(3872, N, parts=16)
        ab = room(4384, 4)
        gm2 = room(4400, ST, 2 * D)
        oaT = room(8496, 4, S)
        Lb = room(10240, 2, 800)
        PT = room(11840, 2, 1024)
        mx = room(13888, 2, 6)
        sm = room(13900, 2, 6)
        wt = room(13912, 2, 6)
        vb = room(21520, ST, D)
        rx = gateB[:, 0:2, :]
        gainC = gateB[:, 2, :]
        y2 = gm2[:, :, 0:D]
        LEVELS = (128, 64, 32, 16, 8, 4, 2, 1)

        bank = [ctx.enter_context(nc.psum_tensor(f"bank{i}", [P, N], F32)) for i in range(8)]
        acc, trb, misc = bank[0:4], bank[4:6], bank[6:8]

        loaded = [sem(f"chunk_loaded{i}") for i in range(SLOTS)]
        read = [sem(f"chunk_read{i}") for i in range(SLOTS)]
        high_ready = sem("high_parts")
        low_ready = [sem("low_parts_even"), sem("low_parts_odd")]
        step_low = sem("low_parts_step")
        consts = sem("consts_loaded")
        more_consts = sem("more_consts_loaded")
        acc_full = sem("acc_full")
        evac = [sem(f"evacuated{i}") for i in range(4)]
        sil_done = sem("sil_done")
        tr_full = sem("transposed")
        tr_out = sem("transposed_out")
        sc_done = sem("sc_done")
        bc_full = sem("gate_rows_broadcast")
        bc_out = sem("gate_rows_out")
        mod_done = sem("mod_done")
        resid = sem("residual_updated")
        squares = sem("squares_summed")
        var_done = sem("var_done")
        sd_done = sem("sd_done")
        xn_done = sem("xn_done")
        stored = sem("stored")
        bias_in = sem("mix_biases_loaded")
        rows_a = sem("gate_rows_ready")
        rows_b = sem("gate_rows_log")
        rows_c = sem("gate_rows_scanned")
        cols_full = sem("gate_columns")
        cols_out = sem("gate_columns_out")
        em_done = sem("exp_minus_m")
        s_full = sem("mlstm_scores")
        d_done = sem("mlstm_decays")
        p_done = sem("mlstm_weights")
        pm_done = sem("mlstm_weights_masked")
        pv_full = sem("mlstm_values")
        h_done = sem("mlstm_head_done")
        hn_sq = sem("head_norm_squares")
        hn_var = sem("head_norm_var")
        hn_sd = sem("head_norm_sd")
        hn_gate = sem("head_norm_gate")
        hn_out = sem("head_norm_done")
        lb_step = sem("lower_bound")
        bias_rows = sem("bias_rows")
        bias_out = sem("bias_rows_out")
        bias_dma = sem("bias_dma")
        bias_done = sem("bias_toeplitz")
        layer_in = sem("layer_constants_loaded")
        final_in = sem("final_gain_loaded")
        ga_done = sem("branch_gates")
        ns_s = sem("nsa_scores")
        ns_m = sem("nsa_maxima")
        ns_e = sem("nsa_exponentials")
        ns_w = sem("nsa_probabilities")
        ns_t = sem("nsa_transposed")
        ns_pa = sem("nsa_transposed_out_a")
        ns_pb = sem("nsa_transposed_out_b")
        ns_o = sem("nsa_outputs")
        ns_h = sem("nsa_head_done")
        gl_a = sem("gla_abs")
        gl_l = sem("gla_log")
        pad_set = sem("pad_set")
        out_done = sem("out_done")
        masks_in = sem("level_masks_loaded")
        permuted = sem("column_major_input")
        lf_done = sem("log_decays")
        lv_d = sem("level_differences")
        lv_e = sem("level_decays")
        lv_g = sem("level_operands")
        lv_a = sem("level_products")
        lv_p = sem("level_collected")
        attn_done = sem("attention_whole")
        merge_gate = sem("merge_gate")
        y_done = sem("merged")
        ones_set = sem("ones_set")
        dve_seq = sem("vector_step")
        act_seq = sem("scalar_step")

        NCH = t["stream"].shape[0]
        block = ctx.enter_context(nc.Block())

        class Count:
            def __init__(self):
                self.lowstep, self.low, self.high, self.block = 0, [0, 0], 0, 0
                self.chunk = self.acc = self.tr = self.bc = self.sil = self.resid = self.norm = self.xn = self.seq = 0
                self.hn = self.y = self.d = self.e = self.g = self.a = self.p = 0
                self.lf = self.ns = self.layer = self.at = 0

        block_chunk = []

        def chunks_split(nt):
            return 2 * UG if nt == 4 else 2 * UG + 2 * FT // CW

        def lows(nt, odd):
            return (chunks_split(nt) + 1 - odd) // 2

        def up(v, i, per):
            return v if i is None else v + i * per

        @block.sync
        def _(sp):
            for j in range(SLOTS):
                sp.dma_start(ring[:, j], t["stream"][j]).then_inc(loaded[j], 16)
            turns = NCH // SLOTS
            with sp.Fori(1, turns) as i:
                for j in range(SLOTS):
                    sp.wait_ge(read[j], i)
                    sp.dma_start(ring[:, j], t["stream"][i * SLOTS + j]).then_inc(loaded[j], 16)
            for n in range(turns * SLOTS, NCH):
                sp.wait_ge(read[n % SLOTS], n // SLOTS)
                sp.dma_start(ring[:, n % SLOTS], t["stream"][n]).then_inc(loaded[n % SLOTS], 16)

        @block.tensor
        def _(pe):
            c = Count()
            owed = []

            def mm(o, l, r, start, stop, inc=None):
                m = pe.matmul(o, l, r, start=start, stop=stop)
                if inc is not None:
                    m.then_inc(inc, 1)
                elif owed:
                    m.then_inc(owed.pop(), 1)

            def chunk_wait(n, i=None, per=0):
                pe.wait_ge(loaded[n % SLOTS], up(16 * (n // SLOTS + 1), i, 16 * per))

            def bank_wait(n, i=None, per=0):
                if n >= 4:
                    pe.wait_ge(evac[n % 4], up(n // 4, i, per))

            def low_wait(j, i=None):
                pe.wait_ge(low_ready[j % 2], up(c.low[j % 2] + j // 2 + 1, i, 2))

            def mm3(o, lh, ll, slot, k, start, stop, inc=None):
                w = high[:, slot, k * N:(k + 1) * N]
                mm(o, lh, ring_r[:, slot, k, :], start, False)
                mm(o, ll, w, False, False)
                mm(o, lh, w, False, stop, inc)

            def group_tile(n, ch, first, last, lhs, width, rows=P, i=None, cper=0, nper=0):
                bank_wait(n, i, nper)
                for k in range(KD):
                    if first and k % CW == 0:
                        chunk_wait(ch + k // CW, i, cper)
                    inc = None
                    if k == KD - 1:
                        inc = acc_full
                    elif last and k == CW - 1:
                        inc = read[ch % SLOTS]
                    mm(acc[n % 4][0:rows, 0:width], lhs(k), ring[:, (ch + k // CW) % SLOTS, k % CW, 0:width],
                       k == 0, k == KD - 1, inc)
                if last:
                    owed.append(read[(ch + 1) % SLOTS])

            def modulation():
                pe.wait_ge(consts, FIRST_CONSTS)
                pe.wait_ge(sc_done, 1)

                def rows_of(g, i=None):
                    group_tile(c.acc + g, c.chunk + 2 * g, True, True, lambda k: scT[:, k, :], N, 2, i, 2, 1)

                def turn(g, i=None):
                    pe.wait_ge(evac[g % 4], up(g // 4 + 1, i, 1))
                    if g >= 2:
                        pe.wait_ge(tr_out, up(g - 1, i, 4))
                    for j in range(4):
                        m = pe.matmul(trb[g % 2][:, 2 * j:2 * j + 2], modrow[:, g % 2, j * P:(j + 1) * P],
                                      ident[0:2, 0:2], start=True, stop=True)
                        if j == 0 and owed:
                            m.then_inc(owed.pop(), 1)
                    m.then_inc(tr_full, 1)

                rows_of(0)
                for g in range(1, 4):
                    rows_of(g)
                    turn(g - 1)
                with pe.Fori(0, 2) as i:
                    for g in range(4, 8):
                        rows_of(g, i)
                        turn(g - 1, i)
                turn(11)
                c.acc += 12
                c.chunk += 24
                c.tr += 12

                def spread(g):
                    n = c.acc + g
                    pe.wait_ge(evac[n % 4], n // 4 + 1)
                    for r in range(2 if g < 2 else 1):
                        if c.bc >= 2:
                            pe.wait_ge(bc_out, c.bc - 1)
                        mm(misc[c.bc % 2][:, :], pick[:, r, :], modrow[:, g % 2, :], True, True, bc_full)
                        c.bc += 1

                rows_of(0)
                for g in range(1, 6):
                    rows_of(g)
                    spread(g - 1)
                spread(5)
                c.acc += 6
                c.chunk += 12

            def norm(tiles, for_ffn=False):
                for t_ in tiles:
                    pe.wait_ge(xn_done, c.xn + 1)
                    for h in range(2):
                        pe.wait_ge(tr_out, c.tr - 1) if c.tr >= 2 else None
                        for j in range(4):
                            m = pe.transpose(trb[c.tr % 2][:, j * P:(j + 1) * P],
                                             xn[:, c.xn % 2, (4 * h + j) * P:(4 * h + j + 1) * P], ident[:, :])
                        m.then_inc(tr_full, 1)
                        c.tr += 1
                    c.xn += 1
                pe.wait_ge(tr_out, c.tr - 2 if for_ffn else c.tr)

            def ffn(nt):
                block_chunk.append(c.chunk)

                def flip(n, tr, i=None, nper=0, tper=0):
                    pe.wait_ge(evac[n % 4], up(n // 4 + 1, i, nper))
                    pe.wait_ge(tr_out, up(tr - 1, i, tper))
                    for j in range(2):
                        m = pe.transpose(trb[tr % 2][:, j * P:(j + 1) * P], gtok[:, tr % 2, j * P:(j + 1) * P],
                                         ident[:, :])
                        if j == 0 and owed:
                            m.then_inc(owed.pop(), 1)
                    m.then_inc(tr_full, 1)

                def group(g, i=None):
                    for t_ in range(nt):
                        q = g * nt + t_
                        n, ch = c.acc + q, c.chunk + 2 * g
                        if q == nt - 1:
                            pe.wait_ge(tr_out, c.tr)
                        bank_wait(n, i, nt // 2)
                        for k in range(KD):
                            if t_ == 0 and k % CW == 0:
                                low_wait(2 * g + k // CW, i)
                            last = t_ == nt - 1
                            inc = acc_full if k == KD - 1 else read[ch % SLOTS] if last and k == CW - 1 else None
                            mm3(acc[n % 4][:, :], xT_r[:, k, t_ * P:(t_ + 1) * P], x_low(nt, k, t_, True),
                                (ch + k // CW) % SLOTS, k % CW, k == 0, k == KD - 1, inc)
                        if last:
                            owed.append(read[(ch + 1) % SLOTS])
                        if q:
                            flip(c.acc + q - 1, c.tr + q - 1, i, nt // 2, 2 * nt)

                group(0)
                with pe.Fori(0, (UG - 1) // 2) as i:
                    group(1, i)
                    group(2, i)
                c.acc += UG * nt
                c.chunk += 2 * UG
                c.tr += UG * nt
                pe.wait_ge(tr_out, c.tr - nt)
                last = c.acc - 1
                down(nt, FT, gT, split=nt == 2, between=lambda: flip(last, c.tr - 1))
                for odd in range(2):
                    c.low[odd] += lows(nt, odd)

            def down(nt, kt, src, split=False, between=None):
                for n in range(2):
                    for k in range(kt):
                        q = n * kt + k
                        ch = c.chunk + q // CW
                        if between and q == CW:
                            between()
                        if between and q == kt - 2:
                            pe.wait_ge(tr_out, c.tr)
                        if q % CW == 0:
                            if split:
                                low_wait(2 * UG + q // CW)
                            else:
                                chunk_wait(ch)
                        for t_ in range(nt):
                            if k == 0:
                                bank_wait(c.acc + t_)
                            inc = None
                            if k == kt - 1:
                                inc = acc_full
                            elif q % CW == CW - 1 and t_ == nt - 1:
                                inc = read[ch % SLOTS]
                            if split:
                                mm3(acc[(c.acc + t_) % 4][:, :], gT_r[:, k, t_ * P:(t_ + 1) * P],
                                    gT_r[:, k, S + t_ * P:S + (t_ + 1) * P], ch % SLOTS, q % CW, k == 0,
                                    k == kt - 1, inc)
                            else:
                                mm(acc[(c.acc + t_) % 4][:, :], src[:, k, t_ * P:(t_ + 1) * P],
                                   ring[:, ch % SLOTS, q % CW, :], k == 0, k == kt - 1, inc)
                            if k == kt - 1 and q % CW == CW - 1 and t_ == nt - 1:
                                owed.append(read[ch % SLOTS])
                    c.acc += nt
                c.chunk += 2 * kt // CW

            def settled():
                for n in range(c.acc - 4, c.acc):
                    pe.wait_ge(evac[n % 4], n // 4 + 1)

            def dense_tokens(groups, tiles, src, width=N):
                for g in range(groups):
                    for n, t_ in enumerate(tiles):
                        group_tile(c.acc, c.chunk, n == 0, n == len(tiles) - 1,
                                   lambda k: src[:, k, t_ * P:(t_ + 1) * P], width)
                        c.acc += 1
                    c.chunk += 2

            def token_tile(tiles, n):
                t_, last = tiles[n], n == len(tiles) - 1
                group_tile(c.acc, c.chunk, n == 0, last, lambda k: xT[:, k, t_ * P:(t_ + 1) * P], N)
                c.acc += 1
                if last:
                    c.chunk += 2

            def dense_features(lo, hi, jobs=(0, 1, 2, 3), rows=P):
                for m, j in enumerate(jobs):
                    bank_wait(c.acc)
                    last = m == len(jobs) - 1
                    for k in range(KD):
                        if m == 0 and k % CW == 0:
                            chunk_wait(c.chunk + k // CW)
                        inc = acc_full if k == KD - 1 else read[c.chunk % SLOTS] if last and k == CW - 1 else None
                        mm(acc[c.acc % 4][0:rows, 0:hi - lo],
                           ring[:, (c.chunk + k // CW) % SLOTS, k % CW, j * P:j * P + rows], xT[:, k, lo:hi],
                           k == 0, k == KD - 1, inc)
                    c.acc += 1
                owed.append(read[(c.chunk + 1) % SLOTS])
                c.chunk += 2

            def flips(src, tiles, kt):
                for t_ in tiles:
                    for u in range(kt // 4):
                        pe.wait_ge(tr_out, c.tr - 1)
                        for j in range(4):
                            m = pe.transpose(trb[c.tr % 2][:, j * P:(j + 1) * P],
                                             src[:, t_, (4 * u + j) * P:(4 * u + j + 1) * P], ident[:, :])
                        m.then_inc(tr_full, 1)
                        c.tr += 1
                pe.wait_ge(tr_out, c.tr)

            def mlstm():
                dense_features(0, S)
                dense_features(0, 2 * S)
                dense_tokens(2, range(4), xT)
                bank_wait(c.acc)
                for k in range(KD):
                    mm(acc[c.acc % 4][:, :], wg[:, k, :], xT[:, k, :], k == 0, k == KD - 1,
                       acc_full if k == KD - 1 else None)
                c.acc += 1
                dense_tokens(2, range(2), xT)
                dense_tokens(2, range(2), xT)
                settled()
                pe.wait_ge(rows_c, 2)
                for n in range(4):
                    pe.matmul(misc[0][:, n * 40:(n + 1) * 40], gr[:, n * P:(n + 1) * P], ident[0:40, 0:40],
                              start=True, stop=True)
                pe.wait_ge(em_done, 1)
                for n in range(2):
                    m = pe.matmul(misc[0][:, (4 + n) * 40:(5 + n) * 40], lfr[:, n * P:(n + 1) * P],
                                  ident[0:40, 0:40], start=True, stop=True)
                m.then_inc(cols_full, 1)
                pe.wait_ge(cols_out, 1)

                def scores(h):
                    a, lo = 2 * (h % 2), 64 * (h % 2)
                    if h >= 2:
                        pe.wait_ge(p_done, 2 * (h - 1))
                    for n in range(4):
                        pe.matmul(acc[a + n // 2][:, (n % 2) * S:(n % 2 + 1) * S],
                                  km[lo:lo + 64, h // 2, n * P:(n + 1) * P], qm[lo:lo + 64, h // 2, :],
                                  start=True, stop=True)
                    for d in range(2):
                        m = pe.matmul(trb[h % 2][:, d * S:(d + 1) * S],
                                      ident[0:40, 32 * d + h:32 * d + h + 1].to_broadcast([40, P]), zr[:, 0:S],
                                      start=True, stop=True)
                    m.then_inc(s_full, 1)

                def values(h):
                    if h >= 1:
                        pe.wait_ge(h_done, h)
                    for d in range(2):
                        pe.wait_ge(pm_done, 2 * h + d + 1)
                        for tt in range(2):
                            keys = [n for n in range(4) if n >= 2 or (n <= tt if d == 0 else n >= tt)]
                            for n in keys:
                                m = pe.matmul(misc[d][:, tt * 129:(tt + 1) * 129],
                                              Pm[:, 2 * (h % 2) + d, n, tt * P:(tt + 1) * P], va[:, n, h, :],
                                              start=n == keys[0], stop=n == keys[-1])
                    m.then_inc(pv_full, 1)

                for h in range(H + 1):
                    if h < H:
                        scores(h)
                    if h >= 1:
                        values(h - 1)

            def branch_out(src):
                c.hn += 1
                pe.wait_ge(hn_out, c.hn)
                flips(src, range(2), KD)
                dense_tokens(2, range(2), hT)

            def mix_out():
                c.y += 4
                pe.wait_ge(y_done, c.y)
                flips(y, range(2), KD)
                dense_tokens(2, range(2), hT)

            def pairs(l):
                return (trb, misc)[l % 2]

            def levels(d, between=None):
                for l, B in enumerate(LEVELS):
                    c.g += 1
                    pe.wait_ge(lv_g, c.g)
                    for hh in range(4):
                        if B == P:
                            k_, q_ = (0, 1) if d == 0 else (1, 0)
                            m = pe.matmul(pairs(l)[0][:, hh * P:(hh + 1) * P], G[:, l % 2, hh, k_ * P:(k_ + 1) * P],
                                          G[:, l % 2, hh, q_ * P:(q_ + 1) * P], start=True, stop=True)
                        else:
                            for st in range(2):
                                v = G[:, l % 2, hh, st * P:(st + 1) * P]
                                m = pe.matmul(pairs(l)[st][:, hh * P:(hh + 1) * P], v, v, start=True, stop=True)
                    m.then_inc(lv_a, 1)
                    if between:
                        between(l)
                c.p += 8

            def context_products():
                c.g += 1
                pe.wait_ge(lv_g, c.g)
                for hh in range(4):
                    bank_wait(c.acc)
                    for st in range(2):
                        m = pe.matmul(acc[c.acc % 4][:, st * S:(st + 1) * S], G[:, 0, hh, st * P:(st + 1) * P],
                                      G[:, 1, hh, :], start=True, stop=True)
                    m.then_inc(acc_full, 1)
                    c.acc += 1

            def diagonal():
                pe.wait_ge(lv_p, c.p - 1)
                for hh in range(4):
                    for st in range(2):
                        m = pe.matmul(trb[st][:, hh * P:(hh + 1) * P], kd[:, hh, st * P:(st + 1) * P],
                                      qh[:, hh, st * P:(st + 1) * P], start=True, stop=True)
                m.then_inc(lv_a, 1)

            def hgrn():
                dense_tokens(2, range(2), xT)
                pe.wait_ge(permuted, 1)

                def values(l):
                    if l % 2 == 0:
                        token_tile(range(4), l // 2)

                for hg in range(2):
                    dense_features(0, S)
                    for d in range(2):
                        dense_features(0, 2 * S)
                        levels(d, None if hg else values)
                        context_products()
                    diagonal()
                    c.at += 1
                    pe.wait_ge(attn_done, c.at)
                    for tt in range(2):
                        bank_wait(c.acc)
                        for hh in range(4):
                            for n in range(4):
                                src = (Pl if n < 2 else Pc)[:, hh, n % 2, tt * P:(tt + 1) * P]
                                h = 4 * hg + hh
                                mm(acc[c.acc % 4][:, hh * P:(hh + 1) * P], src, vi[:, n, h * P:(h + 1) * P],
                                   n == 0, n == 3, acc_full if n == 3 and hh == 3 else None)
                        c.acc += 1
                dense_tokens(2, range(2), xT)

            def bias_toeplitz():
                pe.wait_ge(bias_dma, 32)
                for h in range(H):
                    if h >= 2:
                        pe.wait_ge(bias_out, h - 1)
                    pe.matmul(misc[h % 2][:, 0:RW], table[:, h:h + 1].to_broadcast([33, P]), onehot,
                              start=True, stop=True).then_inc(bias_rows, 1)

            def compress():
                for x in range(2):
                    bank_wait(c.acc)
                    for ht in range(2):
                        for l in range(16):
                            ch = c.chunk + l // 8
                            if ht == 0 and l % 8 == 0:
                                chunk_wait(ch)
                            inc = None
                            if ht == 1 and l == 15:
                                inc = acc_full
                            elif ht == 1 and l == 7:
                                inc = read[ch % SLOTS]
                            mm(acc[c.acc % 4][:, ht * 32:ht * 32 + 30],
                               ring[:, ch % SLOTS, l // 2 % CW, (l % 2) * S + ht * P:(l % 2) * S + (ht + 1) * P],
                               KK[:, x, :, l * 15:(l + 1) * 15], l == 0, l == 15, inc)
                    owed.append(read[(c.chunk + 1) % SLOTS])
                    c.acc += 1
                    c.chunk += 2
                settled()
                bank_wait(c.acc)
                b = acc[c.acc % 4]
                for g in range(2):
                    for ht in range(2):
                        mm(b[64 * g:64 * g + 64, 0:15], w2c[:, 0, ht, :], hid[:, 0, ht, 15 * g:15 * g + 15],
                           ht == 0, ht == 1)
                for g in range(2):
                    for ht in range(2):
                        mm(b[0:15, 64 + 64 * g:128 + 64 * g], hid[:, 1, ht, 15 * g:15 * g + 15], w2c[:, 1, ht, :],
                           ht == 0, ht == 1, acc_full if g and ht else None)
                c.acc += 1

            def attention():
                def scores(h):
                    g, j = divmod(h, 4)
                    a, f = 2 * (h % 2), slice(64 * g, 64 * g + 64)
                    if h >= 2:
                        pe.wait_ge(ns_m, c.ns + h - 1)
                    for kind in range(2):
                        b = acc[a + kind]
                        pe.matmul(b[:, 0:P], qa[f, j, 0:P], kk[f, kind, 0:P], start=True, stop=True)
                        pe.matmul(b[:, P:P + S], qa[f, j, P:S], kk[f, kind, :], start=True, stop=True)
                    pe.matmul(acc[a][:, 384:391], qa[f, j, 0:P], kcT[f, 0:7], start=True, stop=True)
                    pe.matmul(acc[a][:, 400:415], qa[f, j, P:S], kcT[f, 0:15], start=True,
                              stop=True).then_inc(ns_s, 1)

                def turn(h):
                    pe.wait_ge(ns_w, c.ns + h + 1)
                    if c.ns + h:
                        pe.wait_ge(ns_pa, c.ns + h)
                        pe.wait_ge(ns_pb, c.ns + h)
                    L = Lb[:, h % 2, :]
                    for kind in range(2):
                        for u in range(3):
                            o = kind * 384 + u * P
                            pe.transpose(trb[kind][:, u * P:(u + 1) * P], L[:, o:o + P], ident[:, :])
                    for tt in range(2):
                        m = pe.transpose(trb[tt][0:15, 384:N], L[:, 768 + 16 * tt:783 + 16 * tt], ident[:, :])
                    m.then_inc(ns_t, 1)

                def values(h):
                    g = h // 4
                    if h >= 2:
                        pe.wait_ge(ns_h, c.ns + h - 1)
                    pe.wait_ge(ns_pa, c.ns + h + 1)
                    pe.wait_ge(ns_pb, c.ns + h + 1)
                    f = slice(64 * g, 64 * g + 64)
                    b, T = misc[h % 2], PT[:, h % 2, :]
                    for kind in range(2):
                        pe.matmul(b[f, 0:S], vsw[:, 0, kind * P + 64 * g:kind * P + 64 * g + 64],
                                  T[:, kind * 384:kind * 384 + S], start=kind == 0, stop=False)
                    pe.matmul(b[f, 0:S], vcmp[:, g, :], T[0:15, 768:1024], start=False, stop=False)
                    for kind in range(2):
                        m = pe.matmul(b[f, P:S], vsw[:, 1, kind * P + 64 * g:kind * P + 64 * g + 64],
                                      T[:, kind * 384 + S:kind * 384 + 384], start=False, stop=kind == 1)
                    m.then_inc(ns_o, 1)

                for h in range(H + 2):
                    if h < H:
                        scores(h)
                    if h >= 2:
                        values(h - 2)
                    if 1 <= h <= H:
                        turn(h - 1)
                c.ns += H
                pe.wait_ge(ns_h, c.ns)

            def layer():
                norm(range(2), for_ffn=True)
                ffn(2)
                norm(range(2))
                if not c.layer:
                    bias_toeplitz()
                dense_features(0, S)
                dense_features(0, S)
                bank_wait(c.acc)
                for k in range(KD):
                    if k % CW == 0:
                        chunk_wait(c.chunk + k // CW)
                    mm(acc[c.acc % 4][0:16, 0:S], ring[:, (c.chunk + k // CW) % SLOTS, k % CW, 280:296],
                       xT[:, k, 0:S], k == 0, k == KD - 1, acc_full if k == KD - 1 else None)
                c.acc += 1
                dense_tokens(1, range(2), xT, 280)
                settled()
                c.layer += 1
                pe.wait_ge(layer_in, LAYER * c.layer)
                compress()
                dense_tokens(2, range(2), xT)
                settled()
                attention()
                down(2, 4, oaT)
                dense_features(0, S)
                dense_features(0, S)
                for j in range(4):
                    bank_wait(c.acc)
                    mm(acc[c.acc % 4][:, 0:S], wa2[:, j * P:(j + 1) * P], alr, True, True, acc_full)
                    c.acc += 1
                levels(0, lambda l: token_tile(range(2), l % 2))
                diagonal()
                c.at += 1
                pe.wait_ge(attn_done, c.at)
                settled()
                for tt in range(2):
                    for pair in range(2):
                        bank_wait(c.acc)
                        for hh in range(2):
                            for n in range(tt + 1):
                                h = 2 * pair + hh
                                mm(acc[c.acc % 4][:, hh * S:(hh + 1) * S], Pl[:, h, n, tt * P:(tt + 1) * P],
                                   vb[:, n, h * S:(h + 1) * S], n == 0, n == tt,
                                   acc_full if n == tt and hh == 1 else None)
                        c.acc += 1
                dense_tokens(2, range(2), xT)
                branch_out(Hx)
                mix_out2()
                norm(range(2), for_ffn=True)
                ffn(2)

            def mix_out2():
                c.y += 4
                pe.wait_ge(y_done, c.y)
                flips(y2, range(2), KD)
                dense_tokens(2, range(2), hT)

            modulation()
            norm(range(4), for_ffn=True)
            ffn(4)
            norm(range(4))
            mlstm()
            branch_out(Hm)
            hgrn()
            branch_out(Hx)
            mix_out()
            norm(range(2), for_ffn=True)
            ffn(2)
            layer()
            layer()

        @block.scalar
        def _(act):
            c = Count()

            def step(ins):
                c.seq += 1
                ins.then_inc(act_seq, 1)
                act.wait_ge(act_seq, c.seq)

            act.dma_start(cT[:, :, :], t["cT"]).then_inc(consts, 16)
            act.dma_start(ident[:, :], t["ident"]).then_inc(consts, 16)
            act.dma_start(pick[:, :, :], t["pick"]).then_inc(consts, 16)
            act.dma_start(adab, t["adab"]).then_inc(consts, 16)
            act.dma_start(gains[:, :, :], t["gains"]).then_inc(more_consts, 16)
            act.dma_start(bF[:, :], t["bF"]).then_inc(more_consts, 16)
            act.dma_start(wg, t["wg"]).then_inc(more_consts, 16)
            act.dma_start(lbl[:, :, :, :], t["lbl"]).then_inc(more_consts, 16)
            act.dma_start(gains2[:, :, :], t["gains2"]).then_inc(more_consts, 16)
            act.dma_start(X[:, 0:2, :], t["x"]).then_inc(more_consts, 16)
            act.dma_start(X[:, 2:4, :], t["ctx"]).then_inc(more_consts, 16)

            def modulation():
                act.wait_ge(consts, FIRST_CONSTS)
                act.activation(scT[:, :, :], cT[:, :, :], ACT.Silu).then_inc(sc_done, 1)
                c.acc += 12
                for g in range(6):
                    for r in range(2 if g < 2 else 1):
                        act.wait_ge(bc_full, c.bc + 1)
                        slot = 3 if r else g // 2
                        act.activation(gateB[:, slot, (g % 2) * N:(g % 2 + 1) * N], misc[c.bc % 2][:, :], ACT.Copy,
                                       scale=1.0 if slot == 1 else 0.5).then_inc(bc_out, 1)
                        c.bc += 1
                c.acc += 6

            def norm(tiles):
                if c.resid:
                    act.wait_ge(resid, c.resid)
                if c.layer:
                    settled()
                for n, t_ in enumerate(tiles):
                    if n:
                        act.wait_ge(act_seq, c.seq)
                    ins = act.activation(junk, X[:, t_, :], ACT.Square, accum_out=ss[:, n:n + 1])
                    if n < len(tiles) - 1:
                        c.seq += 1
                        ins.then_inc(act_seq, 1)
                ins.then_inc(squares, 1)
                c.norm += 1
                act.wait_ge(var_done, c.norm)
                act.activation(sd[:, 0:len(tiles)], var[:, 0:len(tiles)], ACT.Sqrt).then_inc(sd_done, 1)

            def ffn(nt):
                def gate(q, i=None):
                    n = c.acc + q
                    act.wait_ge(acc_full, up(n + 1, i, 2 * nt))
                    if q >= 2:
                        act.wait_ge(evac[(n - 2) % 4], up((n - 2) // 4 + 1, i, nt // 2))
                    act.activation(sil[:, n % 2, :], acc[n % 4][:, 0:256], ACT.Silu).then_inc(sil_done, 1)

                first = block_chunk[c.block]

                def split(j, i=None):
                    ch = first + j
                    act.wait_ge(loaded[ch % SLOTS], up(16 * (ch // SLOTS + 1), i, 16))
                    act.activation(high[:, ch % SLOTS, :],
                                   ring[:, ch % SLOTS].rearrange("p a b -> p (a b)"), ACT.Copy).then_inc(high_ready, 1)

                def group(g, i=None, ahead=2):
                    for t_ in range(nt):
                        if t_ < ahead:
                            split(2 * g + 2 + t_, i)
                        gate(g * nt + t_, i)

                for j in range(4):
                    split(j)
                group(0, ahead=0)
                with act.Fori(0, (UG - 3) // 2) as i:
                    group(1, i)
                    group(2, i)
                group(UG - 2)
                group(UG - 1, ahead=0 if nt == 4 else 2)
                for j in range(2 * UG + 2, chunks_split(nt)):
                    split(j)
                c.high += chunks_split(nt)
                c.block += 1
                c.acc += UG * nt + 2 * nt

            def mlstm():
                act.wait_ge(tr_out, 12 + 8 + 4 * UG + 8)
                act.dma_start(biasB, t["bT"][0:1, 0:3 * D].to_broadcast([P, 3 * D])).then_inc(bias_in, 16)
                act.dma_start(gainB, t["mgain"].to_broadcast([P, D])).then_inc(bias_in, 16)
                c.acc += 4
                for j in range(4):
                    act.wait_ge(acc_full, c.acc + 1)
                    act.activation(km[:, j, :], acc[c.acc % 4][:, :], ACT.Identity,
                                   bias=bF[:, 4 + j:5 + j]).then_inc(evac[c.acc % 4], 1)
                    c.acc += 1
                c.acc += 8 + 1 + 4 + 4
                act.wait_ge(rows_a, 1)
                step(act.activation(br, br, ACT.Exp, scale=-1.0))
                act.activation(br, br, ACT.Ln, bias=1.0).then_inc(rows_b, 1)
                act.wait_ge(rows_c, 2)
                act.activation(lfr[:, 0:S], lfr[:, 0:S], ACT.Exp, scale=-1.0).then_inc(em_done, 1)
                act.wait_ge(cols_out, 1)
                for h in range(H):
                    act.wait_ge(s_full, h + 1)
                    if h >= 2:
                        act.wait_ge(pv_full, h - 1)
                    for d in range(2):
                        for n in range(4):
                            lo = P if (n == 1 and d == 0) else 0
                            hi = P if (n == 0 and d == 1) else S
                            ins = act.activation(Pm[:, 2 * (h % 2) + d, n, lo:hi],
                                                 trb[h % 2][:, d * S + lo:d * S + hi], ACT.Exp,
                                                 bias=gcol[:, n, 32 * d + h:32 * d + h + 1])
                        ins.then_inc(d_done, 1)
                act.wait_ge(h_done, H)
                head_norm(ACT.Sigmoid, Hm, om)
                act.activation(gmx, gmx, ACT.Sigmoid).then_inc(merge_gate, 1)
                c.acc += 4
                c.tr += 4
                settled()

            def lower_bounds():
                act.wait_ge(lb_step, 1)
                act.activation(lbl[:, :, :, :], lbl[:, :, :, :], ACT.Exp).then_inc(lb_step, 1)

            def levels(d, between=None):
                for l, B in enumerate(LEVELS):
                    c.d += 1
                    act.wait_ge(lv_d, c.d)
                    v = E[:, l % 2, :, :].rearrange("p h (n a b) -> p (h n) a b", a=2, b=B)
                    act.activation(v[:, :, 1, :], v[:, :, 1, :], ACT.Exp)
                    act.activation(v[:, :, 0, :], v[:, :, 0, :], ACT.Exp, scale=-1.0).then_inc(lv_e, 1)
                    if between and l:
                        between(l - 1)
                if between:
                    between(7)

            def hgrn():
                act.dma_start(biasB, t["bT"][0:1, 3 * D:6 * D].to_broadcast([P, 3 * D])).then_inc(bias_in, 16)
                act.dma_start(gainB, t["hgain"].to_broadcast([P, D])).then_inc(bias_in, 16)
                act.dma_start(gateB[:, 3, 0:7 * P], t["masks"][0]).then_inc(masks_in, 16)
                act.dma_start(tmp[:, :, :].rearrange("p a b -> p (a b)")[:, 0:7 * P],
                              t["masks"][1]).then_inc(masks_in, 16)
                c.acc += 4
                for hg in range(2):
                    if hg:
                        act.wait_ge(attn_done, hg)
                    for j in range(4):
                        act.wait_ge(acc_full, c.acc + 1)
                        act.activation(qh[:, j, :], acc[c.acc % 4][:, 0:S], ACT.Silu,
                                       bias=bF[:, 8 + 4 * hg + j:9 + 4 * hg + j]).then_inc(evac[c.acc % 4], 1)
                        c.acc += 1
                    for d in range(2):
                        if d:
                            settled()
                        for j in range(4):
                            act.wait_ge(acc_full, c.acc + 1)
                            col = 16 + 8 * d + 4 * hg + j
                            act.activation(kh[:, j, :], acc[c.acc % 4][:, :], ACT.Sigmoid, scale=-1.0,
                                           bias=nbF[:, col:col + 1])
                            act.activation(lf[:, j, :], acc[c.acc % 4][:, :], ACT.Sigmoid,
                                           bias=bF[:, col:col + 1]).then_inc(evac[c.acc % 4], 1)
                            c.acc += 1
                        settled()
                        for j in range(4):
                            h = 4 * hg + j
                            ins = act.activation(lf[:, j, :], lf[:, j, :], ACT.Ln, scale=omlb[:, d, h:h + 1],
                                                 bias=lb[:, d, h:h + 1])
                        ins.then_inc(lf_done, 1)
                        levels(d)
                        if hg == 0:
                            c.acc += 4
                        c.g += 8
                        act.wait_ge(lv_g, c.g)
                        for j in range(4):
                            if d == 0:
                                act.activation(E[:, 0, j, :], cum[:, j, 1, 1:], ACT.Exp, scale=-1.0,
                                               bias=cum[:, j, 1, S:S + 1])
                            else:
                                act.activation(E[:, 1, j, :], cum[:, j, 0, 0:S], ACT.Exp, scale=-1.0,
                                               bias=cum[:, j, 0, S:S + 1])
                        if d == 0:
                            ins = act.activation(E[:, 1, :, :], cum[:, :, 0, 1:], ACT.Exp)
                        else:
                            ins = act.activation(E[:, 0, :, :], cum[:, :, 1, 0:S], ACT.Exp)
                        ins.then_inc(lv_e, 1)
                        c.g += 1
                        c.acc += 4
                    c.acc += 2
                for n in (c.acc - 2, c.acc - 1):
                    act.wait_ge(evac[n % 4], n // 4 + 1)
                c.acc += 4
                head_norm(ACT.Silu, Hx, gx)
                act.activation(ghx, ghx, ACT.Sigmoid).then_inc(merge_gate, 1)
                c.acc += 4 + 4
                c.resid += 4

            def settled():
                for n in range(c.acc - 4, c.acc):
                    act.wait_ge(evac[n % 4], n // 4 + 1)

            def head_norm(func, src, gate, heads=H):
                c.hn += 1
                act.activation(Pm[:, 0:2, :, :].rearrange("p a b c -> p (a b c)"),
                               src.rearrange("p a b -> p (a b)"), ACT.Square).then_inc(hn_sq, 1)
                act.wait_ge(hn_var, c.hn)
                act.activation(ssq[:, 0:2 * heads], ssq[:, 0:2 * heads], ACT.Sqrt).then_inc(hn_sd, 1)
                settled()
                act.activation(gate, gate, func).then_inc(hn_gate, 1)

            def attention():
                def exps(h):
                    act.wait_ge(ns_m, c.ns + h + 1)
                    L = Lb[:, h % 2, :]
                    for i, (lo, hi) in enumerate(SEGMENTS):
                        ins = act.activation(L[:, lo:hi], L[:, lo:hi], ACT.Exp, bias=mx[:, h % 2, i:i + 1],
                                             accum_out=sm[:, h % 2, i:i + 1])
                    ins.then_inc(ns_e, 1)

                def turned(h):
                    act.wait_ge(ns_t, c.ns + h + 1)
                    if h >= 2:
                        act.wait_ge(ns_o, c.ns + h - 1)
                    act.activation(PT[:, h % 2, 0:384], trb[0][:, 0:384], ACT.Copy)
                    act.activation(PT[0:15, h % 2, 768:896], trb[0][0:15, 384:N], ACT.Copy).then_inc(ns_pa, 1)

                def output(h):
                    act.wait_ge(ns_o, c.ns + h + 1)
                    g, j = divmod(h, 4)
                    f = slice(64 * g, 64 * g + 64)
                    act.activation(oaT[f, j, :], misc[h % 2][f, 0:S], ACT.Copy).then_inc(ns_h, 1)

                for h in range(H + 3):
                    if h < H:
                        exps(h)
                    if 2 <= h < H + 2:
                        turned(h - 2)
                    if h >= 3:
                        output(h - 3)
                c.ns += H

            def layer(l):
                norm(range(2))
                c.layer += 1
                ffn(2)
                norm(range(2))
                act.wait_ge(squares, c.norm)
                act.dma_start(pos, t["pos"][l]).then_inc(layer_in, 16)
                act.dma_start(w2c, t["w2c"][l]).then_inc(layer_in, 16)
                act.dma_start(wa2, t["wa2"][l]).then_inc(layer_in, 16)
                act.dma_start(ab, t["ab"][l]).then_inc(layer_in, 16)
                act.dma_start(gainC, t["ggain"][l:l + 1].to_broadcast([P, D])).then_inc(layer_in, 16)
                c.acc += 4 + 4 + 1 + 2
                settled()
                for x in range(2):
                    act.wait_ge(acc_full, c.acc + 1)
                    act.activation(hid[:, x, :, 0:30],
                                   acc[c.acc % 4][:, 0:64].rearrange("p (a b) -> p a b", b=32)[:, :, 0:30],
                                   ACT.Silu).then_inc(evac[c.acc % 4], 1)
                    c.acc += 1
                act.activation(ga, ga, ACT.Sigmoid).then_inc(ga_done, 1)
                c.acc += 1
                for g in range(2):
                    for t_ in range(2):
                        act.wait_ge(acc_full, c.acc + 1)
                        act.activation(gm2[:, t_, g * N:(g + 1) * N], acc[c.acc % 4][:, :],
                                       ACT.Sigmoid).then_inc(evac[c.acc % 4], 1)
                        c.acc += 1
                attention()
                c.acc += 4
                c.acc += 4
                for j in range(4):
                    act.wait_ge(acc_full, c.acc + 1)
                    act.activation(kh[:, j, 0:S], acc[c.acc % 4][:, 0:S], ACT.Copy).then_inc(evac[c.acc % 4], 1)
                    c.acc += 1
                c.acc += 4
                act.wait_ge(gl_a, 2 * l + 1)
                step(act.activation(G[:, 0, :, :], G[:, 0, :, :], ACT.Exp, scale=-1.0))
                act.activation(G[:, 0, :, :], G[:, 0, :, :], ACT.Ln, bias=1.0).then_inc(gl_l, 1)

                def take(dst, n, func=ACT.Copy):
                    act.wait_ge(acc_full, c.acc + 1)
                    g, t_ = divmod(n, 2)
                    act.activation(dst[:, t_, g * N:(g + 1) * N], acc[c.acc % 4][:, :],
                                   func).then_inc(evac[c.acc % 4], 1)
                    c.acc += 1

                levels(0, lambda n: take(vb if n < 4 else rx, n % 4))
                c.g += 8
                c.acc += 4
                settled()
                head_norm(ACT.Silu, Hx, rx, 4)
                for n in range(4):
                    take(gm2[:, :, D:2 * D], n, ACT.Sigmoid)
                c.acc += 4 + 4
                c.tr += 8
                norm(range(2))
                ffn(2)

            modulation()
            act.wait_ge(more_consts, MORE_CONSTS)
            lower_bounds()
            norm(range(4))
            ffn(4)
            c.resid += 8
            norm(range(4))
            mlstm()
            hgrn()
            norm(range(2))
            ffn(2)
            c.resid += 4
            norm(range(2))
            c.resid += 2
            layer(0)
            layer(1)
            norm(range(2))

        @block.vector
        def _(dve):
            c = Count()

            def step(ins):
                c.seq += 1
                ins.then_inc(dve_seq, 1)
                dve.wait_ge(dve_seq, c.seq)

            def modulation():
                dve.wait_ge(consts, FIRST_CONSTS)

                def row(g, i=None):
                    n = c.acc + g
                    dve.wait_ge(acc_full, up(n + 1, i, 4))
                    a = adab[:, n * N:(n + 1) * N] if i is None else adab[:, bass.ds(i * (4 * N) + n * N, N)]
                    dve.tensor_tensor(out=modrow[:, n % 2, :], in0=acc[n % 4][0:2, :], in1=a,
                                      op=ALU.add).then_inc(evac[n % 4], 1)

                def collect(g, i=None):
                    dve.wait_ge(tr_full, up(g + 1, i, 4))
                    at = slice(4 * g, 4 * g + 4) if i is None else bass.ds(i * 16 + 4 * g, 4)
                    dve.tensor_copy(modT[:, at, :],
                                    trb[g % 2][:, 0:8].rearrange("p (a b) -> p a b", b=2)).then_inc(tr_out, 1)

                row(0)
                for g in range(1, 4):
                    row(g)
                    collect(g - 1)
                with dve.Fori(0, 2) as i:
                    for g in range(4, 8):
                        row(g, i)
                        collect(g - 1, i)
                collect(11)
                c.acc += 12
                c.tr += 12
                for g in range(6):
                    if g >= 2:
                        dve.wait_ge(bc_full, 2 * (g - 1) if g <= 3 else g + 1)
                    row(g)
                c.acc += 6
                dve.wait_ge(tr_out, c.tr)
                dve.wait_ge(more_consts, MORE_CONSTS)
                for u, (s, r) in enumerate(((0, 0), (0, 1), (1, 0), (1, 1), (2, 0))):
                    dve.scalar_tensor_tensor(out=normA[:, u, :], in0=modT[:, (2 * s + 1) * 8:(2 * s + 2) * 8, r],
                                             scalar=1.0, in1=gains[:, s, :], op0=ALU.add,
                                             op1=ALU.mult).then_inc(mod_done, 1)
                dve.wait_ge(mod_done, 5)

            def norm(tiles, a_of, b_of, split=0):
                c.norm += 1
                m = len(tiles)
                dve.wait_ge(squares, c.norm)
                dve.tensor_scalar(var[:, 0:m], ss[:, 0:m], 1.0 / D, EPS, ALU.mult, ALU.add).then_inc(var_done, 1)
                dve.wait_ge(sd_done, c.norm)
                step(dve.reciprocal(rstd[:, 0:m], sd[:, 0:m]))

                def scale(n):
                    if n >= 2:
                        dve.wait_ge(tr_full, c.tr + 2 * (n - 1))
                    dve.tensor_scalar(xn[:, (c.xn + n) % 2, :], X[:, tiles[n], :], rstd[:, n:n + 1], None,
                                      ALU.mult).then_inc(xn_done, 1)

                scale(0)
                for n, t_ in enumerate(tiles):
                    if n + 1 < m:
                        scale(n + 1)
                    for h in range(2):
                        tr = c.tr + 2 * n + h
                        dve.wait_ge(tr_full, tr + 1)
                        ks = slice(4 * h, 4 * h + 4)
                        for j in range(4):
                            k = 4 * h + j
                            a, b = a_of(t_), b_of(t_)
                            ins = dve.tensor_scalar(x_low(split, k, t_) if split else xT[:, k, t_ * P:(t_ + 1) * P],
                                                    trb[tr % 2][:, j * P:(j + 1) * P],
                                                    a[:, k:k + 1], None if b is None else b[:, k:k + 1], ALU.mult,
                                                    *([] if b is None else [ALU.add]))
                        if split:
                            step(ins)
                            high_, whole = xT_r[:, ks, t_ * P:(t_ + 1) * P], x_low(split, ks, t_)
                            step(dve.tensor_copy(high_, whole))
                            ins = dve.tensor_tensor(out=x_low(split, ks, t_, True), in0=whole, in1=high_,
                                                    op=ALU.subtract)
                        ins.then_inc(tr_out, 1)
                c.tr += 2 * m
                c.xn += m

            def ffn(nt, update):
                def product(q, i=None):
                    n = c.acc + q
                    dve.wait_ge(sil_done, up(c.sil + q + 1, i, 2 * nt))
                    if q >= 2:
                        dve.wait_ge(tr_full, up(c.tr + q - 1, i, 2 * nt))
                    dve.tensor_tensor(out=gtok[:, (c.tr + q) % 2, :], in0=sil[:, n % 2, :], in1=acc[n % 4][:, 256:512],
                                      op=ALU.mult).then_inc(evac[n % 4], 1)

                def collect(q, i=None):
                    tr = c.tr + q
                    dve.wait_ge(tr_full, up(tr + 1, i, 2 * nt))
                    g, t_ = divmod(q, nt)
                    ks = slice(2 * g, 2 * g + 2) if i is None else bass.ds(i * 4 + 2 * g, 2)
                    dst = gT[:, ks, t_ * P:(t_ + 1) * P]
                    src = trb[tr % 2][:, 0:256].rearrange("p (a b) -> p a b", b=P)
                    if nt == 4:
                        dve.tensor_copy(dst, src).then_inc(tr_out, 1)
                    else:
                        dve.tensor_copy(gT_r[:, ks, t_ * P:(t_ + 1) * P], src).then_inc(step_low, 1)
                        dve.wait_ge(step_low, up(c.lowstep + q + 1, i, 2 * nt))
                        dve.tensor_tensor(out=gT_r[:, ks, S + t_ * P:S + (t_ + 1) * P], in0=src,
                                          in1=gT_r[:, ks, t_ * P:(t_ + 1) * P], op=ALU.subtract).then_inc(tr_out, 1)

                def low(j, i=None):
                    slot = (block_chunk[c.block] + j) % SLOTS
                    dve.wait_ge(high_ready, up(c.high + j + 1, i, 4))
                    w = ring[:, slot].rearrange("p a b -> p (a b)")
                    dve.tensor_tensor(out=ring_r[:, slot].rearrange("p a b -> p (a b)"), in0=w, in1=high[:, slot, :],
                                      op=ALU.subtract).then_inc(low_ready[1], 1)

                def group(g, i=None, ahead=True):
                    for t_ in range(nt):
                        q = g * nt + t_
                        product(q, i)
                        if q:
                            collect(q - 1, i)
                        if ahead and t_ == 0:
                            low(2 * g + 3, i)

                low(1)
                low(3)
                group(0, ahead=False)
                with dve.Fori(0, (UG - 3) // 2) as i:
                    group(1, i)
                    group(2, i)
                group(UG - 2)
                group(UG - 1, ahead=nt == 2)
                c.acc += UG * nt
                c.sil += UG * nt
                collect(UG * nt - 1)
                c.tr += UG * nt
                if nt == 2:
                    c.lowstep += UG * nt
                for j in range(2 * UG + 3, chunks_split(nt), 2):
                    low(j)
                c.high += chunks_split(nt)
                c.block += 1
                for n in range(2):
                    for t_ in range(nt):
                        a = c.acc
                        dve.wait_ge(acc_full, a + 1)
                        update(t_, n, a)
                        c.acc += 1

            def gated(slot_of):
                def update(t_, n, a):
                    cols = slice(n * N, (n + 1) * N)
                    dve.tensor_tensor(out=tmp[:, a % 2, :], in0=acc[a % 4][:, :], in1=gateB[:, slot_of(t_), cols],
                                      op=ALU.mult).then_inc(evac[a % 4], 1)
                    dve.wait_ge(evac[a % 4], a // 4 + 1)
                    dve.tensor_tensor(out=X[:, t_, cols], in0=X[:, t_, cols], in1=tmp[:, a % 2, :],
                                      op=ALU.add).then_inc(resid, 1)
                return update

            def evacuate(dst, fn):
                dve.wait_ge(acc_full, c.acc + 1)
                fn(dst, acc[c.acc % 4]).then_inc(evac[c.acc % 4], 1)
                c.acc += 1

            def mlstm():
                dve.wait_ge(bias_in, 32)
                dve.memset(zr, 0.0)
                dve.memset(va[:, :, :, P:P + 1], 1.0)
                for j in range(4):
                    evacuate(qm[:, j, :], lambda o, b: dve.tensor_scalar(o, b[:, 0:S], bF[:, j:j + 1],
                                                                         64 ** -0.5, ALU.add, ALU.mult))
                c.acc += 4
                for g in range(2):
                    for t_ in range(4):
                        evacuate(va[:, t_, 4 * g:4 * g + 4, 0:P], lambda o, b: dve.tensor_tensor(
                            out=o, in0=b[:, :].rearrange("p (a b) -> p a b", b=P),
                            in1=biasB[:, g * N:(g + 1) * N].rearrange("p (a b) -> p a b", b=P), op=ALU.add))
                dve.wait_ge(acc_full, c.acc + 1)
                b = acc[c.acc % 4]
                dve.tensor_scalar(igr, b[0:40, :], bF[0:40, 32:33], None, ALU.add)
                dve.tensor_scalar(zr, b[64:104, :], bF[64:104, 32:33], None,
                                  ALU.add).then_inc(evac[c.acc % 4], 1)
                dve.wait_ge(evac[c.acc % 4], c.acc // 4 + 1)
                dve.scalar_tensor_tensor(out=br, in0=zr, scalar=-1.0, in1=zr, op0=ALU.mult,
                                         op1=ALU.max).then_inc(rows_a, 1)
                c.acc += 1
                for dst, off in ((om, D), (gmx, 2 * D)):
                    for g in range(2):
                        for t_ in range(2):
                            evacuate(dst[:, t_, g * N:(g + 1) * N], lambda o, b: dve.tensor_tensor(
                                out=o, in0=b[:, :], in1=biasB[:, off + g * N:off + (g + 1) * N], op=ALU.add))
                dve.wait_ge(rows_b, 1)
                step(dve.scalar_tensor_tensor(out=lfr, in0=zr, scalar=0.0, in1=br, op0=ALU.min,
                                              op1=ALU.subtract))
                LAT, CTX = slice(0, S), slice(S, 2 * S)
                BLAT, BCTX = slice(S - 1, None, -1), slice(2 * S - 1, S - 1, -1)

                def scan(dst, src, one, op0, op1, first):
                    for lo, cx, lt, end in ((0, CTX, LAT, 2 * S - 1), (32, BCTX, BLAT, S)):
                        r = slice(lo, lo + 8)
                        x0, x1 = (src[r, cx], src[r, lt]) if one is None else (one[r, 0:S], one[r, 0:S])
                        step(dve.tensor_tensor_scan(dst[r, cx], x0, src[r, cx], first, op0, op1))
                        step(dve.tensor_tensor_scan(dst[r, lt], x1, src[r, lt], dst[r, end:end + 1], op0, op1))

                step(dve.memset(br, 0.0))
                scan(br, lfr, ones, ALU.mult, ALU.add, 0.0)
                step(dve.tensor_tensor(out=gr, in0=igr, in1=br, op=ALU.subtract))
                dve.memset(zr, 0.0).then_inc(rows_c, 1)
                dve.wait_ge(rows_c, 1)
                scan(zr, gr, None, ALU.max, ALU.max, 0.0)
                dve.tensor_tensor(out=lfr[:, 0:S], in0=br[:, 0:S], in1=zr[:, 0:S], op=ALU.add)
                dve.tensor_scalar(zr[:, 0:S], zr[:, 0:S], -1.0, None, ALU.mult).then_inc(rows_c, 1)
                dve.wait_ge(cols_full, 1)
                dve.tensor_copy(gcol[:, :, :], misc[0][:, 0:160].rearrange("p (a b) -> p a b", b=40))
                dve.tensor_copy(emc[:, :, :],
                                misc[0][:, 160:240].rearrange("p (a b) -> p a b", b=40)).then_inc(cols_out, 1)
                dve.wait_ge(cols_out, 1)

                def weights(h):
                    for d in range(2):
                        dve.wait_ge(d_done, 2 * h + d + 1)
                        a = 2 * (h % 2)
                        Q = Pm[:, a + d, :, :]
                        lat = acc[a][:, :].rearrange("p (a b) -> p a b", b=S)
                        cx = acc[a + 1][:, :].rearrange("p (a b) -> p a b", b=S)
                        lo, hi = (0, S) if d == 0 else (0, P)
                        dve.tensor_tensor(out=Q[:, 0, lo:hi], in0=lat[:, 0, lo:hi], in1=Q[:, 0, lo:hi], op=ALU.mult)
                        lo, hi = (P, S) if d == 0 else (0, S)
                        dve.tensor_tensor(out=Q[:, 1, lo:hi], in0=lat[:, 1, lo:hi], in1=Q[:, 1, lo:hi], op=ALU.mult)
                        dve.tensor_tensor(out=Q[:, 2:4, :], in0=cx, in1=Q[:, 2:4, :], op=ALU.mult).then_inc(p_done, 1)

                def outputs(h):
                    dve.wait_ge(pv_full, h + 1)
                    for d in range(2):
                        o = misc[d][:, 0:258].rearrange("p (a b) -> p a b", b=129)
                        ins = dve.tensor_tensor(out=den[:, d, :], in0=o[:, :, P], in1=emc[:, :, 32 * d + h],
                                                op=ALU.max)
                    step(ins)
                    for d in range(2):
                        o = misc[d][:, 0:258].rearrange("p (a b) -> p a b", b=129)
                        ins = dve.scalar_tensor_tensor(out=den[:, d, :], in0=o[:, :, P], scalar=-1.0,
                                                       in1=den[:, d, :], op0=ALU.mult, op1=ALU.max)
                    step(ins)
                    step(dve.reciprocal(rden[:, :, :], den[:, :, :]))
                    cols = slice(h * P, (h + 1) * P)
                    for tt in range(2):
                        ins = dve.tensor_scalar(Hm[:, tt, cols], misc[0][:, tt * 129:tt * 129 + P],
                                                rden[:, 0, tt:tt + 1], None, ALU.mult)
                    step(ins)
                    for tt in range(2):
                        ins = dve.scalar_tensor_tensor(out=Hm[:, tt, cols], in0=misc[1][:, tt * 129:tt * 129 + P],
                                                       scalar=rden[:, 1, tt:tt + 1], in1=Hm[:, tt, cols],
                                                       op0=ALU.mult, op1=ALU.add)
                    ins.then_inc(h_done, 1)

                for h in range(H + 1):
                    if h < H:
                        weights(h)
                    if h >= 1:
                        outputs(h - 1)
                dve.wait_ge(h_done, H)
                head_norm(H, P, Hm, om)

            def head_norm(heads, w, dst, gate, gain=gainB):
                c.hn += 1
                m = 2 * heads
                v = dst.rearrange("p a (b c) -> p (a b) c", c=w)
                dve.wait_ge(hn_sq, c.hn)
                step(dve.tensor_reduce(ssq[:, 0:m],
                                       Pm[:, 0:2, :, :].rearrange("p a b c -> p (a b c)").rearrange(
                                           "p (a b) -> p a b", b=w), AX.X, ALU.add))
                dve.tensor_scalar(ssq[:, 0:m], ssq[:, 0:m], 1.0 / w, EPS, ALU.mult, ALU.add).then_inc(hn_var, 1)
                dve.wait_ge(hn_sd, c.hn)
                step(dve.reciprocal(ssq[:, 0:m], ssq[:, 0:m]))
                step(dve.tensor_tensor(out=v, in0=v, in1=ssq[:, 0:m].unsqueeze(2).to_broadcast([P, m, w]),
                                       op=ALU.mult))
                step(dve.tensor_tensor(out=dst, in0=dst, in1=gain.unsqueeze(1).to_broadcast([P, 2, D]), op=ALU.mult))
                dve.wait_ge(hn_gate, c.hn)
                dve.tensor_tensor(out=dst, in0=dst, in1=gate, op=ALU.mult).then_inc(hn_out, 1)

            def collect_flips(dst, tiles, kt, grid=False):
                for t_ in tiles:
                    for u in range(kt // 4):
                        dve.wait_ge(tr_full, c.tr + 1)
                        src = trb[c.tr % 2][:, :].rearrange("p (a b) -> p a b", b=P)
                        if grid:
                            o = dst[:, 4 * u:4 * u + 4, :].rearrange("p a (r w) -> p a w r", r=4)
                            o = o[:, :, t_ * 32:(t_ + 1) * 32, :]
                            src = src.rearrange("p a (w r) -> p a w r", r=4)
                            for j in range(4):
                                ins = dve.tensor_copy(o[:, j], src[:, j])
                        else:
                            ins = dve.tensor_copy(dst[:, 4 * u:4 * u + 4, t_ * P:(t_ + 1) * P], src)
                        ins.then_inc(tr_out, 1)
                        c.tr += 1

            def merge_first():
                collect_flips(hT, range(2), KD)
                dve.wait_ge(merge_gate, 1)
                for g in range(2):
                    for t_ in range(2):
                        evacuate(y[:, t_, g * N:(g + 1) * N], lambda o, b: dve.tensor_tensor(
                            out=o, in0=b[:, :], in1=gmx[:, t_, g * N:(g + 1) * N], op=ALU.mult))

            def lower_bounds():
                m = den[:, :, :].rearrange("p a b -> p (a b)")
                dve.tensor_scalar(nbF[:, :], bF[:, :], -1.0, None, ALU.mult)
                step(dve.tensor_tensor(out=lb[:, :, :], in0=lbl[:, :, 0, :], in1=lbl[:, :, 1, :], op=ALU.max))
                dve.tensor_tensor(out=lbl[:, :, :, :].rearrange("p a b c -> p b a c")[:, 0], in0=lbl[:, :, 0, :],
                                  in1=lb[:, :, :], op=ALU.subtract)
                dve.tensor_tensor(out=lbl[:, :, 1, :], in0=lbl[:, :, 1, :], in1=lb[:, :, :],
                                  op=ALU.subtract).then_inc(lb_step, 1)
                dve.wait_ge(lb_step, 2)
                step(dve.tensor_tensor(out=omlb[:, :, :], in0=lbl[:, :, 0, :], in1=lbl[:, :, 1, :], op=ALU.add))
                step(dve.reciprocal(omlb[:, :, :], omlb[:, :, :]))
                step(dve.tensor_tensor(out=lb[:, :, :], in0=lbl[:, :, 0, :], in1=omlb[:, :, :], op=ALU.mult))
                dve.tensor_scalar(omlb[:, :, :], lb[:, :, :], -1.0, 1.0, ALU.mult, ALU.add).then_inc(lb_step, 1)

            def levels(d, mask, between=None):
                g0 = c.g

                def difference(l):
                    B = LEVELS[l]
                    if l >= 2:
                        dve.wait_ge(lv_g, g0 + l - 1)
                    nb = S // (2 * B)
                    v = cum[:, :, 0, 1 - d:S + 1 - d].rearrange("p h (n w) -> p h n w", w=2 * B)
                    ref = cum[:, :, 0, B:S:2 * B].unsqueeze(3).to_broadcast([P, 4, nb, 2 * B])
                    o = E[:, l % 2, :, :].rearrange("p h (n w) -> p h n w", w=2 * B)
                    dve.tensor_tensor(out=o, in0=v, in1=ref, op=ALU.subtract).then_inc(lv_d, 1)

                def operands(l):
                    B = LEVELS[l]
                    c.e += 1
                    dve.wait_ge(lv_e, c.e)
                    for half in range(2):
                        src = qh if half != d else kh[:, :, 0:S]
                        e_, g_, s_ = (v.rearrange("p h (n a b) -> p h n a b", a=2, b=B)[:, :, :, half, :]
                                      for v in (E[:, l % 2, :, :], G[:, l % 2, :, :], src))
                        ins = dve.tensor_tensor(out=g_, in0=s_, in1=e_, op=ALU.mult)
                    ins.then_inc(lv_g, 1)
                    c.g += 1

                def collect(l):
                    pair = (trb, misc)[l % 2]
                    c.a += 1
                    dve.wait_ge(lv_a, c.a)
                    if c.p:
                        dve.wait_ge(lv_p, c.p)
                    c.p += 1
                    if LEVELS[l] == P:
                        o = Pl[:, :, 0, P:S] if d == 0 else Pl[:, :, 1, 0:P]
                        dve.tensor_copy(o, pair[0][:, :].rearrange("p (h b) -> p h b", b=P)).then_inc(lv_p, 1)
                    else:
                        for st in range(2):
                            ins = dve.copy_predicated(Pl[:, :, st, st * P:(st + 1) * P],
                                                mask[:, l - 1, :].unsqueeze(1).to_broadcast([P, 4, P]),
                                                pair[st][:, :].rearrange("p (h b) -> p h b", b=P))
                        ins.then_inc(lv_p, 1)

                difference(0)
                for l in range(8):
                    if l < 7:
                        difference(l + 1)
                    operands(l)
                    if l:
                        collect(l - 1)
                        if between:
                            between(l - 1)
                collect(7)

            def diagonal():
                c.a += 1
                dve.wait_ge(lv_a, c.a)
                dve.wait_ge(lv_p, c.p)
                for st in range(2):
                    ins = dve.copy_predicated(Pl[:, :, st, st * P:(st + 1) * P],
                                              ident[:, :].bitcast(I32).unsqueeze(1).to_broadcast([P, 4, P]),
                                              trb[st][:, :].rearrange("p (h b) -> p h b", b=P))
                ins.then_inc(attn_done, 1)

            def hgrn():
                dve.wait_ge(bias_in, 64)
                dve.wait_ge(masks_in, 32)
                for g in range(2):
                    for t_ in range(2):
                        evacuate(ghx[:, t_, g * N:(g + 1) * N], lambda o, b: dve.tensor_tensor(
                            out=o, in0=b[:, :], in1=biasB[:, g * N:(g + 1) * N], op=ALU.add))
                step(dve.tensor_copy(xn[:, :, :].rearrange("p a b -> p (a b)").rearrange(
                    "p (a w r) -> p a w r", w=64, r=4), xT[:, :, 0:S].rearrange("p a (r w) -> p a w r", r=4)))
                dve.tensor_copy(xT[:, :, 0:S], xn[:, :, :].rearrange("p a b -> p (a b)").rearrange(
                    "p (a b) -> p a b", b=S)).then_inc(permuted, 1)

                def values(g, l):
                    if l % 2 == 0:
                        evacuate(vi[:, l // 2, g * N:(g + 1) * N], lambda o, b: dve.tensor_tensor(
                            out=o, in0=b[:, :], in1=biasB[:, D + g * N:D + (g + 1) * N], op=ALU.add))

                for hg in range(2):
                    c.acc += 4
                    for d in range(2):
                        dve.memset(cum[:, :, :, 0:1], 0.0)
                        c.acc += 4
                        c.lf += 1
                        dve.wait_ge(lf_done, c.lf)
                        for j in range(4):
                            h = 4 * hg + j
                            dve.tensor_scalar(kh[:, j, :], kh[:, j, :], omlb[:, d, h:h + 1], None, ALU.mult)
                            for sg in range(2):
                                ins = dve.tensor_tensor_scan(cum[:, j, sg, 1:], ones[:, :],
                                                             lf[:, j, sg * S:(sg + 1) * S], 0.0, ALU.mult, ALU.add)
                        step(ins)
                        if d == 0:
                            step(dve.tensor_copy(kd, kh[:, :, 0:S]))
                        else:
                            step(dve.tensor_tensor(out=kd, in0=kd, in1=kh[:, :, 0:S], op=ALU.add))
                        levels(d, (maskf, maskb)[d], (lambda l: values(d, l)) if hg == 0 else None)
                        c.e += 1
                        dve.wait_ge(lv_e, c.e)
                        dve.tensor_tensor(out=G[:, 0, :, :], in0=kh[:, :, S:2 * S], in1=E[:, 0, :, :], op=ALU.mult)
                        dve.tensor_tensor(out=G[:, 1, :, :], in0=qh, in1=E[:, 1, :, :],
                                          op=ALU.mult).then_inc(lv_g, 1)
                        c.g += 1
                        for j in range(4):
                            o = Pc[:, j, :, :].rearrange("p a b -> p (a b)")
                            evacuate(o, (lambda o, b: dve.tensor_copy(o, b[:, :])) if d == 0 else
                                     (lambda o, b: dve.tensor_tensor(out=o, in0=b[:, :], in1=o, op=ALU.add)))
                    diagonal()
                    for tt in range(2):
                        evacuate(Hx[:, tt, hg * N:(hg + 1) * N], lambda o, b: dve.tensor_copy(o, b[:, :]))
                for g in range(2):
                    for t_ in range(2):
                        evacuate(gx[:, t_, g * N:(g + 1) * N], lambda o, b: dve.tensor_tensor(
                            out=o, in0=b[:, :], in1=biasB[:, 2 * D + g * N:2 * D + (g + 1) * N], op=ALU.add))
                head_norm(H, P, Hx, gx)

            def merge_second():
                collect_flips(hT, range(2), KD, grid=True)
                dve.wait_ge(merge_gate, 2)
                scratch = cum.rearrange("p a b c -> p (a b c)")
                for g in range(2):
                    for t_ in range(2):
                        part = scratch[:, (2 * g + t_) * N:(2 * g + t_ + 1) * N]
                        cols = slice(g * N, (g + 1) * N)
                        evacuate(part, lambda o, b: dve.tensor_tensor(
                            out=o, in0=b[:, :], in1=ghx[:, t_, cols], op=ALU.mult))
                        n = c.acc - 1
                        dve.wait_ge(evac[n % 4], n // 4 + 1)
                        dve.tensor_tensor(out=y[:, t_, cols], in0=y[:, t_, cols], in1=part,
                                          op=ALU.add).then_inc(y_done, 1)
                collect_flips(hT, range(2), KD)

            def residual(update):
                for n in range(2):
                    for t_ in range(2):
                        dve.wait_ge(acc_full, c.acc + 1)
                        update(t_, n, c.acc)
                        c.acc += 1

            def bias_toeplitz():
                for h in range(H):
                    dve.wait_ge(bias_rows, h + 1)
                    dve.tensor_copy(rep_rows[:, h, :], misc[h % 2][:, 0:RW]).then_inc(bias_out, 1)

            def halved(t_, n, a):
                cols = slice(n * N, (n + 1) * N)
                dve.scalar_tensor_tensor(out=X[:, t_, cols], in0=acc[a % 4][:, :], scalar=0.5, in1=X[:, t_, cols],
                                         op0=ALU.mult, op1=ALU.add).then_inc(evac[a % 4], 1)

            def plain(t_, n, a):
                cols = slice(n * N, (n + 1) * N)
                dve.tensor_tensor(out=X[:, t_, cols], in0=acc[a % 4][:, :], in1=X[:, t_, cols],
                                  op=ALU.add).then_inc(evac[a % 4], 1)

            def attention():
                def maxima(h):
                    dve.wait_ge(ns_s, c.ns + h + 1)
                    if h >= 2:
                        dve.wait_ge(ns_t, c.ns + h - 1)
                    a, L = 2 * (h % 2), Lb[:, h % 2, :]
                    for i, (lo, hi) in enumerate(SEGMENTS):
                        tt = i % 2
                        if i < 4:
                            src = acc[a + i // 2][:, (P if tt else 0):(P + S if tt else P)]
                            b = TB[:, h, 0 if tt else P:S]
                        else:
                            src = acc[a][:, 384 + 16 * tt:384 + 16 * tt + hi - lo]
                            b = TB[:, h, (31 if tt else 159):S:16]
                        ins = dve.tensor_tensor_reduce(L[:, lo:hi], src, b, 1.0, MASK_FLOOR, ALU.add, ALU.max,
                                                       mx[:, h % 2, i:i + 1])
                    step(ins)
                    dve.tensor_scalar(mx[:, h % 2, :], mx[:, h % 2, :], -1.0, None, ALU.mult).then_inc(ns_m, 1)

                def scale(h):
                    dve.wait_ge(ns_e, c.ns + h + 1)
                    z, w, L = sm[:, h % 2, :], wt[:, h % 2, :], Lb[:, h % 2, :]
                    step(dve.tensor_scalar(z, z, 1e-30, None, ALU.max))
                    step(dve.reciprocal(z, z))
                    for kind, i in ((1, 0), (2, 2), (0, 4)):
                        ins = dve.tensor_tensor(out=w[:, i:i + 2], in0=z[:, i:i + 2], in1=ga[:, :, 3 * h + kind],
                                                op=ALU.mult)
                    step(ins)
                    for i, (lo, hi) in enumerate(SEGMENTS):
                        ins = dve.tensor_scalar(L[:, lo:hi], L[:, lo:hi], w[:, i:i + 1], None, ALU.mult)
                    ins.then_inc(ns_w, 1)

                def turned(h):
                    dve.wait_ge(ns_t, c.ns + h + 1)
                    if h >= 2:
                        dve.wait_ge(ns_o, c.ns + h - 1)
                    dve.tensor_copy(PT[:, h % 2, 384:768], trb[1][:, 0:384])
                    dve.tensor_copy(PT[0:15, h % 2, 896:1024], trb[1][0:15, 384:N]).then_inc(ns_pb, 1)

                dve.wait_ge(ga_done, c.layer)
                dve.wait_ge(bias_done, 32)
                for h in range(H + 2):
                    if h < H:
                        maxima(h)
                    if h >= 2:
                        turned(h - 2)
                    if 1 <= h <= H:
                        scale(h - 1)
                c.ns += H

            def layer(l):
                c.layer += 1
                norm(range(2), lambda t_: gains2[:, 3 * l, :], lambda t_: None, 2)
                ffn(2, halved)
                norm(range(2), lambda t_: gains2[:, 3 * l + 1, :], lambda t_: None)
                if l == 0:
                    bias_toeplitz()
                dve.wait_ge(layer_in, LAYER * c.layer)
                for j in range(4):
                    evacuate(qa[:, j, :], lambda o, b: dve.tensor_scalar(o, b[:, 0:S], 64 ** -0.5, None, ALU.mult))
                for j in range(2):
                    evacuate(kk[:, j, :], lambda o, b: dve.tensor_copy(o, b[:, 0:S]))
                for x in range(2):
                    dve.wait_ge(acc_full, c.acc + 1)
                    for g in range(2):
                        for half in range(2):
                            f = slice(64 * half, 64 * half + 64)
                            o = KK[f, x, g, :].rearrange("p (l c) -> p l c", c=15)
                            src = acc[c.acc % 4][64 * g:64 * g + 64, 16 * half:16 * half + 240]
                            ins = dve.tensor_tensor(out=o, in0=src.rearrange("p (c l) -> p l c", l=16),
                                                    in1=pos[f, x, :].unsqueeze(2).to_broadcast([64, 16, 15]),
                                                    op=ALU.add)
                    ins.then_inc(evac[c.acc % 4], 1)
                    c.acc += 1
                evacuate(alr, lambda o, b: dve.tensor_copy(o, b[0:16, 0:S]))
                for t_ in range(2):
                    dve.wait_ge(acc_full, c.acc + 1)
                    dve.tensor_copy(ga[:, t_, :], acc[c.acc % 4][:, S:S + 24])
                    dve.tensor_copy(vsw[:, t_, :], acc[c.acc % 4][:, 0:S]).then_inc(evac[c.acc % 4], 1)
                    c.acc += 1
                dve.memset(Lb[:, :, 768:800], 0.0).then_inc(pad_set, 1)
                dve.wait_ge(pad_set, l + 1)
                c.acc += 2
                dve.wait_ge(acc_full, c.acc + 1)
                dve.tensor_copy(kcT[:, 0:15], acc[c.acc % 4][:, 0:15])
                dve.tensor_copy(vcmp.rearrange("p a b -> p (a b)"),
                                acc[c.acc % 4][0:15, 64:192]).then_inc(evac[c.acc % 4], 1)
                c.acc += 1
                c.acc += 4
                attention()
                for n in range(2):
                    for t_ in range(2):
                        cols = slice(n * N, (n + 1) * N)
                        evacuate(y2[:, t_, cols], lambda o, b: dve.tensor_tensor(out=o, in0=b[:, :], in1=o,
                                                                                 op=ALU.mult))
                for j in range(4):
                    evacuate(qh[:, j, :], lambda o, b: dve.tensor_scalar(o, b[:, 0:S], 128 ** -0.5, None, ALU.mult))
                c.acc += 4
                for j in range(4):
                    evacuate(lf[:, j, 0:S], lambda o, b: dve.tensor_scalar(o, b[:, 0:S], ab[:, j:j + 1], None,
                                                                           ALU.add))
                n = c.acc - 1
                dve.wait_ge(evac[n % 4], n // 4 + 1)
                dve.scalar_tensor_tensor(out=G[:, 0, :, :], in0=lf[:, :, 0:S], scalar=-1.0, in1=lf[:, :, 0:S],
                                         op0=ALU.mult, op1=ALU.max).then_inc(gl_a, 1)
                dve.memset(cum[:, :, :, 0:1], 0.0)
                dve.memset(Pl[:, :, :, :], 0.0)
                dve.wait_ge(gl_l, l + 1)
                step(dve.scalar_tensor_tensor(out=lf[:, :, 0:S], in0=lf[:, :, 0:S], scalar=0.0, in1=G[:, 0, :, :],
                                              op0=ALU.min, op1=ALU.subtract))
                step(dve.tensor_scalar(lf[:, :, 0:S], lf[:, :, 0:S], 1.0 / 16, None, ALU.mult))
                for j in range(4):
                    ins = dve.tensor_tensor_scan(cum[:, j, 0, 1:], ones[:, :], lf[:, j, 0:S], 0.0, ALU.mult, ALU.add)
                step(ins)
                n = c.acc - 5
                dve.wait_ge(evac[n % 4], n // 4 + 1)
                dve.tensor_copy(kd, kh[:, :, 0:S]).then_inc(gl_a, 1)
                dve.wait_ge(gl_a, 2 * l + 2)
                levels(0, maskf)
                c.acc += 8
                diagonal()
                for tt in range(2):
                    for pair in range(2):
                        evacuate(Hx[:, tt, pair * N:(pair + 1) * N], lambda o, b: dve.tensor_copy(o, b[:, :]))
                head_norm(4, S, Hx, rx, gainC)
                c.acc += 4
                collect_flips(hT, range(2), KD)
                scratch = cum.rearrange("p a b c -> p (a b c)")
                for g in range(2):
                    for t_ in range(2):
                        part = scratch[:, (2 * g + t_) * N:(2 * g + t_ + 1) * N]
                        cols = slice(g * N, (g + 1) * N)
                        gate = gm2[:, t_, D + g * N:D + (g + 1) * N]
                        evacuate(part, lambda o, b: dve.tensor_tensor(out=o, in0=b[:, :], in1=gate, op=ALU.mult))
                        n = c.acc - 1
                        dve.wait_ge(evac[n % 4], n // 4 + 1)
                        dve.tensor_tensor(out=y2[:, t_, cols], in0=y2[:, t_, cols], in1=part,
                                          op=ALU.add).then_inc(y_done, 1)
                collect_flips(hT, range(2), KD)
                residual(plain)
                norm(range(2), lambda t_: gains2[:, 3 * l + 2, :], lambda t_: None, 2)
                ffn(2, halved)

            def block_norm(dst, gain, done):
                c.norm += 1
                dve.wait_ge(squares, c.norm)
                dve.tensor_scalar(var[:, 0:2], ss[:, 0:2], 1.0 / D, EPS, ALU.mult, ALU.add).then_inc(var_done, 1)
                dve.wait_ge(sd_done, c.norm)
                step(dve.reciprocal(rstd[:, 0:2], sd[:, 0:2]))
                for t_ in range(2):
                    dve.scalar_tensor_tensor(out=dst[:, t_, :], in0=X[:, t_, :], scalar=rstd[:, t_:t_ + 1],
                                             in1=gain, op0=ALU.mult, op1=ALU.mult).then_inc(done, 1)

            modulation()
            dve.wait_ge(bc_out, 8)
            lower_bounds()
            norm(range(4), lambda t_: normA[:, t_ // 2, :], lambda t_: modT[:, 0:8, t_ // 2], 4)
            ffn(4, gated(lambda t_: 0 if t_ < 2 else 3))
            norm(range(4), lambda t_: normA[:, 2 + t_ // 2, :], lambda t_: modT[:, 16:24, t_ // 2])
            dve.memset(ones[:, :], 1.0).then_inc(ones_set, 1)
            dve.wait_ge(ones_set, 1)
            mlstm()
            merge_first()
            hgrn()
            merge_second()
            residual(gated(lambda t_: 1))
            norm(range(2), lambda t_: normA[:, 4, :], lambda t_: modT[:, 32:40, 0], 2)
            ffn(2, gated(lambda t_: 2))
            dve.wait_ge(final_in, 16)
            block_norm(X, gateB[:, 1, :], resid)
            layer(0)
            layer(1)
            dve.wait_ge(final_in, 32)
            block_norm(xn, gainC, out_done)

        @block.gpsimd
        def _(gp):
            c = Count()

            def low(j, i=None):
                slot = (block_chunk[c.block] + j) % SLOTS
                gp.wait_ge(high_ready, up(c.high + j + 1, i, 4))
                w = ring[:, slot].rearrange("p a b -> p (a b)")
                gp.tensor_tensor(out=ring_r[:, slot].rearrange("p a b -> p (a b)"), in0=w, in1=high[:, slot, :],
                                 op=ALU.subtract).then_inc(low_ready[0], 1)

            def ffn(nt):
                low(0)
                low(2)
                with gp.Fori(0, (UG - 3) // 2) as i:
                    low(4, i)
                    low(6, i)
                for j in range(2 * UG - 2, chunks_split(nt), 2):
                    low(j)
                c.high += chunks_split(nt)
                c.block += 1

            ffn(4)
            for h in range(H):
                for d in range(2):
                    gp.wait_ge(p_done, 2 * h + d + 1)
                    for n in range(2):
                        v = Pm[:, 2 * (h % 2) + d, n, n * P:(n + 1) * P]
                        sign = 1 if d == 0 else -1
                        ins = gp.affine_select(out=v, in_=v, compare_op=ALU.is_ge, fill=0.0, base=0,
                                               pattern=[[sign, P]], channel_multiplier=-sign)
                    ins.then_inc(pm_done, 1)
            gp.wait_ge(resid, 12)
            gp.dma_start(gateB[:, 1, :], t["fgain"][0:1].to_broadcast([P, D])).then_inc(final_in, 16)
            gp.dma_start(onehot, t["onehot"]).then_inc(bias_dma, 16)
            gp.dma_start(table, t["table"]).then_inc(bias_dma, 16)
            ffn(2)
            ffn(2)
            gp.wait_ge(bias_out, H)
            gp.dma_start(t["scratch"], rep_rows).then_inc(bias_done, 16)
            gp.wait_ge(bias_done, 16)
            gp.dma_start(TB, bass.AP(t["scratch"].tensor, P - 1, [[H * RW - 1, P], [RW, H], [1, S]])).then_inc(
                bias_done, 16)
            for _ in range(2):
                ffn(2)
            gp.wait_ge(hn_out, 4)
            gp.dma_start(gainC, t["fgain"][1:2].to_broadcast([P, D])).then_inc(final_in, 16)
            ffn(2)
            for t_ in range(2):
                gp.wait_ge(out_done, t_ + 1)
                gp.dma_start(out[0, t_ * P:(t_ + 1) * P, :], xn[:, t_, :]).then_inc(stored, 16)
            gp.wait_ge(stored, 32)


FIRST_CONSTS = 16 * 4
MORE_CONSTS = 16 * 7
LAYER = 16 * 5
MASK_FLOOR = -1e25
SEGMENTS = ((0, 128), (128, 384), (384, 512), (512, 768), (768, 775), (784, 799))


def level_masks():
    p = np.arange(P)
    out = np.zeros((2, P, 7, P), np.float32)
    for n in range(7):
        B = 64 >> n
        m = (p[:, None] // (2 * B) == p // (2 * B)) & (p[:, None] % (2 * B) < B) & (p % (2 * B) >= B)
        out[0, :, n], out[1, :, n] = m, m.T
    return out.reshape(2, P, 7 * P)


def distance_buckets():
    d = 255 - np.arange(384)
    nf = np.maximum(d, 1).astype(np.float32)
    b = 16 + (np.log(nf / np.float32(16)) / np.float32(math.log(64)) * np.float32(16)).astype(np.int32)
    b = np.where(d < 0, 32, np.where(d < 16, d, np.minimum(b, 31)))
    return (b == np.arange(33)[:, None]).astype(np.float32)


def groups_of(w, col_lists):
    k = w.shape[0] // P
    for cols in col_lists:
        g = np.zeros((P, k, N), np.float32)
        g[:, :, :len(cols)] = w[:, cols].reshape(k, P, len(cols)).transpose(1, 0, 2)
        yield g


def kernel(**inputs):
    import concourse.bacc as bacc
    from concourse.bass_utils import run_bass_kernel_spmd as run

    v = {k: np.asarray(a) for k, a in inputs.items()}
    r = np.arange
    tiles = []

    def add(w, col_lists):
        for g in groups_of(w, col_lists):
            tiles.extend(g[:, k] for k in range(g.shape[1]))

    halves = [r(0, N), r(N, 2 * N)]
    add(v["ada_w"][0], [m * D + h for m in MODS for h in halves])
    up_cols = [np.concatenate([g * 256 + r(256), F + g * 256 + r(256)]) for g in range(UG)]
    add(v["ffn1_w_in"][0], up_cols)
    add(v["ffn1_w_out"][0], halves)
    w, b = v["mix_w_in"][0], v["mix_b_in"][0]
    Q0, K0, V0, O0, I0, F0, HQ0, HF0, HI0, HG0, GM0, GH0 = np.cumsum(
        [0, 512, 512, D, D, 16, 16, D, 2 * D, D, D, D])
    add(w, [Q0 + r(N), K0 + r(N), V0 + r(N), V0 + N + r(N), O0 + r(N), O0 + N + r(N), GM0 + r(N), GM0 + N + r(N)])
    add(v["proj_m"][0], halves)
    add(w, [GH0 + r(N), GH0 + N + r(N)])
    add(w, [HQ0 + r(N), HF0 + r(N), HI0 + r(N), HF0 + D + r(N), HI0 + N + r(N)])
    add(w, [HQ0 + N + r(N), HF0 + N + r(N), HF0 + D + N + r(N)])
    add(w, [HG0 + r(N), HG0 + N + r(N)])
    add(v["proj_h"][0], halves)
    add(v["mix_w_out"][0], halves)
    add(v["ffn2_w_in"][0], up_cols)
    add(v["ffn2_w_out"][0], halves)
    WI = np.cumsum([0, 512, 768, 24, 512, 512, D, 16, D, 2 * D])
    QA, KV, GA, QB, KB, VB, AL, RB, GM = WI[:9]
    head_pairs = np.concatenate([np.concatenate([h * 64 + r(64), (h + 4) * 64 + r(64)]) for h in range(4)])
    for l in range(2):
        w2 = v["w_in_2"][l]

        def ffn(a, b, c_):
            add(np.concatenate([v[a][l], v[b][l]], 1), up_cols)
            add(v[c_][l], halves)

        ffn("ffn1_w_gate_2", "ffn1_w_up_2", "ffn1_w_down_2")
        kv = [KV + n * P + r(P) for n in range(6)]
        add(w2, [QA + head_pairs, np.concatenate([kv[2], kv[4], kv[0], kv[1]]),
                 np.concatenate([kv[3], kv[5], GA + r(24), AL + r(16)])])
        for name in ("cmp_k_w1_2", "cmp_v_w1_2"):
            w1 = v[name][l].reshape(2, 16, 64, S).transpose(0, 2, 1, 3).reshape(P, KD, N)
            tiles.extend(w1[:, k] for k in range(KD))
        add(w2, [GM + r(N), GM + N + r(N)])
        add(v["w_branch_nsa_2"][l][head_pairs], halves)
        add(w2, [QB + r(N), KB + r(N), VB + r(N), VB + N + r(N), RB + r(N), RB + N + r(N),
                 GM + D + r(N), GM + D + N + r(N)])
        add(v["w_branch_gla_2"][l], halves)
        add(v["w_out_2"][l], halves)
        ffn("ffn2_w_gate_2", "ffn2_w_up_2", "ffn2_w_down_2")
    wg = np.zeros((D, P), np.float32)
    bg = np.zeros(P, np.float32)
    for n, at in enumerate((I0, I0 + 8, F0, F0 + 8)):
        wg[:, 32 * n:32 * n + 8] = w[:, at:at + 8]
        bg[32 * n:32 * n + 8] = b[at:at + 8]
    bF = np.concatenate([b[Q0:V0], b[HQ0:HI0], bg]).reshape(33, P).T
    bT = np.concatenate([b[V0:I0], b[GM0:GH0], b[GH0:], b[HI0:GM0]])[None]
    stream = np.stack(tiles).reshape(-1, CW, P, N).transpose(0, 2, 1, 3)

    def feat(a):
        return np.moveaxis(a.reshape(*a.shape[:-1], KD, P), -1, 0)

    arrays = {
        "stream": stream,
        "cT": feat(np.stack([v["c"][0], v["c_ctx"]])).transpose(0, 2, 1),
        "ident": np.eye(P, dtype=np.float32),
        "pick": np.repeat(np.eye(2, dtype=np.float32)[:, :, None], P, 2),
        "adab": np.repeat(np.concatenate([v["ada_b"][0][m * D:(m + 1) * D] for m in MODS])[None], 2, 0),
        "gains": feat(np.stack([v["ffn1_norm"][0], v["mix_norm"][0], v["ffn2_norm"][0]])),
        "bF": bF,
        "bT": bT,
        "mgain": v["mlstm_norm"],
        "hgain": v["hgrn_norm"],
        "lbl": v["hgrn_lb_logits"].reshape(2, 2, KD, P).transpose(3, 0, 1, 2),
        "masks": level_masks(),
        "gains2": feat(np.stack([v[n][l] for l in range(2) for n in ("ffn1_norm_2", "mix_norm_2", "ffn2_norm_2")])),
        "onehot": distance_buckets(),
        "table": np.concatenate([v["rel_table_2"], np.full((1, 8), -1e30, np.float32)]),
        "pos": np.stack([v["cmp_pos_k_2"], v["cmp_pos_v_2"]], 1).reshape(2, 2, 2, 16, 64)
                 .transpose(0, 2, 4, 1, 3).reshape(2, P, 2, 16),
        "w2c": np.stack([v["cmp_k_w2_2"], v["cmp_v_w2_2"]], 1).reshape(2, 2, 2, P, 64).transpose(0, 3, 1, 2, 4),
        "wa2": v["gla_a_w2_2"],
        "ab": v["gla_a_b_2"].reshape(2, 4, P).transpose(0, 2, 1),
        "ggain": v["gla_out_norm_2"],
        "fgain": np.stack([v["final_norm"], v["final_norm_2"]]),
        "wg": wg.reshape(KD, P, P).transpose(1, 0, 2),
        "x": v["x"][0].reshape(ST, P, D).transpose(1, 0, 2),
        "ctx": v["ctx"][0].reshape(ST, P, D).transpose(1, 0, 2),
    }
    arrays = {k: np.ascontiguousarray(a) for k, a in arrays.items()}
    nc = bacc.Bacc("TRN2", target_bir_lowering=False, num_devices=1)
    t = {k: nc.dram_tensor("in_" + k, a.shape, F32, kind="ExternalInput").ap() for k, a in arrays.items()}
    t["scratch"] = nc.dram_tensor("bias_scratch", (P, 8, 384), F32).ap()
    out = nc.dram_tensor("out", (1, S, D), F32, kind="ExternalOutput").ap()
    build(nc, t, out)
    res = run(nc, [{"in_" + k: a for k, a in arrays.items()}], core_ids=[0])
    return res.results[0]["out"]
```
